# Optimizing a Trainium2 kernel written in Bass

```python
import jax, jax.numpy as jnp
from jax import lax
import numpy as np
import math

D_MODEL = 2048
BATCH = 1
SEQ = 256
DEPTH = 1

GRID_W = 64
GM_GROUPS = 8
GM_HEAD = 128
GM_WIDTH = GM_GROUPS * GM_HEAD
CHUNK = 128
NA_HEADS = 16
NA_HEAD_DIM = 64
NA_WIDTH = NA_HEADS * NA_HEAD_DIM
NA_KR = 8
NA_KC = 16
N_BRANCH = 2
IN_COLS = 2 * GM_WIDTH + 3 * NA_WIDTH + N_BRANCH * D_MODEL
D_FF = 5504
CONV_W = 3
RMS_EPS = 1e-6
LN_EPS = 1e-5
NEG_INF = -1e30


def rms_norm(x, g):
    xf = x.astype(jnp.float32)
    y = xf * lax.rsqrt(jnp.mean(xf * xf, axis=-1, keepdims=True) + RMS_EPS)
    return (y * g.astype(jnp.float32)).astype(x.dtype)

def gmlp_branch(uv, ln_g, ln_b, w_s, b_s):
    b, t, _ = uv.shape
    uv = jax.nn.gelu(uv)
    u, v = jnp.split(uv, 2, axis=-1)
    vf = v.astype(jnp.float32)
    mu = jnp.mean(vf, axis=-1, keepdims=True)
    var = jnp.mean(jnp.square(vf - mu), axis=-1, keepdims=True)
    v = ((vf - mu) * lax.rsqrt(var + LN_EPS) * ln_g.astype(jnp.float32)
         + ln_b.astype(jnp.float32)).astype(u.dtype)
    v = v.reshape(b, t // CHUNK, CHUNK, GM_GROUPS, GM_HEAD)
    mixed = jnp.einsum('gpq,bnqgc->bnpgc', w_s, v) + b_s.T[None, None, :, :, None]
    return u * mixed.reshape(b, t, GM_WIDTH)

def neighbourhood_attn(q, k, v, rpb):
    b, t, _ = q.shape
    rows = t // GRID_W
    kr = min(NA_KR, rows)

    def to_grid(z):
        return z.reshape(b, rows, GRID_W, NA_HEADS, NA_HEAD_DIM).transpose(0, 3, 1, 2, 4)

    qg, kg, vg = to_grid(q), to_grid(k), to_grid(v)
    r = jnp.arange(rows)
    row_start = jnp.clip(r - kr // 2, 0, rows - kr)
    row_idx = row_start[:, None] + jnp.arange(kr)[None, :]
    k_blk = kg[:, :, row_idx]
    v_blk = vg[:, :, row_idx]

    c = jnp.arange(GRID_W)
    col_start = jnp.clip(c - NA_KC // 2, 0, GRID_W - NA_KC)
    in_win = (c[None, :] >= col_start[:, None]) & (c[None, :] < col_start[:, None] + NA_KC)
    dr_i = (row_idx - r[:, None]) + (NA_KR - 1)
    dc_i = jnp.clip(c[None, :] - c[:, None], -(NA_KC - 1), NA_KC - 1) + (NA_KC - 1)
    bias = rpb.astype(jnp.float32)[:, dr_i[:, None, :, None], dc_i[None, :, None, :]]
    bias = jnp.where(in_win[None, None, :, None, :], bias, NEG_INF)

    scale = NA_HEAD_DIM ** -0.5
    s = jnp.einsum('bhrcd,bhrikd->bhrcik', qg.astype(jnp.float32),
                   k_blk.astype(jnp.float32)) * scale + bias[None]
    p = jax.nn.softmax(s.reshape(b, NA_HEADS, rows, GRID_W, kr * GRID_W), axis=-1)
    p = p.reshape(b, NA_HEADS, rows, GRID_W, kr, GRID_W)
    o = jnp.einsum('bhrcik,bhrikd->bhrcd', p, v_blk.astype(jnp.float32))
    return o.transpose(0, 2, 3, 1, 4).reshape(b, t, NA_WIDTH).astype(q.dtype)

def mixer_block(x, g_norm, w_in, ln_g, ln_b, w_s, b_s, rpb, w_branch, w_out):
    h = rms_norm(x, g_norm)
    proj = h @ w_in
    uv, qkv, gates = jnp.split(proj, [2 * GM_WIDTH, 2 * GM_WIDTH + 3 * NA_WIDTH], axis=-1)
    q, k, v = jnp.split(qkv, 3, axis=-1)
    y_a = gmlp_branch(uv, ln_g, ln_b, w_s, b_s)
    y_b = neighbourhood_attn(q, k, v, rpb)
    g_a, g_b = jnp.split(jax.nn.sigmoid(gates), 2, axis=-1)
    merged = g_a * (y_a @ w_branch[:GM_WIDTH]) + g_b * (y_b @ w_branch[GM_WIDTH:])
    return x + merged @ w_out

def conv_ffn(x, g_norm, w_up, conv_k, conv_b, w_down):
    h = rms_norm(x, g_norm)
    up = h @ w_up
    t = up.shape[1]
    pad = jnp.pad(up, ((0, 0), (1, 1), (0, 0)))
    up = (pad[:, :t] * conv_k[0] + pad[:, 1:t + 1] * conv_k[1]
          + pad[:, 2:t + 2] * conv_k[2] + conv_b)
    gate, val = jnp.split(up, 2, axis=-1)
    return x + (jax.nn.silu(gate) * val) @ w_down

def first_inputs(seed: int = 0) -> dict:
    key = jax.random.key(seed)
    ks = jax.random.split(key, 17)
    f32 = jnp.float32
    n = lambda k, s: jax.random.normal(k, s, f32)
    return {
        "x": n(ks[0], (BATCH, SEQ, D_MODEL)),
        "norm_mix": 1.0 + 0.1 * n(ks[1], (DEPTH, D_MODEL)),
        "w_in": n(ks[2], (DEPTH, D_MODEL, IN_COLS)) * D_MODEL ** -0.5,
        "gm_ln_g": 1.0 + 0.1 * n(ks[3], (DEPTH, GM_WIDTH)),
        "gm_ln_b": 0.01 * n(ks[4], (DEPTH, GM_WIDTH)),
        "gm_w_s": n(ks[5], (DEPTH, GM_GROUPS, CHUNK, CHUNK)) * CHUNK ** -0.5,
        "gm_b_s": 1.0 + 0.1 * n(ks[6], (DEPTH, GM_GROUPS, CHUNK)),
        "na_rpb": 0.5 * n(ks[7], (DEPTH, NA_HEADS, 2 * NA_KR - 1, 2 * NA_KC - 1)),
        "w_branch": n(ks[8], (DEPTH, GM_WIDTH + NA_WIDTH, D_MODEL)) * GM_WIDTH ** -0.5,
        "w_out": n(ks[9], (DEPTH, D_MODEL, D_MODEL)) * D_MODEL ** -0.5,
        "norm_ffn": 1.0 + 0.1 * n(ks[10], (DEPTH, D_MODEL)),
        "w_up": n(ks[11], (DEPTH, D_MODEL, 2 * D_FF)) * D_MODEL ** -0.5,
        "conv_k": n(ks[12], (DEPTH, CONV_W, 2 * D_FF)) * CONV_W ** -0.5,
        "conv_b": 0.01 * n(ks[13], (DEPTH, 2 * D_FF)),
        "w_down": n(ks[14], (DEPTH, D_FF, D_MODEL)) * D_FF ** -0.5,
        "norm_final": 1.0 + 0.1 * n(ks[15], (D_MODEL,)),
    }

def first_block(x, norm_mix, w_in, gm_ln_g, gm_ln_b, gm_w_s, gm_b_s, na_rpb, w_branch, w_out,
              norm_ffn, w_up, conv_k, conv_b, w_down, norm_final):
    for l in range(DEPTH):
        x = mixer_block(x, norm_mix[l], w_in[l], gm_ln_g[l], gm_ln_b[l], gm_w_s[l], gm_b_s[l],
                        na_rpb[l], w_branch[l], w_out[l])
        x = conv_ffn(x, norm_ffn[l], w_up[l], conv_k[l], conv_b[l], w_down[l])
    return rms_norm(x, norm_final)


DEPTH_2 = 2

CHUNK_2 = 64
N_MIXERS = 2
EPS = 1e-6

A_HEADS = 16
A_HEAD_DIM = 128
A_INNER = A_HEADS * A_HEAD_DIM
CONV_K = 4

B_HEADS = 16
B_HEAD_DIM = 128
B_INNER = B_HEADS * B_HEAD_DIM
LEFT_CHUNKS = 8
BAND = (LEFT_CHUNKS + 1) * CHUNK_2
REL_CLIP = 256


def rms_norm_2(x, w):
    xf = x.astype(jnp.float32)
    y = xf * lax.rsqrt(jnp.mean(xf * xf, axis=-1, keepdims=True) + EPS)
    return (y * w.astype(jnp.float32)).astype(x.dtype)

def l2_norm(x):
    xf = x.astype(jnp.float32)
    return xf * lax.rsqrt(jnp.sum(xf * xf, axis=-1, keepdims=True) + EPS)

def causal_depthwise_conv(x, w):
    c = x.shape[-1]
    return lax.conv_general_dilated(
        x, w[:, None, :].astype(x.dtype), window_strides=(1,),
        padding=[(CONV_K - 1, 0)], dimension_numbers=("NWC", "WIO", "NWC"),
        feature_group_count=c)

def gated_deltanet(h, w_in, conv_w, a_log, dt_bias, out_norm_w, w_out):
    bsz, t, _ = h.shape
    nc = t // CHUNK_2
    proj = h @ w_in.astype(h.dtype)
    qkv = proj[..., :3 * A_INNER]
    z = proj[..., 3 * A_INNER:4 * A_INNER]
    a_in = proj[..., 4 * A_INNER:4 * A_INNER + A_HEADS]
    b_in = proj[..., 4 * A_INNER + A_HEADS:]
    qkv = jax.nn.silu(causal_depthwise_conv(qkv, conv_w))
    q = qkv[..., :A_INNER].reshape(bsz, t, A_HEADS, A_HEAD_DIM)
    k = qkv[..., A_INNER:2 * A_INNER].reshape(bsz, t, A_HEADS, A_HEAD_DIM)
    v = qkv[..., 2 * A_INNER:].reshape(bsz, t, A_HEADS, A_HEAD_DIM).astype(jnp.float32)
    q = l2_norm(q) * (A_HEAD_DIM ** -0.5)
    k = l2_norm(k)
    beta = jax.nn.sigmoid(b_in.astype(jnp.float32))
    g = -jnp.exp(a_log.astype(jnp.float32)) * jax.nn.softplus(
        a_in.astype(jnp.float32) + dt_bias.astype(jnp.float32))

    def to_chunks(u):
        u = u.reshape((bsz, nc, CHUNK_2) + u.shape[2:])
        return jnp.moveaxis(u, 3, 1)

    q, k, v = to_chunks(q), to_chunks(k), to_chunks(v)
    beta, g = to_chunks(beta), to_chunks(g)
    gc = jnp.cumsum(g, axis=-1)
    tri_incl = jnp.tril(jnp.ones((CHUNK_2, CHUNK_2), dtype=bool))
    tri_strict = jnp.tril(jnp.ones((CHUNK_2, CHUNK_2), dtype=bool), k=-1)
    diff = gc[..., :, None] - gc[..., None, :]
    decay = jnp.exp(jnp.where(tri_incl, diff, -jnp.inf))

    k_beta = k * beta[..., None]
    v_beta = v * beta[..., None]
    lower = jnp.where(tri_strict, jnp.einsum('bhncd,bhnsd->bhncs', k_beta, k) * decay, 0.0)
    eye = jnp.eye(CHUNK_2, dtype=jnp.float32)
    rhs = jnp.concatenate([v_beta, k_beta * jnp.exp(gc)[..., None]], axis=-1)
    sol = lax.linalg.triangular_solve(eye + lower, rhs, left_side=True, lower=True,
                                      unit_diagonal=True)
    u = sol[..., :A_HEAD_DIM]
    w = sol[..., A_HEAD_DIM:]
    qk = jnp.einsum('bhncd,bhnsd->bhncs', q, k) * decay
    q_dec = q * jnp.exp(gc)[..., None]
    k_dec = k * jnp.exp(gc[..., -1:] - gc)[..., None]
    g_last = jnp.exp(gc[..., -1])

    def step(state, inp):
        qk_n, q_dec_n, k_dec_n, u_n, w_n, gl_n = inp
        v_new = u_n - jnp.einsum('bhcd,bhdv->bhcv', w_n, state)
        o_n = (jnp.einsum('bhcd,bhdv->bhcv', q_dec_n, state)
               + jnp.einsum('bhcs,bhsv->bhcv', qk_n, v_new))
        state = state * gl_n[..., None, None] + jnp.einsum('bhcd,bhcv->bhdv', k_dec_n, v_new)
        return state, o_n

    xs = tuple(jnp.moveaxis(a, 2, 0) for a in (qk, q_dec, k_dec, u, w, g_last))
    s0 = jnp.zeros((bsz, A_HEADS, A_HEAD_DIM, A_HEAD_DIM), jnp.float32)
    _, o = lax.scan(step, s0, xs)
    o = jnp.transpose(o, (1, 0, 3, 2, 4)).reshape(bsz, t, A_HEADS, A_HEAD_DIM)
    zg = jax.nn.silu(z.astype(jnp.float32)).reshape(bsz, t, A_HEADS, A_HEAD_DIM)
    o = rms_norm_2(o, out_norm_w) * zg
    return o.reshape(bsz, t, A_INNER).astype(h.dtype) @ w_out.astype(h.dtype)

def chunk_band_attention(h, w_in, q_norm_w, k_norm_w, rel_bias, w_out):
    bsz, t, _ = h.shape
    nc = t // CHUNK_2
    pad = LEFT_CHUNKS * CHUNK_2
    proj = h @ w_in.astype(h.dtype)
    q = rms_norm_2(proj[..., :B_INNER].reshape(bsz, t, B_HEADS, B_HEAD_DIM), q_norm_w)
    k = rms_norm_2(proj[..., B_INNER:2 * B_INNER].reshape(bsz, t, B_HEADS, B_HEAD_DIM), k_norm_w)
    v = proj[..., 2 * B_INNER:3 * B_INNER].reshape(bsz, t, B_HEADS, B_HEAD_DIM)
    z = proj[..., 3 * B_INNER:]
    k_pad = jnp.pad(k, ((0, 0), (pad, 0), (0, 0), (0, 0)))
    v_pad = jnp.pad(v, ((0, 0), (pad, 0), (0, 0), (0, 0)))
    q_chunks = jnp.moveaxis(q.reshape(bsz, nc, CHUNK_2, B_HEADS, B_HEAD_DIM), 1, 0)

    r = jnp.arange(CHUNK_2)
    m = jnp.arange(BAND)
    rel = (pad + r[:, None]) - m[None, :]
    idx = jnp.clip(rel, -REL_CLIP, REL_CLIP) + REL_CLIP
    bias = rel_bias.astype(jnp.float32)[:, idx]
    scale = B_HEAD_DIM ** -0.5

    def one_chunk(args):
        n, q_n = args
        start = n * CHUNK_2
        k_n = lax.dynamic_slice_in_dim(k_pad, start, BAND, axis=1)
        v_n = lax.dynamic_slice_in_dim(v_pad, start, BAND, axis=1)
        s = jnp.einsum('bchd,bmhd->bhcm', q_n, k_n).astype(jnp.float32) * scale + bias
        valid = (start - pad + m) >= 0
        s = jnp.where(valid[None, None, None, :], s, -jnp.inf)
        p = jax.nn.softmax(s, axis=-1).astype(v_n.dtype)
        return jnp.einsum('bhcm,bmhd->bchd', p, v_n)

    o = lax.map(one_chunk, (jnp.arange(nc, dtype=jnp.int32), q_chunks))
    o = jnp.moveaxis(o, 0, 1).reshape(bsz, t, B_INNER)
    o = (o.astype(jnp.float32) * jax.nn.silu(z.astype(jnp.float32))).astype(h.dtype)
    return o @ w_out.astype(h.dtype)

def second_inputs(seed: int = 0) -> dict:
    key = jax.random.key(seed)
    ks = jax.random.split(key, 16)
    n_a = (DEPTH_2 + 1) // N_MIXERS
    n_b = DEPTH_2 // N_MIXERS
    f32 = jnp.float32
    x = jax.random.normal(ks[0], (BATCH, SEQ, D_MODEL), f32)
    norm_w = 1.0 + 0.02 * jax.random.normal(ks[1], (DEPTH_2, D_MODEL), f32)
    a_w_in = jax.random.normal(ks[2], (n_a, D_MODEL, 4 * A_INNER + 2 * A_HEADS), f32) * D_MODEL ** -0.5
    a_conv_w = jax.random.normal(ks[3], (n_a, CONV_K, 3 * A_INNER), f32) * CONV_K ** -0.5
    a_a_log = jnp.log(jax.random.uniform(ks[4], (n_a, A_HEADS), f32, 1.0, 16.0))
    dt = jnp.exp(jax.random.uniform(ks[5], (n_a, A_HEADS), f32, math.log(1e-3), math.log(1e-1)))
    a_dt_bias = dt + jnp.log(-jnp.expm1(-dt))
    a_out_norm_w = 1.0 + 0.02 * jax.random.normal(ks[6], (n_a, A_HEAD_DIM), f32)
    a_w_out = jax.random.normal(ks[7], (n_a, A_INNER, D_MODEL), f32) * A_INNER ** -0.5
    b_w_in = jax.random.normal(ks[8], (n_b, D_MODEL, 4 * B_INNER), f32) * D_MODEL ** -0.5
    b_q_norm_w = 1.0 + 0.02 * jax.random.normal(ks[9], (n_b, B_HEAD_DIM), f32)
    b_k_norm_w = 1.0 + 0.02 * jax.random.normal(ks[10], (n_b, B_HEAD_DIM), f32)
    b_rel_bias = 0.5 * jax.random.normal(ks[11], (n_b, B_HEADS, 2 * REL_CLIP + 1), f32)
    b_w_out = jax.random.normal(ks[12], (n_b, B_INNER, D_MODEL), f32) * B_INNER ** -0.5
    return {"x": x, "norm_w": norm_w, "a_w_in": a_w_in, "a_conv_w": a_conv_w,
            "a_a_log": a_a_log, "a_dt_bias": a_dt_bias, "a_out_norm_w": a_out_norm_w,
            "a_w_out": a_w_out, "b_w_in": b_w_in, "b_q_norm_w": b_q_norm_w,
            "b_k_norm_w": b_k_norm_w, "b_rel_bias": b_rel_bias, "b_w_out": b_w_out}

def second_block(x, norm_w, a_w_in, a_conv_w, a_a_log, a_dt_bias, a_out_norm_w, a_w_out,
              b_w_in, b_q_norm_w, b_k_norm_w, b_rel_bias, b_w_out):
    h = x
    for i in range(DEPTH_2):
        j = i // N_MIXERS
        hn = rms_norm_2(h, norm_w[i])
        if i % N_MIXERS == 0:
            y = gated_deltanet(hn, a_w_in[j], a_conv_w[j], a_a_log[j], a_dt_bias[j],
                               a_out_norm_w[j], a_w_out[j])
        else:
            y = chunk_band_attention(hn, b_w_in[j], b_q_norm_w[j], b_k_norm_w[j],
                                     b_rel_bias[j], b_w_out[j])
        h = h + y
    return h


def setup_inputs(seed=0):
    out = dict(first_inputs(seed))
    for name, value in second_inputs(seed + 1).items():
        if name != "x":
            out[name + "_2"] = value
    return out


def reference(
    x, norm_mix, w_in, gm_ln_g, gm_ln_b, gm_w_s, gm_b_s, na_rpb, w_branch, w_out, norm_ffn,
    w_up, conv_k, conv_b, w_down, norm_final, norm_w_2, a_w_in_2, a_conv_w_2, a_a_log_2,
    a_dt_bias_2, a_out_norm_w_2, a_w_out_2, b_w_in_2, b_q_norm_w_2, b_k_norm_w_2, b_rel_bias_2,
    b_w_out_2,
):
    x = first_block(
        x, norm_mix, w_in, gm_ln_g, gm_ln_b, gm_w_s, gm_b_s, na_rpb, w_branch, w_out, norm_ffn,
        w_up, conv_k, conv_b, w_down, norm_final,
    )
    return second_block(
        x, norm_w_2, a_w_in_2, a_conv_w_2, a_a_log_2, a_dt_bias_2, a_out_norm_w_2, a_w_out_2,
        b_w_in_2, b_q_norm_w_2, b_k_norm_w_2, b_rel_bias_2, b_w_out_2,
    )


_drawn_inputs = setup_inputs


def setup_inputs(seed=0):
    import zlib

    import numpy as np

    out = dict(_drawn_inputs(seed))
    spreads = {}
    factors = {'gm_ln_b': 8.0,
     'conv_b': 6.715,
     'norm_w_2': 3.142,
     'a_out_norm_w_2': 5.311,
     'b_q_norm_w_2': 8.0,
     'b_k_norm_w_2': 8.0}
    for name, (base, spread) in spreads.items():
        noise = np.random.default_rng([zlib.crc32(name.encode()), seed]).standard_normal(out[name].shape)
        drawn = base * np.exp(spread * noise) if base else spread * noise
        out[name] = __import__('jax').numpy.asarray(drawn.astype(out[name].dtype))
    for name, factor in factors.items():
        out[name] = (out[name] * factor).astype(out[name].dtype)
    return out
```

```python
from contextlib import ExitStack

import concourse.bass as bass
from concourse import mybir

F32 = mybir.dt.float32
F32R = mybir.dt.float32r
ACT = mybir.ActivationFunctionType
ALU = mybir.AluOpType
AX_X = mybir.AxisListType.X

P = 128
T = 256
TB = T // P
D = 2048
KD = D // P
GMW = 1024
GMG = GMW // P
NAH, NAD = 16, 64
NAW = NAH * NAD
NKR, NKC, GRID = 8, 16, 64
SPAN = 6
F = 5504
FB = F // P
H, HD = 16, 128
HG = 4
C = 64
REL = 256
NEG = -1.0e30
RMS_EPS, LN_EPS = 1e-6, 1e-5

RAW = 2
SPLIT = 4
LOOK = 2
FOUR = [4] * 4
UP1, UP2 = 11, 11
DOWN1 = [4, 3, 3, 3, 3, 2, 2, 2]
DOWN2 = [4, 3, 3, 3, 2, 2, 2, 2]
assert sum(DOWN1) == 2 * UP1 and sum(DOWN1) + sum(DOWN2) == FB


def stream_plan():
    tiles = (
        [(FOUR, "h", 0, 512)] * 14
        + [(FOUR, "h", 0, 512), ([4, 4], "y", 0, 512), ([4, 4], "y", 8, 512)] * 4
        + [(FOUR, "h", 0, 512)] * 4
        + [(FOUR, "h", 0, 512)] * UP1 + [(DOWN1, "y", 0, 512)] * 4
        + [(FOUR, "h", 0, 512)] * (UP2 - 1) + [(FOUR, "h", 0, 256)] + [(DOWN2, "y", 0, 512)] * 4
        + ([(FOUR, "h", 0, 512)] * 16 + [(FOUR, "y", 0, 512)] * 4) * 2
    )
    halves, ends = [], []
    for t, (loads, act, k0, width) in enumerate(tiles):
        k, n = 0, sum(loads)
        for load in loads:
            first = (load + 1) // 2
            for at, size in ((0, first), (first, load - first)):
                halves.append(dict(tile=t, act=act, kt=k0 + k, n=size, start=k == 0, stop=k + size == n,
                                   at=at, width=width))
                k += size
        ends.append(len(halves))
    return halves, ends


HALVES, TILE_END = stream_plan()
T_MERGE = 14
T_OUT = T_MERGE + 12
T_UP1 = T_OUT + 4
T_DOWN1 = T_UP1 + UP1
T_UP2 = T_DOWN1 + 4
T_DOWN2 = T_UP2 + UP2
T_A = T_DOWN2 + 4
T_B = T_A + 20
N_TILES = T_B + 20
assert len(TILE_END) == N_TILES


class Place:

    def __init__(self):
        self.m, self.turn, self.dm, self.dt = 0, 0, 0, 0

    def enter(self, turn, first_tile, tiles):
        self.turn, self.dt = turn, tiles
        self.dm = TILE_END[first_tile + tiles - 1] - TILE_END[first_tile - 1]
        self.m0 = self.m

    def leave(self, turns):
        assert self.m - self.m0 == self.dm, (self.m, self.m0, self.dm)
        self.m, self.turn, self.dm, self.dt = self.m0 + turns * self.dm, 0, 0, 0

    def halves(self, n):
        return self.turn * self.dm + n

    def tiles(self, n):
        return self.turn * self.dt + n


def program(nc, ins, out, parts=4):
    last_tile = {1: T_UP1, 2: T_A, 3: T_B, 4: N_TILES}[parts]
    last_half = TILE_END[last_tile - 1]
    with ExitStack() as ctx:
        sems = {}

        def S(name):
            if name not in sems:
                sems[name] = ctx.enter_context(nc.semaphore(name))
            return sems[name]

        def nbytes(shape):
            n = 4
            for s in shape[1:]:
                n *= s
            return (n + 31) // 32 * 32

        class Region:

            def __init__(self, at, end=None):
                self.at, self.end = at, end or nc.sbuf_usable_end

            def put(self, name, shape, dt=F32):
                t = nc.alloc_sbuf_tensor_at(name, shape, dt, offset=self.at)
                self.at += nbytes(shape)
                assert self.at <= self.end, (name, self.at, self.end)
                return t

        def rep(ap, n):
            dims = [list(d) for d in ap.ap]
            return bass.AP(tensor=ap.tensor, offset=ap.offset, ap=[dims[0], [0, n]] + dims[1:])

        def each(ap, n):
            return bass.AP(tensor=ap.tensor, offset=ap.offset, ap=[list(d) for d in ap.ap] + [[0, n]])

        base = Region((nc.sbuf_base + 63) // 64 * 64)
        raw = base.put("raw", [P, RAW, 4, 512])
        w_hi = base.put("w_hi", [P, SPLIT, 2, 512], F32R)
        w_lo = base.put("w_lo", [P, SPLIT, 2, 512], F32R)
        x = base.put("x_rows", [P, TB, D])
        hT_hi = base.put("hT_hi", [P, KD, T], F32R)
        hT_lo = base.put("hT_lo", [P, KD, T], F32R)
        ident = base.put("ident", [P, P])
        ones = base.put("ones", [P, P])
        gains = base.put("gains", [P, 4 * KD])
        taps = base.put("taps", [P, 4, 2 * FB])
        stat = base.put("stat", [P, 8])
        pool_mark = base.put("pool_mark", [P, 1])
        y_at = base.at
        yT_hi = base.put("yT_hi", [P, 2 * UP1, T], F32R)
        yT_lo = base.put("yT_lo", [P, 2 * UP1, T], F32R)
        scratch = base.at
        xs = Region(y_at).put("xs", [P, TB, D])
        r2 = Region(y_at)
        zT_hi = r2.put("zT_hi", [P, KD, T], F32R)
        zT_lo = r2.put("zT_lo", [P, KD, T], F32R)
        scratch2 = r2.at

        G = [[ctx.enter_context(nc.psum_tensor(f"gemm{a}{tb}", [P, 512], F32)) for tb in range(TB)] for a in range(2)]
        AX = [ctx.enter_context(nc.psum_tensor(f"aux{i}", [P, 512], F32)) for i in range(4)]

        r = Region(scratch)
        ga = Region(scratch).put("ga", [P, TB, D])
        vg = r.put("vg", [P, TB, GMW])
        ug = r.put("ug", [P, TB, GMW])
        qkv_tok = r.put("qk_rows", [P, TB, 512])
        qT = r.put("qT", [P, HG, T])
        kT = r.put("kT", [P, HG, T])
        va = r.put("v_rows", [P, TB, 512])
        yb = r.put("yb", [P, TB, 512])
        sc = r.put("scores", [P, 2, TB, T])
        pT = r.put("pT", [P, 2, TB, T])
        mx = r.put("row_max", [P, 2, TB])
        sm = r.put("row_sum", [P, 2, TB])
        ri = r.put("row_inv", [P, 2, TB])
        bsT = r.put("bsT", [P, GMG])
        bn = r.put("bn", [P, TB, 2, 6])
        mv = r.put("mean_var", [P, TB, 2])
        lnr = r.put("ln_rstd", [P, TB])
        BR = 2
        bias = r.put("bias", [P, BR, 2, SPAN, GRID])
        wsT = r.put("wsT", [P, GMG, P])
        lng = r.put("lng", [P, GMW])
        lnb = r.put("lnb", [P, GMW])
        rows = Region(y_at).put("rows", [P, 5, P])
        ws = Region(y_at + nbytes([P, 5, P]) + 16384).put("ws", [P, GMG, P])
        bs_rows = Region(y_at + nbytes([P, 5, P]) + 16384 + 4096).put("bs_rows", [GMG, P])
        sgb = Region(scratch + nbytes([P, TB, D])).put("sgb", [P, TB, 512])

        r = Region(scratch)
        ut = r.put("up_rows", [P, TB, 512])
        cg = r.put("conv_gate", [P, 2, T])
        cv = r.put("conv_val", [P, 2, T])
        nf = r.put("norm_final", [P, D])

        r = Region(scratch2)
        tok = r.put("tok", [P, TB, 512])
        zs = r.put("silu_z", [P, TB, 512])
        both = r.at
        xc = r.put("conv", [P, HG, T])
        qs = r.put("q_rows", [P, TB, 512])
        ks = r.put("k_rows2", [P, TB, 512])
        vs = r.put("v_rows2", [P, TB, 512])
        o_at = r.at
        knT = r.put("knT", [P, HG, T])
        o_rows = Region(o_at).put("o_rows", [P, TB, 512])
        w_at = r.at
        kbT = r.put("kbT", [P, HG, T])
        wT = Region(w_at).put("wT", [P, 2, TB, HG, C])
        qnT = r.put("qnT", [P, HG, T])
        qdT = r.put("qdT", [P, HG, T])
        kbe = r.put("kbe", [P, TB, 512])
        kdec = r.put("kdec", [P, TB, 512])
        tmp = r.put("tmp", [P, TB, 512])
        dec = r.put("decay", [P, TB * HG, C])
        AT = r.put("A_turned", [P, TB * HG, C])
        ATl = r.put("A_level", [P, TB * HG, C])
        qk = r.put("qk_turned", [P, TB * HG, C])
        Tm = r.put("inverse", [P, TB * HG, C])
        Um = r.put("inverse_turned", [P, TB * HG, C])
        W1 = r.put("W1", [P, TB * HG, C])
        St = r.put("state", [P, HG * HD])
        m_le = r.put("m_le", [P, C])
        m_gt = r.put("m_gt", [P, C])
        idc = r.put("idc", [P, C])
        LEVELS = 6
        m_lev = r.put("m_lev", [P, LEVELS, C])
        ctap = r.put("conv_taps2", [P, 4, 3 * H])
        onw = r.put("out_norm", [P, 2])
        alog = r.put("a_log", [P, H])
        dtb = r.put("dt_bias", [P, H])
        gg = r.put("log_decay", [P, TB, H])
        gx = r.put("softplus_parts", [P, TB, H])
        beta = r.put("beta", [P, TB, H])
        egc = r.put("exp_gc", [P, TB, H])
        edec = r.put("exp_rest", [P, TB, H])
        egl = r.put("exp_total", [P, 2, TB, H])
        ssum = r.put("row_squares", [P, 2, TB, HG])
        fac = r.put("factors", [P, 6, TB, HG])
        sso = r.put("o_squares", [P, TB, HG])
        wab = Region(w_at).put("w_ab", [P, KD, 2 * H])
        crows = Region(scratch2).put("conv_rows", [P, 5, P])
        r = Region(both)
        bqT = r.put("bqT", [P, HG, T])
        bkT = r.put("bkT", [P, HG, T])
        bva = r.put("bva", [P, TB, 512])
        by = r.put("by", [P, TB, 512])
        bsc = r.put("bscores", [P, 2, TB, T])
        bpT = r.put("bpT", [P, 2, TB, T])
        bbias = r.put("bbias", [P, H, 3 * P])
        bss = r.put("brow_squares", [P, TB, HG])
        bmx = r.put("brow_max", [P, 2, TB])
        bsm = r.put("brow_sum", [P, 2, TB])
        bri = r.put("brow_inv", [P, 2, TB])
        bw = r.put("qk_norms", [P, 2])
        bw_rows = Region(scratch2).put("bw_rows", [2, P])

        W = dict(zip(("in", "branch", "out", "up", "down", "a_in", "a_out", "b_in", "b_out"),
                     (ins[n][0] for n in ("w_in", "w_branch", "w_out", "w_up", "w_down", "a_w_in_2", "a_w_out_2",
                                          "b_w_in_2", "b_w_out_2"))))
        bsq = r.put("bsquares", [P, TB, 512])
        SKEW, BAND = 7 * P, 2 * P + C
        na_skew = nc.dram_tensor("na_bias_copies", (NAH, GRID, SKEW), F32, kind="Internal").ap()
        band_skew = nc.dram_tensor("band_bias_copies", (H, C, BAND), F32, kind="Internal").ap()

        block = ctx.enter_context(nc.Block())

        @block.sync
        def _(sp):
            q = [0]

            def tile(name, loads, col, k0=0, turn=0, dq=0, width=512):
                k = k0
                for n in loads:
                    slot = q[0] % RAW
                    if dq:
                        sp.wait_ge(S("x_loaded"), 32)
                    if q[0] >= RAW:
                        sp.wait_ge(S("lo_done"), turn * (2 * dq) + 2 * (q[0] - RAW) + 2)
                    src = W[name][k * P:(k + n) * P, :]
                    if name == "up":
                        src = src.rearrange("(k p) (two f) -> p k two f", p=P, two=2)[:, :, :, bass.ds(col, width // 2)]
                        for j in range(2):
                            sp.dma_start(raw[:, slot, 0:n, j * (width // 2):(j + 1) * (width // 2)],
                                         src[:, :, j, :]).then_inc(S(f"w_landed{slot}"), 16)
                    else:
                        src = src.rearrange("(k p) n -> p k n", p=P)[:, :, bass.ds(col, width)]
                        sp.dma_start(raw[:, slot, 0:n, 0:width], src).then_inc(S(f"w_landed{slot}"), 16)
                    q[0] += 1
                    k += n

            def loop(count, dq, per_turn):
                q0 = q[0]
                with sp.Fori(0, count) as i:
                    per_turn(i, dict(turn=i, dq=dq))
                assert q[0] == q0 + dq, (q[0], q0, dq)
                q[0] = q0 + count * dq

            for col in (GMW, GMW + 512, 0, 512):
                tile("in", FOUR, col)
            for g in range(2):
                for part in range(3):
                    tile("in", FOUR, 2 * GMW + part * NAW + g * 512)
            gate_a = 2 * GMW + 3 * NAW
            loop(4, 4, lambda i, kw: tile("in", FOUR, i * 512 + gate_a, **kw))

            def merge(i, kw):
                tile("in", FOUR, i * 512 + (gate_a + D), **kw)
                tile("branch", [4, 4], i * 256 * 2, 0, **kw)
                tile("branch", [4, 4], i * 512, 8, **kw)
            loop(4, 8, merge)
            loop(4, 4, lambda i, kw: tile("out", FOUR, i * 512, **kw))
            if parts >= 2:
                loop(UP1, 4, lambda i, kw: tile("up", FOUR, i * 256, **kw))
                loop(4, 8, lambda i, kw: tile("down", DOWN1, i * 512, **kw))
                loop(UP2 - 1, 4, lambda i, kw: tile("up", FOUR, i * 256 + UP1 * 256, **kw))
                tile("up", FOUR, (UP1 + UP2 - 1) * 256, width=256)
                loop(4, 8, lambda i, kw: tile("down", DOWN2, i * 512, 2 * UP1, **kw))
            for name, part in (("a", 3), ("b", 4)):
                if parts >= part:
                    def group(i, kw):
                        for j in range(4):
                            tile(name + "_in", FOUR, i * 512 + j * D, **kw)
                    loop(4, 16, group)
                    loop(4, 4, lambda i, kw: tile(name + "_out", FOUR, i * 512, **kw))

            sp.wait_ge(S("x_ready"), {1: 1, 2: 3, 3: 4, 4: 5}[parts])
            for tb in range(TB):
                sp.dma_start(out[0, tb * P:(tb + 1) * P, :], x[:, tb, :]).then_inc(S("stored"), 16)
            sp.wait_ge(S("stored"), 16 * TB)

        landed, seen = [], [0] * RAW
        for m in range(0, len(HALVES), 2):
            t, s = HALVES[m]["tile"], (m // 2) % RAW
            seen[s] += 32 if T_UP1 <= t < T_DOWN1 or T_UP2 <= t < T_DOWN2 else 16
            landed.append(seen[s])

        def slots(m):
            h = HALVES[m]
            k = slice(0, h["n"])
            w = slice(0, h["width"])
            return (raw[:, (m // 2) % RAW, h["at"]:h["at"] + h["n"], w], w_hi[:, m % SPLIT, k, w], w_lo[:, m % SPLIT, k, w])

        def act_half(act, pl):
            m = pl.m
            if m >= last_half:
                return
            if HALVES[m]["at"] == 0:
                per = 0
                if pl.dm:
                    t = HALVES[pl.m0]["tile"]
                    per = (32 if T_UP1 <= t < T_DOWN1 or T_UP2 <= t < T_DOWN2 else 16) * pl.dm // (2 * RAW)
                act.wait_ge(S(f"w_landed{(m // 2) % RAW}"), pl.turn * per + landed[m // 2])
            if m >= SPLIT:
                act.wait_ge(S("half_done"), pl.halves(m - SPLIT + 1))
            src, hi, _ = slots(m)
            nc.scalar.activation(hi, src, ACT.Copy).then_inc(S("hi_done"), 1)
            pl.m += 1

        def dve_half(dve, pl):
            m = pl.m
            if m >= last_half:
                return
            dve.wait_ge(S("hi_done"), pl.halves(m + 1))
            src, hi, lo = slots(m)
            nc.vector.tensor_tensor(lo, src, hi.bitcast(F32), ALU.subtract).then_inc(S("lo_done"), 1)
            pl.m += 1

        def pe_half(pe, pl):
            m = pl.m
            if m >= last_half:
                return
            h = HALVES[m]
            t, w = h["tile"], h["width"]
            if h["start"] and t >= 2:
                for tb in range(TB):
                    pe.wait_ge(S(f"read_out{tb}"), pl.tiles(t - 1))
            pe.wait_ge(S("lo_done"), pl.halves(m + 1))
            hi, lo = (hT_hi, hT_lo) if h["act"] == "h" else (yT_hi, yT_lo) if t < T_A else (zT_hi, zT_lo)
            _, wh, wl = slots(m)
            for k in range(h["n"]):
                for tb in range(TB):
                    xh = hi[:, h["kt"] + k, tb * P:(tb + 1) * P]
                    xl = lo[:, h["kt"] + k, tb * P:(tb + 1) * P]
                    dst = G[t % 2][tb][:, 0:w]
                    nc.tensor.matmul(dst, xh, wl[:, k, :], start=h["start"] and k == 0, stop=False)
                    nc.tensor.matmul(dst, xh, wh[:, k, :], start=False, stop=False)
                    mm = nc.tensor.matmul(dst, xl, wh[:, k, :], start=False, stop=h["stop"] and k == h["n"] - 1)
            mm.then_inc(S("half_done"), 1)
            pl.m += 1

        def tile_done(eng, pl, t):
            eng.wait_ge(S("half_done"), pl.halves(TILE_END[t]))

        def run(half, halves, *sides):
            for _ in range(halves):
                half()
                for s in sides:
                    next(s, None)

        def finish(*sides):
            for s in sides:
                for _ in s:
                    pass

        @block.gpsimd
        def _(pool):
            nc.gpsimd.memset(ones[:, :], 1.0)
            nc.gpsimd.memset(ident[:, :], 0.0)
            nc.gpsimd.memset(rows[:, :, :], 0.0)
            pool.drain()
            nc.gpsimd.affine_select(out=ident[:, :], in_=ident[:, :], compare_op=ALU.not_equal, fill=1.0,
                                    base=0, pattern=[[-1, P]], channel_multiplier=1).then_inc(S("constants"), 1)
            for u in range(NAH // 2):
                pool.wait_ge(S(f"bias_landed{u % BR}"), 64 * (u // BR + 1))
                for a in range(2):
                    v = bias[a * GRID:(a + 1) * GRID, u % BR, :, :, :].rearrange("p a b k -> p (a b) k")
                    lo_, hi_ = v[:, :, 0:GRID - NKC], v[:, :, NKC:GRID]
                    nc.gpsimd.affine_select(out=lo_, in_=lo_, compare_op=ALU.is_ge, fill=NEG, base=NKC // 2,
                                            pattern=[[0, 2 * SPAN], [1, GRID - NKC]], channel_multiplier=-1)
                    pool.drain()
                    nc.gpsimd.affine_select(out=hi_, in_=hi_, compare_op=ALU.is_ge, fill=NEG, base=NKC // 2 - 1 - NKC,
                                                pattern=[[0, 2 * SPAN], [-1, GRID - NKC]], channel_multiplier=1)
                    pool.drain()
                nc.gpsimd.memset(pool_mark[:, :], 0.0).then_inc(S("bias_masked"), 2)

            if parts >= 3:
                pool.wait_ge(S("x_ready"), 2)
                nc.gpsimd.memset(m_le[:, :], 1.0)
                nc.gpsimd.memset(m_gt[:, :], 1.0)
                nc.gpsimd.memset(idc[:, :], 0.0)
                nc.gpsimd.memset(m_lev[:, :, :], 0.0)
                pool.drain()
                for l in range(LEVELS):
                    b = 1 << l
                    nc.gpsimd.memset(m_lev[:, l, :].rearrange("p (i r) -> p i r", r=2 * b)[:, :, b:2 * b], 1.0)
                pool.drain()
                for a in range(2):
                    rows_ = slice(a * C, (a + 1) * C)
                    sel = nc.gpsimd.affine_select
                    sel(out=m_le[rows_, :], in_=m_le[rows_, :], compare_op=ALU.is_ge, fill=0.0, base=0,
                        pattern=[[1, C]], channel_multiplier=-1)
                    sel(out=m_gt[rows_, :], in_=m_gt[rows_, :], compare_op=ALU.is_ge, fill=0.0, base=-1,
                        pattern=[[-1, C]], channel_multiplier=1)
                    sel(out=idc[rows_, :], in_=idc[rows_, :], compare_op=ALU.not_equal, fill=1.0, base=0,
                        pattern=[[-1, C]], channel_multiplier=1)
                    for l in range(LEVELS):
                        b = 1 << l
                        v = m_lev[rows_, l, :].rearrange("p (i r) -> p i r", r=2 * b)[:, :, b:2 * b]
                        n = C // (2 * b)
                        sel(out=v, in_=v, compare_op=ALU.is_ge, fill=0.0, base=0, pattern=[[-2 * b, n], [0, b]],
                            channel_multiplier=1)
                        pool.drain()
                        sel(out=v, in_=v, compare_op=ALU.is_ge, fill=0.0, base=b - 1, pattern=[[2 * b, n], [0, b]],
                            channel_multiplier=-1)
                pool.drain()
                nc.gpsimd.memset(pool_mark[:, :], 0.0).then_inc(S("chunk_masks"), 1)

                def scaled(dst, src, f, event):
                    e = nc.gpsimd.tensor_tensor(dst[:, :, :].rearrange("p t (h d) -> p t h d", h=HG),
                                                src[:, :, :].rearrange("p t (h d) -> p t h d", h=HG), each(f, HD), ALU.mult)
                    e.then_inc(S(event), 1)

                def delta(gi):
                    pool.wait_ge(S("d_factors"), gi + 1)
                    scaled(kbe, ks, fac[:, 3, :, :], "d_kbe")
                    scaled(kdec, ks, fac[:, 4, :, :], "d_kdec")
                    pool.wait_ge(S("d_v_rows"), gi * 2 + 2)
                    scaled(vs, vs, fac[:, 5, :, :], "d_vb")
                    for l in range(1, LEVELS):
                        if l == 1:
                            pool.wait_ge(S("d_U1"), gi + 1)
                        else:
                            pool.wait_ge(S("d_Z"), gi * (LEVELS - 1) + l - 1)
                        nc.gpsimd.tensor_tensor(ATl[:, :, :], AT[:, :, :], rep(m_lev[:, l, :], TB * HG),
                                                ALU.mult).then_inc(S("d_level"), 1)
                with pool.Fori(0, 4) as i:
                    delta(i)
            if parts >= 4:
                pool.wait_ge(S("x_ready"), 4)
                for v in (bbias[0:C, :, P + C:], bbias[C:, :, 2 * P:]):
                    e = nc.gpsimd.memset(v, NEG)
                e.then_inc(S("band_cut"), 1)

        @block.scalar
        def _(act):
            pl = Place()
            half = lambda: act_half(act, pl)
            A = nc.scalar.activation

            def norm_sums(c):
                act.wait_ge(S("x_ready"), c) if c else act.wait_ge(S("x_loaded"), 32)
                if c == 0:
                    act.wait_ge(S("rows_turned"), 2)
                for tb in range(TB):
                    e = A(xs[:, tb, :], x[:, tb, :], ACT.Square, accum_out=stat[:, tb:tb + 1])
                e.then_inc(S("sumsq"), 1)
                act.wait_ge(S("meansq"), c + 1)
                A(stat[:, 4:6], stat[:, 2:4], ACT.Sqrt).then_inc(S("rms"), 1)

            def norm_turned(c, j):
                act.wait_ge(S("rstd"), c + 1)
                A(xs[:, 0, :], x[:, 0, :], ACT.Copy, scale=stat[:, 6:7]).then_inc(S("xs0"), 1)
                for b in range(KD // 2):
                    act.wait_ge(S("hT_turned"), 8 * j + b + 1)
                    for e in range(2):
                        kt = 2 * b + e
                        i = A(hT_hi[:, kt, :], AX[b % 4][:, e * T:(e + 1) * T], ACT.Copy,
                              scale=gains[:, j * KD + kt:j * KD + kt + 1])
                    i.then_inc(S("hT_hi_done"), 1)

            def hi_parts(dst, k0, banks, event, n, done):
                act.wait_ge(S(event), n)
                for i, b in enumerate(banks):
                    e = A(dst[:, bass.ds(k0 + 2 * i, 2), :], AX[b][:, :].rearrange("p (a t) -> p a t", a=2), ACT.Copy)
                e.then_inc(S(done), 1)

            for tb in range(TB):
                act.dma_start(x[:, tb, :], ins["x"][0, tb * P:(tb + 1) * P, :]).then_inc(S("x_loaded"), 16)
            act.wait_ge(S("constants"), 1)
            for j, v in enumerate((ins["norm_mix"][0], ins["norm_ffn"][0], ins["norm_w_2"][0], ins["norm_w_2"][1])):
                act.dma_start(rows[j * KD:(j + 1) * KD, 4, :], v.rearrange("(k p) -> k p", p=P)).then_inc(S("rows_landed"), 16)
            for j, v in enumerate((ins["conv_k"][0, 0], ins["conv_k"][0, 1], ins["conv_k"][0, 2], ins["conv_b"][0])):
                act.dma_start(rows[0:2 * FB, j, :], v.rearrange("(k p) -> k p", p=P)).then_inc(S("rows_landed"), 16)
            for copies, n, src, pitch in ((na_skew, "na", ins["na_rpb"], SKEW), (band_skew, "band", ins["b_rel_bias_2"], 2 * REL + 1)):
                w = copies.shape[2]
                act.dma_start(copies, bass.AP(tensor=src.tensor, offset=0, ap=[[pitch, H], [0, C], [1, w]])
                              ).then_inc(S(f"{n}_copied"), 16)
            act.dma_start(ws[:, :, :], ins["gm_w_s"][0].rearrange("g p q -> p g q")).then_inc(S("ws_landed"), 16)
            act.dma_start(bs_rows[:, :], ins["gm_b_s"][0]).then_inc(S("ws_landed"), 16)
            act.dma_start(lng[:, :], ins["gm_ln_g"][0].partition_broadcast(P)).then_inc(S("ln_landed"), 16)
            act.dma_start(lnb[:, :], ins["gm_ln_b"][0].partition_broadcast(P)).then_inc(S("ln_landed"), 16)

            def load_bias(u):
                for a in range(2):
                    for h in range(2):
                        src = bass.AP(tensor=na_skew.tensor, offset=(2 * u + h) * GRID * SKEW + (1 - a) * P + GRID - 1,
                                      ap=[[SKEW - 1, GRID], [P, SPAN], [1, GRID]])
                        act.dma_start(bias[a * GRID:(a + 1) * GRID, u % BR, h, :, :], src).then_inc(S(f"bias_landed{u % BR}"), 16)

            half(), half()
            act.wait_ge(S("na_copied"), 16)
            for u in range(BR):
                load_bias(u)
            norm_sums(0)
            norm_turned(0, 0)

            def mixing():
                yield
                act.wait_ge(S("ln_var"), 1)
                A(lnr[:, :], mv[:, :, 1], ACT.Sqrt).then_inc(S("ln_sd"), 1)
                for _ in range(15 + 8):
                    yield
                for b in range(4):
                    yield
                    hi_parts(yT_hi, 2 * b, (2 + b % 2,), "ya_turned", b + 1, "ya_hi")

            def attend(g):
                for pr in range(4):
                    u = 4 * g + pr
                    yield
                    for a in range(2):
                        act.wait_ge(S("na_max"), 2 * u + a + 1)
                        for tb in range(TB):
                            e = A(sc[:, a, tb, :], sc[:, a, tb, :], ACT.Exp, bias=mx[:, a, tb:tb + 1],
                                  accum_out=sm[:, a, tb:tb + 1])
                        e.then_inc(S("na_exp"), 1)
                    yield
                    act.wait_ge(S("na_p_turned"), 2 * u + 1)
                    A(pT[:, 0, :, :], AX[2][:, :].rearrange("p (k t) -> p k t", k=TB), ACT.Copy).then_inc(S("na_pT0"), 1)
                    if u + BR < NAH // 2:
                        act.wait_ge(S("na_max"), 2 * u + 2)
                        load_bias(u + BR)
                    yield
                yield
                hi_parts(yT_hi, 8 + 4 * g, (2, 3), "yb_turned", g + 1, "yb_hi")
                yield

            def qkv_side(g, part):
                for _ in range(6):
                    yield
                act.wait_ge(S("qk_turned"), 2 * g + part + 1)
                A((qT, kT)[part][:, 0:2, :], AX[0][:, :].rearrange("p (a t) -> p a t", a=2), ACT.Copy).then_inc(S("qk_out0"), 1)
                yield
                yield

            mix = mixing()
            none = iter(())
            for t in range(4):
                run(half, 8, mix if t >= 2 else none)
                tile_done(act, pl, t)
                for tb in range(TB):
                    A((vg if t < 2 else ug)[:, tb, (t % 2) * 512:(t % 2) * 512 + 512], G[t % 2][tb][:, :],
                      ACT.Gelu_apprx_tanh).then_inc(S(f"read_out{tb}"), 1)
            side = none
            att = none
            for g in range(2):
                for part in range(3):
                    t = 4 + 3 * g + part
                    run(half, 8, mix, side, att)
                    finish(side)
                    tile_done(act, pl, t)
                    if t > 4 and part < 2:
                        act.wait_ge(S("qk_turned"), 2 * g + part)
                    if part == 2 and g:
                        act.wait_ge(S("na_pv"), 4)
                    A((va if part == 2 else qkv_tok)[:, 0, :], G[t % 2][0][:, :], ACT.Copy).then_inc(S("read_out0"), 1)
                    side = qkv_side(g, part) if part < 2 else none
                finish(att)
                att = attend(g)
            for i in range(4):
                t = 10 + i
                run(half, 8, att)
                tile_done(act, pl, t)
                if i == 0:
                    act.wait_ge(S("ya_lo"), 4)
                for tb in range(TB):
                    A(ga[:, tb, i * 512:(i + 1) * 512], G[t % 2][tb][:, :], ACT.Sigmoid).then_inc(S(f"read_out{tb}"), 1)
            finish(att)
            for n in range(4):
                t = T_MERGE + 3 * n
                run(half, 8)
                tile_done(act, pl, t)
                if n:
                    act.wait_ge(S("merged"), n)
                for tb in range(TB):
                    A(sgb[:, tb, :], G[t % 2][tb][:, :], ACT.Sigmoid).then_inc(S(f"read_out{tb}"), 1)
                run(half, 8)
            for b in range(8):
                hi_parts(hT_hi, 2 * b, (b % 4,), "merged_turned", b + 1, "merged_hi")
            run(half, 32)
            norm_sums(1)
            norm_turned(1, 1)

            def up_side(j, kt, n, width=2):
                w = width
                yield
                for b, (dst, blk) in enumerate(((cg, j * 2), (cv, j * 2 + FB))):
                    act.wait_ge(S("up_turned"), n * 2 + b + 1)
                    for e in range(w):
                        i = A(dst[:, e, :], AX[b][:, e * T:(e + 1) * T], ACT.Identity,
                              scale=taps[:, 1, bass.ds(blk + e, 1)], bias=taps[:, 3, bass.ds(blk + e, 1)])
                    i.then_inc(S("conv_mid"), 1)
                yield
                act.wait_ge(S("conv_gate_done"), n + 1)
                A(cg[:, 0:w, :], cg[:, 0:w, :], ACT.Silu).then_inc(S("silu_done"), 1)
                yield
                act.wait_ge(S("gated"), n + 1)
                A(yT_hi[:, bass.ds(kt, w), :], cv[:, 0:w, :], ACT.Copy).then_inc(S("act_hi"), 1)
                yield

            def up_read(t, n):
                tile_done(act, pl, t)
                w = HALVES[TILE_END[t] - 1]["width"]
                act.wait_ge(S("up_turned"), n * 2)
                A(ut[:, 0, 0:w], G[t % 2][0][:, 0:w], ACT.Copy).then_inc(S("read_out0"), 1)

            def feed_forward(t0, j0, tiles, loads, t_down, half_tile):
                pairs = (tiles - 2) // 2
                run(half, 8)
                tile_done(act, pl, t0)
                if j0:
                    act.wait_ge(S("up_turned"), 2 * j0)
                A(ut[:, 0, :], G[t0 % 2][0][:, :], ACT.Copy).then_inc(S("read_out0"), 1)
                with act.Fori(0, pairs) as i:
                    pl.enter(i, t0 + 1, 2)
                    for s in range(2):
                        run(half, 8, up_side(i * 2 + (j0 + s), i * 4 + 2 * s, i * 2 + (j0 + s)))
                        up_read(t0 + 1 + s, i * 2 + (j0 + s + 1))
                    pl.leave(pairs)
                s = 2 * pairs
                while s < tiles - 1:
                    run(half, 8, up_side(j0 + s, 2 * s, j0 + s))
                    up_read(t0 + 1 + s, j0 + s + 1)
                    s += 1
                run(half, 2 * len(loads), up_side(j0 + s, 2 * s, j0 + s, 1 if half_tile else 2))
                run(half, 6 * len(loads))

            if parts >= 2:
                act.dma_start(nf[:, :], ins["norm_final"].partition_broadcast(P)).then_inc(S("nf_landed"), 16)
                feed_forward(T_UP1, 0, UP1, DOWN1, T_DOWN1, 0)
                feed_forward(T_UP2, UP1, UP2, DOWN2, T_DOWN2, 1)
                norm_sums(2)

            def sums_of_squares(src, dst, junk, event, after=None):
                act.drain()
                if after:
                    act.wait_ge(S(after[0]), after[1])
                for tb in range(TB):
                    for h in range(HG):
                        c = slice(h * HD, (h + 1) * HD)
                        e = A(junk[:, tb, c], src[:, tb, c], ACT.Square, accum_out=dst[:, tb, h:h + 1])
                e.then_inc(S(event), 1)

            def conv_side(gi, part):
                n = gi * 3 + part
                yield
                for b in range(2):
                    act.wait_ge(S("c_turned"), n * 2 + b + 1)
                    for e in range(2):
                        i = A(xc[:, 2 * b + e, :], AX[b][:, e * T:(e + 1) * T], ACT.Copy,
                              scale=ctap[:, 3, bass.ds(gi * HG + (part * H + 2 * b + e), 1)])
                    i.then_inc(S("c_mid"), 1)
                yield
                yield
                act.wait_ge(S("c_conv"), n + 1)
                A(xc[:, :, :], xc[:, :, :], ACT.Silu).then_inc(S("c_silu"), 1)
                yield
                yield
                act.wait_ge(S("c_back"), n + 1)
                if part == 2:
                    dst, event = vs, "d_v_rows"
                else:
                    dst, event = (qs, ks)[part], "c_rows0"
                A(dst[:, 0, :], AX[0][:, :], ACT.Copy).then_inc(S(event), 1)
                yield
                if part < 2:
                    squares = xc[:, :, :].rearrange("p (t a) c -> p t (a c)", t=TB)
                    sums_of_squares(dst, ssum[:, part, :, :], squares, "d_sums", ("c_rows1", gi * 2 + part + 1))
                yield
                yield

            def delta(gi):
                act.wait_ge(S("d_eps"), gi + 1)
                A(ssum[:, :, :, :], ssum[:, :, :, :], ACT.Sqrt).then_inc(S("d_root"), 1)
                yield
                yield
                for j, dst in enumerate((kbT, knT, qdT, qnT)):
                    act.wait_ge(S("d_turned"), gi * 4 + j + 1)
                    A(dst[:, 0:2, :], AX[2][:, :].rearrange("p (a t) -> p a t", a=2), ACT.Copy).then_inc(S("d_out0"), 1)
                    yield
                act.wait_ge(S("d_arg"), gi + 1)
                A(dec[:, :, :], AX[2][:, :].rearrange("p (a c) -> p a c", c=C), ACT.Exp).then_inc(S("d_exp"), 1)
                yield
                yield
                act.wait_ge(S("d_T1"), gi + 1)
                A(Tm[:, :, :], AX[2][:, :].rearrange("p (a c) -> p a c", c=C), ACT.Copy).then_inc(S("d_T"), 1)
                yield
                for l in range(1, LEVELS):
                    yield
                    if l < LEVELS - 1:
                        act.wait_ge(S("d_TU"), gi * (LEVELS - 1) + l)
                        A(Tm[:, :, :], AX[2][:, :].rearrange("p (a c) -> p a c", c=C), ACT.Copy).then_inc(S("d_T"), 1)
                    yield
                act.wait_ge(S("d_u"), gi + 1)
                A(tmp[:, 0, :], AX[2][:, :], ACT.Copy).then_inc(S("d_u_out0"), 1)
                yield
                act.wait_ge(S("d_w"), gi + 1)
                A(wT[:, 0, :, :, :], AX[2][:, :].rearrange("p (t h c) -> p t h c", t=TB, h=HG), ACT.Copy).then_inc(S("d_w_out0"), 1)
                yield
                for n in range(4):
                    tb, a = n // 2, n % 2
                    rows_ = slice(a * C, (a + 1) * C)
                    if n:
                        yield
                    act.wait_ge(S("d_S_used"), gi * 4 + n + 1)
                    A(o_rows[rows_, tb, :], AX[3][rows_, :], ACT.Copy).then_inc(S("d_o_out"), 1)
                    yield
                sums_of_squares(o_rows, sso, kbe, "d_o_sums")
                act.wait_ge(S("d_o_mean"), gi + 1)
                A(sso[:, :, :], sso[:, :, :], ACT.Sqrt).then_inc(S("d_o_root"), 1)
                yield
                yield
                yield
                act.wait_ge(S("d_y_turned"), gi + 1)
                for b in range(2):
                    i = A(zT_hi[:, bass.ds(gi * HG + 2 * b, 2), :], AX[2 + b][:, :].rearrange("p (a t) -> p a t", a=2), ACT.Copy,
                          scale=onw[:, 0:1])
                i.then_inc(S("z_hi"), 1)
                yield

            def read_rows(t, part, n, parts_):
                tile_done(act, pl, t)
                if part == 3:
                    for tb in range(TB):
                        A(zs[:, tb, :], G[t % 2][tb][:, :], ACT.Silu).then_inc(S(f"read_out{tb}"), 1)
                else:
                    A(parts_[part][:, 0, :], G[t % 2][0][:, :], ACT.Copy).then_inc(S("read_out0"), 1)

            def stack(t0, side, group, bufs):
                none = iter(())
                s = none
                for part in range(4):
                    run(half, 8, s)
                    finish(s)
                    read_rows(t0 + part, part, part, bufs)
                    s = side(0, part) if part < 3 else none
                with act.Fori(0, 3) as i:
                    pl.enter(i, t0 + 4, 4)
                    g = group(i)
                    for part in range(4):
                        run(half, 8, s, g)
                        finish(s)
                        if part == 3:
                            finish(g)
                        read_rows(t0 + 4 + part, part, 3 + part, bufs)
                        s = side(i + 1, part) if part < 3 else none
                    pl.leave(3)
                finish(group(3))
                run(half, 32)

            if parts >= 3:
                act.wait_ge(S("x_ready"), 3)
                for j in range(4):
                    act.dma_start(crows[0:3 * H, j, :], ins["a_conv_w_2"][0, j].rearrange("(k p) -> k p", p=P)).then_inc(S("crows_landed"), 16)
                act.dma_start(crows[0:1, 4, :], ins["a_out_norm_w_2"]).then_inc(S("crows_landed"), 16)
                act.dma_start(alog[:, :], ins["a_a_log_2"][0].partition_broadcast(P)).then_inc(S("ab_landed"), 16)
                act.dma_start(dtb[:, :], ins["a_dt_bias_2"][0].partition_broadcast(P)).then_inc(S("ab_landed"), 16)
                act.dma_start(wab[:, :, :], W["a_in"][:, 4 * D:].rearrange("(k p) n -> p k n", p=P)).then_inc(S("wab_landed"), 16)
                norm_sums(3)
                norm_turned(3, 2)
                act.wait_ge(S("ab_landed"), 32)
                A(alog[:, :], alog[:, :], ACT.Exp)
                act.wait_ge(S("ab_sum"), 1)
                A(beta[:, :, :], gx[:, :, :], ACT.Abs)
                act.drain()
                A(beta[:, :, :], beta[:, :, :], ACT.Exp, scale=-1.0).then_inc(S("ab_exp"), 1)
                act.wait_ge(S("ab_one"), 1)
                A(beta[:, :, :], beta[:, :, :], ACT.Ln).then_inc(S("ab_ln"), 1)
                act.wait_ge(S("ab_g"), 1)
                A(beta[:, :, :], AX[0][:, 0:TB * 2 * H].rearrange("p (t c) -> p t c", t=TB)[:, :, H:], ACT.Sigmoid).then_inc(S("ab_beta"), 1)
                act.wait_ge(S("gc_done"), 1)
                A(egc[:, :, :], AX[2][:, 0:TB * H].rearrange("p (t h) -> p t h", t=TB), ACT.Exp)
                act.wait_ge(S("g_rest"), 1)
                A(edec[:, :, :], edec[:, :, :], ACT.Exp)
                for a in range(2):
                    e = A(egl[:, a, :, :], AX[a][:, P:P + TB * H].rearrange("p (t h) -> p t h", t=TB), ACT.Exp)
                e.then_inc(S("decays"), 1)
                stack(T_A, conv_side, delta, (tok, tok, tok))

            def rows_side(gi, part):
                n = gi * 2 + part
                if part == 2:
                    return
                sums_of_squares(tok, bss, bsq, "b_sums", ("read_out1", gi * 4 + (T_B + part + 1)))
                yield
                act.wait_ge(S("b_mean"), n + 1)
                A(bss[:, :, :], bss[:, :, :], ACT.Sqrt).then_inc(S("b_root"), 1)
                yield
                yield
                yield
                act.wait_ge(S("b_turned"), n + 1)
                for e in range(2):
                    i = A((bqT, bkT)[part][:, e, :], AX[0][:, e * T:(e + 1) * T], ACT.Copy, scale=bw[:, part:part + 1])
                i.then_inc(S("b_out0"), 1)
                yield

            def band(gi):
                for pr in range(2):
                    n = gi * 2 + pr
                    yield
                    for a in range(2):
                        act.wait_ge(S("b_max"), n * 2 + a + 1)
                        for tb in range(TB):
                            e = A(bsc[:, a, tb, :], bsc[:, a, tb, :], ACT.Exp, bias=bmx[:, a, tb:tb + 1], accum_out=bsm[:, a, tb:tb + 1])
                        e.then_inc(S("b_exp"), 1)
                    yield
                    act.wait_ge(S("b_p_turned"), n * 2 + 1)
                    A(bpT[:, 0, :, :], AX[2][:, :].rearrange("p (k t) -> p k t", k=TB), ACT.Copy).then_inc(S("b_pT0"), 1)
                    yield
                yield
                act.wait_ge(S("b_y_turned"), gi + 1)
                for b in range(2):
                    e = A(zT_hi[:, bass.ds(gi * HG + 2 * b, 2), :], AX[2 + b][:, :].rearrange("p (a t) -> p a t", a=2), ACT.Copy)
                e.then_inc(S("z_hi"), 1)
                yield

            if parts >= 4:
                act.wait_ge(S("x_ready"), 4)
                act.dma_start(bw_rows[0:1, :], ins["b_q_norm_w_2"]).then_inc(S("bw_landed"), 16)
                act.dma_start(bw_rows[1:2, :], ins["b_k_norm_w_2"]).then_inc(S("bw_landed"), 16)
                act.wait_ge(S("band_cut"), 1)
                act.wait_ge(S("band_copied"), 16)
                for a, w in enumerate((P + C, 2 * P)):
                    src = bass.AP(tensor=band_skew.tensor, offset=P - a * C, ap=[[BAND - 1, C], [C * BAND, H], [1, w]])
                    act.dma_start(bbias[a * C:(a + 1) * C, :, 0:w], src).then_inc(S("band_landed"), 16)
                norm_sums(4)
                norm_turned(4, 3)
                stack(T_B, rows_side, band, (tok, tok, bva))

        @block.vector
        def _(dve):
            pl = Place()
            half = lambda: dve_half(dve, pl)
            V = nc.vector

            def norm_sums(c):
                dve.wait_ge(S("sumsq"), c + 1)
                V.tensor_scalar(stat[:, 2:4], stat[:, 0:2], 1.0 / D, RMS_EPS, ALU.mult, ALU.add).then_inc(S("meansq"), 1)
                dve.wait_ge(S("rms"), c + 1)
                V.reciprocal(stat[:, 6:8], stat[:, 4:6]).then_inc(S("rstd"), 1)
                dve.drain()

            def norm_turned(c, j):
                norm_sums(c)
                if c == 0:
                    dve.wait_ge(S("x_loaded"), 32)
                V.tensor_scalar(xs[:, 1, :], x[:, 1, :], stat[:, 7:8], None, ALU.mult).then_inc(S("xs1"), 1)
                for b in range(KD // 2):
                    dve.wait_ge(S("hT_hi_done"), 8 * j + b + 1)
                    for e in range(2):
                        kt = 2 * b + e
                        i = V.scalar_tensor_tensor(out=hT_lo[:, kt, :], in0=AX[b % 4][:, e * T:(e + 1) * T],
                                                   scalar=gains[:, j * KD + kt:j * KD + kt + 1],
                                                   in1=hT_hi[:, kt, :].bitcast(F32), op0=ALU.mult, op1=ALU.subtract)
                    i.then_inc(S("hT_lo_done"), 1)

            def lo_parts(dst, hi, k0, banks, event, n, done):
                dve.wait_ge(S(event), n)
                for i, b in enumerate(banks):
                    at = bass.ds(k0 + 2 * i, 2)
                    e = V.tensor_tensor(dst[:, at, :], AX[b][:, :].rearrange("p (a t) -> p a t", a=2),
                                        hi[:, at, :].bitcast(F32), ALU.subtract)
                e.then_inc(S(done), 1)

            dve.wait_ge(S("rows_turned"), 1)
            V.tensor_copy(gains[:, :], AX[0][:, 0:4 * KD])
            V.tensor_copy(bsT[:, :], AX[0][:, P:P + GMG])
            dve.wait_ge(S("rows_turned"), 2)
            V.tensor_copy(taps[:, :, :], AX[1][:, :].rearrange("p (a b) -> p a b", a=4)[:, :, 0:2 * FB]).then_inc(S("taps_out"), 1)
            for b in range(2):
                dve.wait_ge(S("ws_turned"), b + 1)
                V.tensor_copy(wsT[:, 4 * b:4 * b + 4, :], AX[2 + b][:, :].rearrange("p (a b) -> p a b", a=4)).then_inc(S("wsT_out"), 1)
            half(), half()
            norm_turned(0, 0)

            def mixing():
                for tb in range(TB):
                    if tb == 0:
                        dve.wait_ge(S("read_out1"), 2)
                    for c in range(2):
                        V.bn_stats(bn[:, tb, c, :], vg[:, tb, c * 512:(c + 1) * 512])
                    dve.drain()
                    e = V.bn_aggr(mv[:, tb, :], bn[:, tb, :, :])
                dve.drain()
                V.tensor_scalar(mv[:, :, 1], mv[:, :, 1], LN_EPS, None, ALU.add).then_inc(S("ln_var"), 1)
                yield
                dve.wait_ge(S("ln_sd"), 1)
                V.reciprocal(lnr[:, :], lnr[:, :])
                dve.drain()
                dve.wait_ge(S("ln_landed"), 32)
                for tb in range(TB):
                    V.tensor_scalar(vg[:, tb, :], vg[:, tb, :], mv[:, tb, 0:1], lnr[:, tb:tb + 1], ALU.subtract, ALU.mult)
                    dve.drain()
                    yield
                    V.tensor_tensor(vg[:, tb, :], vg[:, tb, :], lng[:, :], ALU.mult)
                    dve.drain()
                    yield
                    V.tensor_tensor(vg[:, tb, :], vg[:, tb, :], lnb[:, :], ALU.add).then_inc(S("v_normed"), 1)
                    yield
                for _ in range(9):
                    yield
                dve.wait_ge(S("read_out1"), 4)
                for j in range(4):
                    tb, g0 = j // 2, (j % 2) * 4
                    dve.wait_ge(S("mixed"), j + 1)
                    for g in range(4):
                        c = slice((g0 + g) * P, (g0 + g + 1) * P)
                        e = V.scalar_tensor_tensor(out=ug[:, tb, c], in0=AX[2 + j % 2][:, g * P:(g + 1) * P],
                                                   scalar=bsT[:, g0 + g:g0 + g + 1], in1=ug[:, tb, c],
                                                   op0=ALU.add, op1=ALU.mult)
                    e.then_inc(S("ya_done"), 1)
                    yield
                    yield
                for b in range(4):
                    yield
                    lo_parts(yT_lo, yT_hi, 2 * b, (2 + b % 2,), "ya_hi", b + 1, "ya_lo")

            def attend(g):
                for pr in range(4):
                    u = 4 * g + pr
                    dve.wait_ge(S("bias_masked"), 2 * u + 2)
                    for a in range(2):
                        dve.wait_ge(S("na_scores"), 2 * u + a + 1)
                        b0 = bias[:, u % BR, a, 2, 0:1]
                        window = bass.AP(tensor=b0.tensor, offset=b0.offset,
                                         ap=[list(b0.ap[0]), [-2 * GRID, TB], [1, T]])
                        V.scalar_tensor_tensor(out=sc[:, a, :, :], in0=AX[2 + a][:, :].rearrange("p (t k) -> p t k", t=TB),
                                               scalar=float(NAD) ** -0.5, in1=window, op0=ALU.mult, op1=ALU.add)
                        dve.drain()
                        V.tensor_reduce(mx[:, a, :], sc[:, a, :, :], AX_X, ALU.max)
                        dve.drain()
                        V.tensor_scalar(mx[:, a, :], mx[:, a, :], -1.0, None, ALU.mult).then_inc(S("na_max"), 1)
                    yield
                    dve.wait_ge(S("na_exp"), 2 * u + 2)
                    V.reciprocal(ri[:, :, :], sm[:, :, :])
                    yield
                    dve.wait_ge(S("na_p_turned"), 2 * u + 2)
                    V.tensor_copy(pT[:, 1, :, :], AX[3][:, :].rearrange("p (k t) -> p k t", k=TB)).then_inc(S("na_pT1"), 1)
                    dve.wait_ge(S("na_pv"), u + 1)
                    for a in range(2):
                        h = 2 * pr + a
                        e = V.tensor_tensor(yb[:, :, h * NAD:(h + 1) * NAD],
                                            AX[2 + a][:, 0:2 * NAD].rearrange("p (t d) -> p t d", t=TB),
                                            each(ri[:, a, :], NAD), ALU.mult)
                    e.then_inc(S("na_out"), 1)
                    yield
                yield
                yield
                lo_parts(yT_lo, yT_hi, 8 + 4 * g, (2, 3), "yb_hi", g + 1, "yb_lo")

            def qkv_side(g, part):
                for _ in range(6):
                    yield
                dve.wait_ge(S("qk_turned"), 2 * g + part + 1)
                V.tensor_copy((qT, kT)[part][:, 2:4, :], AX[1][:, :].rearrange("p (a t) -> p a t", a=2)).then_inc(S("qk_out1"), 1)
                yield
                yield

            mix = mixing()
            none = iter(())
            for t in range(4):
                run(half, 8, mix if t >= 2 else none)
            side = none
            att = none
            for g in range(2):
                for part in range(3):
                    t = 4 + 3 * g + part
                    run(half, 8, mix, side, att)
                    finish(side)
                    tile_done(dve, pl, t)
                    if t > 4 and part < 2:
                        dve.wait_ge(S("qk_turned"), 2 * g + part)
                    if part == 2 and g:
                        dve.wait_ge(S("na_pv"), 4)
                    V.tensor_copy((va if part == 2 else qkv_tok)[:, 1, :], G[t % 2][1][:, :]).then_inc(S("read_out1"), 1)
                    side = qkv_side(g, part) if part < 2 else none
                finish(att)
                att = attend(g)
            for i in range(4):
                run(half, 8, att)
            finish(att)
            for n in range(4):
                run(half, 8)
                run(half, 4)
                t = T_MERGE + 3 * n + 1
                tile_done(dve, pl, t)
                if n == 0:
                    dve.wait_ge(S("read_out1"), t)
                cols = slice(n * 512, (n + 1) * 512)
                for tb in range(TB):
                    V.tensor_tensor(ga[:, tb, cols], ga[:, tb, cols], G[t % 2][tb][:, :], ALU.mult).then_inc(S(f"read_out{tb}"), 1)
                run(half, 4)
                tile_done(dve, pl, t + 1)
                dve.wait_ge(S("read_out1"), t)
                for tb in range(TB):
                    V.tensor_tensor(sgb[:, tb, :], sgb[:, tb, :], G[(t + 1) % 2][tb][:, :], ALU.mult).then_inc(S(f"read_out{tb}"), 1)
                dve.drain()
                V.tensor_tensor(ga[:, :, cols], ga[:, :, cols], sgb[:, :, :], ALU.add).then_inc(S("merged"), 1)
            for b in range(8):
                lo_parts(hT_lo, hT_hi, 2 * b, (b % 4,), "merged_hi", b + 1, "merged_lo")

            def add_tile(t, at, last=False):
                tile_done(dve, pl, t)
                for tb in range(TB):
                    dst = x[:, tb, bass.ds(at, 512)]
                    V.tensor_tensor(dst, dst, G[t % 2][tb][:, :], ALU.add).then_inc(S(f"read_out{tb}"), 1)

            def output(t0, halves):
                with dve.Fori(0, 2) as i:
                    pl.enter(i, t0, 2)
                    for s in range(2):
                        run(half, halves)
                        add_tile(t0 + s, i * 1024 + s * 512)
                    pl.leave(2)

            def x_is_ready():
                dve.drain()
                V.memset(stat[:, 0:2], 0.0).then_inc(S("x_ready"), 1)
                dve.drain()

            for s in range(4):
                run(half, 8)
                add_tile(T_OUT + s, s * 512)
            x_is_ready()
            norm_turned(1, 1)

            def up_side(j, kt, n, width=2):
                w = width
                yield
                for b, (dst, blk) in enumerate(((cg, j * 2), (cv, j * 2 + FB))):
                    dve.wait_ge(S("conv_mid"), n * 2 + b + 1)
                    for e in range(w):
                        for tap, o, i_ in ((0, slice(1, T), slice(0, T - 1)), (2, slice(0, T - 1), slice(1, T))):
                            src = AX[b][:, e * T:(e + 1) * T]
                            i = V.scalar_tensor_tensor(out=dst[:, e, o], in0=src[:, i_], scalar=taps[:, tap, bass.ds(blk + e, 1)],
                                                       in1=dst[:, e, o], op0=ALU.mult, op1=ALU.add)
                            dve.drain() if tap == 0 else None
                    i.then_inc(S("conv_gate_done" if b == 0 else "conv_val_done"), 1)
                yield
                dve.drain()
                dve.wait_ge(S("silu_done"), n + 1)
                V.tensor_tensor(cv[:, 0:w, :], cg[:, 0:w, :], cv[:, 0:w, :], ALU.mult).then_inc(S("gated"), 1)
                yield
                dve.wait_ge(S("act_hi"), n + 1)
                at = bass.ds(kt, w)
                V.tensor_tensor(yT_lo[:, at, :], cv[:, 0:w, :], yT_hi[:, at, :].bitcast(F32), ALU.subtract).then_inc(S("act_lo"), 1)
                yield

            def up_read(t, n):
                tile_done(dve, pl, t)
                w = HALVES[TILE_END[t] - 1]["width"]
                dve.wait_ge(S("up_turned"), n * 2)
                V.tensor_copy(ut[:, 1, 0:w], G[t % 2][1][:, 0:w]).then_inc(S("read_out1"), 1)

            def feed_forward(t0, j0, tiles, loads, t_down, half_tile):
                pairs = (tiles - 2) // 2
                run(half, 8)
                tile_done(dve, pl, t0)
                if j0:
                    dve.wait_ge(S("up_turned"), 2 * j0)
                V.tensor_copy(ut[:, 1, :], G[t0 % 2][1][:, :]).then_inc(S("read_out1"), 1)
                with dve.Fori(0, pairs) as i:
                    pl.enter(i, t0 + 1, 2)
                    for s in range(2):
                        run(half, 8, up_side(i * 2 + (j0 + s), i * 4 + 2 * s, i * 2 + (j0 + s)))
                        up_read(t0 + 1 + s, i * 2 + (j0 + s + 1))
                    pl.leave(pairs)
                s = 2 * pairs
                while s < tiles - 1:
                    run(half, 8, up_side(j0 + s, 2 * s, j0 + s))
                    up_read(t0 + 1 + s, j0 + s + 1)
                    s += 1
                run(half, 2 * len(loads), up_side(j0 + s, 2 * s, j0 + s, 1 if half_tile else 2))
                add_tile(t_down, 0)
                for s in range(1, 4):
                    run(half, 2 * len(loads))
                    add_tile(t_down + s, s * 512)

            if parts >= 2:
                feed_forward(T_UP1, 0, UP1, DOWN1, T_DOWN1, 0)
                feed_forward(T_UP2, UP1, UP2, DOWN2, T_DOWN2, 1)
                x_is_ready()
                norm_sums(2)
                dve.wait_ge(S("nf_landed"), 16)
                for tb in range(TB):
                    V.scalar_tensor_tensor(out=x[:, tb, :], in0=x[:, tb, :], scalar=stat[:, 6 + tb:7 + tb], in1=nf[:, :],
                                           op0=ALU.mult, op1=ALU.mult)
                x_is_ready()

            def scaled(dst, src, f):
                return V.tensor_tensor(dst[:, :, :].rearrange("p t (h d) -> p t h d", h=HG),
                                       src[:, :, :].rearrange("p t (h d) -> p t h d", h=HG), each(f, HD), ALU.mult)

            def conv_side(gi, part):
                n = gi * 3 + part
                yield
                for b in range(2):
                    dve.wait_ge(S("c_mid"), n * 2 + b + 1)
                    for e in range(2):
                        for tap in range(3):
                            back = 3 - tap
                            src = AX[b][:, e * T:(e + 1) * T]
                            i = V.scalar_tensor_tensor(out=xc[:, 2 * b + e, back:], in0=src[:, 0:T - back],
                                                       scalar=ctap[:, tap, bass.ds(gi * HG + (part * H + 2 * b + e), 1)],
                                                       in1=xc[:, 2 * b + e, back:], op0=ALU.mult, op1=ALU.add)
                            if tap < 2:
                                dve.drain()
                    if b == 0:
                        yield
                i.then_inc(S("c_conv"), 1)
                yield
                yield
                yield
                dve.wait_ge(S("c_back"), n + 1)
                if part == 2:
                    dst, event = vs, "d_v_rows"
                else:
                    dst, event = (qs, ks)[part], "c_rows1"
                V.tensor_copy(dst[:, 1, :], AX[1][:, :]).then_inc(S(event), 1)
                yield
                yield
                yield

            def delta(gi):
                hs = bass.ds(gi * HG, HG)
                dve.wait_ge(S("d_sums"), gi * 2 + 2)
                V.tensor_scalar(ssum[:, :, :, :], ssum[:, :, :, :], RMS_EPS, None, ALU.add).then_inc(S("d_eps"), 1)
                dve.wait_ge(S("d_root"), gi + 1)
                V.reciprocal(ssum[:, :, :, :], ssum[:, :, :, :])
                dve.drain()
                rq, rk = ssum[:, 0, :, :], ssum[:, 1, :, :]
                dve.wait_ge(S("decays"), 1)
                V.tensor_scalar(fac[:, 0, :, :], rq, float(HD) ** -0.5, None, ALU.mult)
                V.tensor_tensor(fac[:, 2, :, :], rk, beta[:, :, hs], ALU.mult)
                V.tensor_tensor(fac[:, 4, :, :], rk, edec[:, :, hs], ALU.mult)
                V.tensor_copy(fac[:, 5, :, :], beta[:, :, hs])
                dve.drain()
                V.tensor_tensor(fac[:, 1, :, :], fac[:, 0, :, :], egc[:, :, hs], ALU.mult)
                V.tensor_tensor(fac[:, 3, :, :], fac[:, 2, :, :], egc[:, :, hs], ALU.mult)
                dve.drain()
                V.memset(stat[:, 0:1], 0.0).then_inc(S("d_factors"), 1)
                yield
                dve.wait_ge(S("c_rows0"), gi * 2 + 2)
                scaled(tmp, ks, fac[:, 2, :, :]).then_inc(S("d_rows"), 1)
                yield
                for j, (dst, nxt) in enumerate(((kbT, "kn"), (knT, "qd"), (qdT, "qn"), (qnT, None))):
                    dve.wait_ge(S("d_turned"), gi * 4 + j + 1)
                    V.tensor_copy(dst[:, 2:4, :], AX[3][:, :].rearrange("p (a t) -> p a t", a=2)).then_inc(S("d_out1"), 1)
                    if nxt == "kn":
                        dve.wait_ge(S("d_kdec"), gi + 1)
                        scaled(ks, ks, rk).then_inc(S("d_rows"), 1)
                    elif nxt == "qd":
                        scaled(tmp, qs, fac[:, 1, :, :]).then_inc(S("d_rows"), 1)
                    elif nxt == "qn":
                        scaled(qs, qs, fac[:, 0, :, :]).then_inc(S("d_rows"), 1)
                    else:
                        dve.wait_ge(S("chunk_masks"), 1)
                        for tb in range(TB):
                            e = V.tensor_tensor(W1[:, tb * HG:(tb + 1) * HG, :], rep(m_le[:, :], HG), each(gg[:, tb, hs], C), ALU.mult)
                        e.then_inc(S("d_gm"), 1)
                    yield
                dve.wait_ge(S("d_exp"), gi + 1)
                V.tensor_tensor(dec[:, :, :], dec[:, :, :], rep(m_le[:, :], TB * HG), ALU.mult)
                dve.drain()
                yield
                dve.wait_ge(S("d_gram"), gi + 1)
                V.tensor_tensor(AT[:, :, :], AX[2][:, :].rearrange("p (a c) -> p a c", c=C), dec[:, :, :], ALU.mult)
                V.tensor_tensor(qk[:, :, :], AX[3][:, :].rearrange("p (a c) -> p a c", c=C), dec[:, :, :], ALU.mult)
                dve.drain()
                V.tensor_tensor(Um[:, :, :], AT[:, :, :], rep(m_lev[:, 0, :], TB * HG), ALU.mult)
                dve.drain()
                V.scalar_tensor_tensor(out=Um[:, :, :], in0=Um[:, :, :], scalar=-1.0, in1=rep(idc[:, :], TB * HG),
                                       op0=ALU.mult, op1=ALU.add).then_inc(S("d_U1"), 1)
                yield
                yield
                for l in range(1, LEVELS):
                    n = gi * (LEVELS - 1) + l
                    dve.wait_ge(S("d_Z"), n)
                    V.scalar_tensor_tensor(out=W1[:, :, :], in0=AX[2][:, :].rearrange("p (a c) -> p a c", c=C), scalar=-1.0,
                                           in1=rep(idc[:, :], TB * HG), op0=ALU.mult, op1=ALU.add).then_inc(S("d_W1"), 1)
                    yield
                    dve.wait_ge(S("d_TU"), n)
                    V.tensor_copy(Um[:, :, :], AX[3][:, :].rearrange("p (a c) -> p a c", c=C)).then_inc(S("d_U"), 1)
                    yield
                dve.wait_ge(S("d_u"), gi + 1)
                V.tensor_copy(tmp[:, 1, :], AX[3][:, :]).then_inc(S("d_u_out1"), 1)
                yield
                dve.wait_ge(S("d_w"), gi + 1)
                V.tensor_copy(wT[:, 1, :, :, :], AX[3][:, :].rearrange("p (t h c) -> p t h c", t=TB, h=HG)).then_inc(S("d_w_out1"), 1)
                yield
                for n in range(4):
                    tb, a = n // 2, n % 2
                    rows_ = slice(a * C, (a + 1) * C)
                    if n:
                        dve.wait_ge(S("d_wS"), gi * 3 + n)
                        V.tensor_tensor(tmp[rows_, tb, :], tmp[rows_, tb, :], AX[2][rows_, :], ALU.subtract).then_inc(S("d_vnew"), 1)
                        yield
                    dve.wait_ge(S("d_S_used"), gi * 4 + n + 1)
                    if n == 0:
                        e = V.tensor_copy(St[:, :], AX[2][:, :])
                    elif n < 3:
                        for h in range(HG):
                            c = slice(h * HD, (h + 1) * HD)
                            e = V.scalar_tensor_tensor(out=St[:, c], in0=St[:, c], scalar=egl[:, a, tb, bass.ds(gi * HG + h, 1)],
                                                       in1=AX[2][:, c], op0=ALU.mult, op1=ALU.add)
                    if n < 3:
                        e.then_inc(S("d_state"), 1)
                    yield
                dve.wait_ge(S("d_o_sums"), gi + 1)
                V.tensor_scalar(sso[:, :, :], sso[:, :, :], 1.0 / HD, RMS_EPS, ALU.mult, ALU.add).then_inc(S("d_o_mean"), 1)
                yield
                dve.wait_ge(S("d_o_root"), gi + 1)
                V.reciprocal(sso[:, :, :], sso[:, :, :])
                dve.drain()
                dve.wait_ge(S("read_out1"), gi * 4 + T_A + 4)
                for tb in range(TB):
                    for h in range(HG):
                        c = slice(h * HD, (h + 1) * HD)
                        e = V.scalar_tensor_tensor(out=o_rows[:, tb, c], in0=o_rows[:, tb, c], scalar=sso[:, tb, h:h + 1],
                                                   in1=zs[:, tb, c], op0=ALU.mult, op1=ALU.mult)
                e.then_inc(S("d_y"), 1)
                yield
                yield
                dve.wait_ge(S("z_hi"), gi + 1)
                for b in range(2):
                    at = bass.ds(gi * HG + 2 * b, 2)
                    e = V.scalar_tensor_tensor(out=zT_lo[:, at, :], in0=AX[2 + b][:, :].rearrange("p (a t) -> p a t", a=2),
                                               scalar=onw[:, 0:1], in1=zT_hi[:, at, :].bitcast(F32), op0=ALU.mult, op1=ALU.subtract)
                e.then_inc(S("z_lo"), 1)
                yield

            def read_rows(t, part, bufs):
                if part < 3:
                    tile_done(dve, pl, t)
                    V.tensor_copy(bufs[part][:, 1, :], G[t % 2][1][:, :]).then_inc(S("read_out1"), 1)

            def stack(t0, side, group, bufs):
                none = iter(())
                s = none
                for part in range(4):
                    run(half, 8, s)
                    finish(s)
                    read_rows(t0 + part, part, bufs)
                    s = side(0, part) if part < 3 else none
                with dve.Fori(0, 3) as i:
                    pl.enter(i, t0 + 4, 4)
                    g = group(i)
                    for part in range(4):
                        run(half, 8, s, g)
                        finish(s)
                        if part == 3:
                            finish(g)
                        read_rows(t0 + 4 + part, part, bufs)
                        s = side(i + 1, part) if part < 3 else none
                    pl.leave(3)
                finish(group(3))
                for s in range(4):
                    run(half, 8)
                    add_tile(t0 + 16 + s, s * 512)
                x_is_ready()

            if parts >= 3:
                dve.wait_ge(S("crows_turned"), 1)
                V.tensor_copy(ctap[:, :, :], AX[0][:, :].rearrange("p (a b) -> p a b", a=4)[:, :, 0:3 * H])
                V.tensor_copy(onw[:, 0:1], AX[1][:, 0:1]).then_inc(S("ctap_out"), 1)
                norm_turned(3, 2)
                ab = AX[0][:, 0:TB * 2 * H].rearrange("p (t c) -> p t c", t=TB)
                dve.wait_ge(S("ab_done"), 1)
                dve.wait_ge(S("ab_landed"), 32)
                for tb in range(TB):
                    e = V.tensor_tensor(gx[:, tb, :], ab[:, tb, 0:H], dtb[:, :], ALU.add)
                e.then_inc(S("ab_sum"), 1)
                dve.wait_ge(S("ab_exp"), 1)
                V.tensor_scalar(beta[:, :, :], beta[:, :, :], 1.0, None, ALU.add).then_inc(S("ab_one"), 1)
                dve.wait_ge(S("ab_ln"), 1)
                V.tensor_scalar(gx[:, :, :], gx[:, :, :], 0.0, None, ALU.max)
                dve.drain()
                V.tensor_tensor(gx[:, :, :], gx[:, :, :], beta[:, :, :], ALU.add)
                dve.drain()
                for tb in range(TB):
                    e = V.scalar_tensor_tensor(out=gg[:, tb, :], in0=gx[:, tb, :], scalar=-1.0, in1=alog[:, :],
                                               op0=ALU.mult, op1=ALU.mult)
                e.then_inc(S("ab_g"), 1)
                dve.wait_ge(S("gc_done"), 1)
                V.tensor_copy(gx[:, :, :], AX[3][:, 0:TB * H].rearrange("p (t h) -> p t h", t=TB))
                dve.drain()
                V.tensor_tensor(edec[:, :, :], gx[:, :, :], AX[3][:, P:P + TB * H].rearrange("p (t h) -> p t h", t=TB),
                                ALU.subtract).then_inc(S("g_rest"), 1)
                stack(T_A, conv_side, delta, (tok, tok, tok))

            def rows_side(gi, part):
                n = gi * 2 + part
                if part == 2:
                    return
                yield
                dve.wait_ge(S("b_sums"), n + 1)
                V.tensor_scalar(bss[:, :, :], bss[:, :, :], 1.0 / HD, RMS_EPS, ALU.mult, ALU.add).then_inc(S("b_mean"), 1)
                yield
                dve.wait_ge(S("b_root"), n + 1)
                V.reciprocal(bss[:, :, :], bss[:, :, :])
                dve.drain()
                scaled(tok, tok, bss[:, :, :]).then_inc(S("b_normed"), 1)
                yield
                yield
                dve.wait_ge(S("b_turned"), n + 1)
                V.tensor_scalar((bqT, bkT)[part][:, 2:4, :], AX[1][:, :].rearrange("p (a t) -> p a t", a=2), bw[:, part:part + 1],
                                None, ALU.mult).then_inc(S("b_out1"), 1)
                yield

            def band(gi):
                for pr in range(2):
                    n = gi * 2 + pr
                    for a in range(2):
                        dve.wait_ge(S("b_scores"), n * 2 + a + 1)
                        for tb in range(TB):
                            window = bbias[:, bass.ds(gi * HG + (2 * pr + a), 1), P - tb * P:P - tb * P + T]
                            V.scalar_tensor_tensor(out=bsc[:, a, tb, :], in0=AX[2 + a][:, tb * T:(tb + 1) * T],
                                                   scalar=float(HD) ** -0.5, in1=window.rearrange("p a k -> p (a k)"),
                                                   op0=ALU.mult, op1=ALU.add)
                        dve.drain()
                        V.tensor_reduce(bmx[:, a, :], bsc[:, a, :, :], AX_X, ALU.max)
                        dve.drain()
                        V.tensor_scalar(bmx[:, a, :], bmx[:, a, :], -1.0, None, ALU.mult).then_inc(S("b_max"), 1)
                    yield
                    dve.wait_ge(S("b_exp"), n * 2 + 2)
                    V.reciprocal(bri[:, :, :], bsm[:, :, :])
                    yield
                    dve.wait_ge(S("b_p_turned"), n * 2 + 2)
                    V.tensor_copy(bpT[:, 1, :, :], AX[3][:, :].rearrange("p (k t) -> p k t", k=TB)).then_inc(S("b_pT1"), 1)
                    dve.wait_ge(S("b_pv"), n + 1)
                    dve.wait_ge(S("read_out1"), gi * 4 + T_B + 4)
                    for a in range(2):
                        c = slice((2 * pr + a) * HD, (2 * pr + a + 1) * HD)
                        for tb in range(TB):
                            e = V.scalar_tensor_tensor(out=by[:, tb, c], in0=AX[2 + a][:, tb * HD:(tb + 1) * HD],
                                                       scalar=bri[:, a, tb:tb + 1], in1=zs[:, tb, c], op0=ALU.mult, op1=ALU.mult)
                    e.then_inc(S("b_y"), 1)
                    yield
                yield
                dve.wait_ge(S("z_hi"), gi + 5)
                for b in range(2):
                    at = bass.ds(gi * HG + 2 * b, 2)
                    e = V.tensor_tensor(zT_lo[:, at, :], AX[2 + b][:, :].rearrange("p (a t) -> p a t", a=2),
                                        zT_hi[:, at, :].bitcast(F32), ALU.subtract)
                e.then_inc(S("z_lo"), 1)
                yield

            if parts >= 4:
                dve.wait_ge(S("bw_turned"), 1)
                V.tensor_copy(bw[:, :], AX[0][:, 0:2]).then_inc(S("bw_out"), 1)
                norm_turned(4, 3)
                dve.wait_ge(S("band_landed"), 32)
                stack(T_B, rows_side, band, (tok, tok, bva))

        @block.tensor
        def _(pe):
            pl = Place()
            half = lambda: pe_half(pe, pl)
            MM, turn = nc.tensor.matmul, nc.tensor.transpose

            def turn_rows(src, banks, event, at=0):
                for i, b in enumerate(banks):
                    for e in range(2):
                        for tb in range(TB):
                            c = (at + 2 * i + e) * P
                            m = turn(AX[b][:, e * T + tb * P:e * T + (tb + 1) * P], src[:, tb, c:c + P], ident[:, :])
                m.then_inc(S(event), 1)

            def norm_turned(j):
                pe.wait_ge(S("xs0"), j + 1)
                pe.wait_ge(S("xs1"), j + 1)
                for b in range(KD // 2):
                    if b >= 4:
                        pe.wait_ge(S("hT_lo_done"), 8 * j + b - 3)
                    turn_rows(xs, (b % 4,), "hT_turned", 2 * b)
                pe.wait_ge(S("hT_lo_done"), 8 * j + 8)

            pe.wait_ge(S("constants"), 1)
            pe.wait_ge(S("rows_landed"), 16 * 8)
            pe.wait_ge(S("ws_landed"), 32)
            turn(AX[0][:, 0:4 * KD], rows[0:4 * KD, 4, :], ident[0:4 * KD, 0:4 * KD])
            turn(AX[0][:, P:P + GMG], bs_rows[:, :], ident[0:GMG, 0:GMG]).then_inc(S("rows_turned"), 1)
            for j in range(4):
                m = turn(AX[1][:, j * P:j * P + 2 * FB], rows[0:2 * FB, j, :], ident[0:2 * FB, 0:2 * FB])
            m.then_inc(S("rows_turned"), 1)
            for g in range(GMG):
                m = turn(AX[2 + g // 4][:, (g % 4) * P:(g % 4 + 1) * P], ws[:, g, :], ident[:, :])
                if g % 4 == 3:
                    m.then_inc(S("ws_turned"), 1)
            pe.wait_ge(S("taps_out"), 1)
            pe.wait_ge(S("wsT_out"), 2)
            norm_turned(0)

            def mixing():
                for _ in range(16):
                    yield
                pe.wait_ge(S("v_normed"), 2)
                for j in range(4):
                    tb, g0 = j // 2, (j % 2) * 4
                    if j >= 2:
                        pe.wait_ge(S("ya_done"), j - 1)
                    for g in range(4):
                        m = MM(AX[2 + j % 2][:, g * P:(g + 1) * P], wsT[:, g0 + g, :], vg[:, tb, (g0 + g) * P:(g0 + g + 1) * P],
                               start=True, stop=True)
                    m.then_inc(S("mixed"), 1)
                    yield
                    yield
                pe.wait_ge(S("ya_done"), 4)
                for b in range(4):
                    if b >= 2:
                        pe.wait_ge(S("ya_lo"), b - 1)
                    turn_rows(ug, (2 + b % 2,), "ya_turned", 2 * b)
                    yield

            def attend(g):
                for pr in range(4):
                    u = 4 * g + pr
                    pe.wait_ge(S("qk_out0"), 2 * g + 2)
                    pe.wait_ge(S("qk_out1"), 2 * g + 2)
                    pe.wait_ge(S("read_out0"), 7 + 3 * g)
                    pe.wait_ge(S("read_out1"), 7 + 3 * g)
                    if pr:
                        pe.wait_ge(S("na_out"), u)
                    elif g:
                        pe.wait_ge(S("yb_lo"), g)
                    else:
                        pe.wait_ge(S("ya_lo"), 4)
                    for a in range(2):
                        rows_ = slice(a * NAD, (a + 1) * NAD)
                        for tb in range(TB):
                            m = MM(AX[2 + a][:, tb * T:(tb + 1) * T], qT[rows_, pr, tb * P:(tb + 1) * P], kT[rows_, pr, :],
                                   start=True, stop=True)
                        m.then_inc(S("na_scores"), 1)
                    yield
                    for a in range(2):
                        pe.wait_ge(S("na_exp"), 2 * u + a + 1)
                        for kb in range(TB):
                            for tb in range(TB):
                                m = turn(AX[2 + a][:, kb * T + tb * P:kb * T + (tb + 1) * P],
                                         sc[:, a, tb, kb * P:(kb + 1) * P], ident[:, :])
                        m.then_inc(S("na_p_turned"), 1)
                    yield
                    pe.wait_ge(S("na_pT0"), u + 1)
                    pe.wait_ge(S("na_pT1"), u + 1)
                    for a in range(2):
                        h = 2 * pr + a
                        for tb in range(TB):
                            for kb in range(TB):
                                m = MM(AX[2 + a][:, tb * NAD:(tb + 1) * NAD], pT[:, a, kb, tb * P:(tb + 1) * P],
                                       va[:, kb, h * NAD:(h + 1) * NAD], start=kb == 0, stop=kb == TB - 1)
                    m.then_inc(S("na_pv"), 1)
                    yield
                pe.wait_ge(S("na_out"), 4 * g + 4)
                turn_rows(yb, (2, 3), "yb_turned")
                yield
                yield
                yield

            def qkv_side(g, part):
                for _ in range(5):
                    yield
                t = 4 + 3 * g + part
                pe.wait_ge(S("read_out0"), t + 1)
                pe.wait_ge(S("read_out1"), t + 1)
                if t > 4:
                    pe.wait_ge(S("qk_out0"), 2 * g + part)
                    pe.wait_ge(S("qk_out1"), 2 * g + part)
                turn_rows(qkv_tok, (0, 1), "qk_turned")
                yield
                yield
                yield

            mix = mixing()
            none = iter(())
            for t in range(4):
                run(half, 8, mix if t >= 2 else none)
            side = none
            att = none
            for g in range(2):
                for part in range(3):
                    run(half, 8, mix, side, att)
                    finish(side)
                    side = qkv_side(g, part) if part < 2 else none
                finish(att)
                att = attend(g)
            for i in range(4):
                run(half, 8, att)
            finish(att)
            pe.wait_ge(S("yb_lo"), 2)
            for n in range(4):
                run(half, 16)
            for b in range(8):
                pe.wait_ge(S("merged"), 4)
                if b >= 4:
                    pe.wait_ge(S("merged_lo"), b - 3)
                turn_rows(ga, (b % 4,), "merged_turned", 2 * b)
            pe.wait_ge(S("merged_lo"), 8)
            run(half, 32)
            norm_turned(1)

            def up_side(t, n, width=2):
                pe.wait_ge(S("read_out0"), t)
                pe.wait_ge(S("read_out1"), t)
                for b in range(2):
                    for e in range(width):
                        for tb in range(TB):
                            c = (b * width + e) * P
                            m = turn(AX[b][:, e * T + tb * P:e * T + (tb + 1) * P], ut[:, tb, c:c + P], ident[:, :])
                    m.then_inc(S("up_turned"), 1)
                yield

            def feed_forward(t0, j0, tiles, loads, t_down, half_tile):
                pairs = (tiles - 2) // 2
                run(half, 8)
                with pe.Fori(0, pairs) as i:
                    pl.enter(i, t0 + 1, 2)
                    for s in range(2):
                        run(half, 8, up_side(i * 2 + (t0 + s + 1), i * 2 + (j0 + s)))
                    pl.leave(pairs)
                s = 2 * pairs
                while s < tiles - 1:
                    run(half, 8, up_side(t0 + s + 1, j0 + s))
                    s += 1
                run(half, 2 * len(loads) - 4, up_side(t0 + s + 1, j0 + s, 1 if half_tile else 2))
                pe.wait_ge(S("act_lo"), j0 + tiles)
                run(half, 6 * len(loads) + 4)

            if parts >= 2:
                feed_forward(T_UP1, 0, UP1, DOWN1, T_DOWN1, 0)
                feed_forward(T_UP2, UP1, UP2, DOWN2, T_DOWN2, 1)

            def chunks():
                for tb in range(TB):
                    for a in range(2):
                        for h in range(HG):
                            yield tb, a, h, slice(a * C, (a + 1) * C), tb * HG + h

            def conv_side(gi, part):
                n = gi * 3 + part
                t = gi * 4 + (T_A + part + 1)
                pe.wait_ge(S("read_out0"), t)
                pe.wait_ge(S("read_out1"), t)
                if not isinstance(gi, int) or gi or part:
                    for event in (("d_v_rows", ) if part == 0 else ("c_rows0", "c_rows1")):
                        pe.wait_ge(S(event), gi * 2 + (0 if part == 0 else part))
                for i in range(2):
                    turn_rows(tok, (i,), "c_turned", 2 * i)
                yield
                yield
                yield
                yield
                pe.wait_ge(S("c_silu"), n + 1)
                for tb in range(TB):
                    for h in range(HG):
                        m = turn(AX[tb][:, h * P:(h + 1) * P], xc[:, h, tb * P:(tb + 1) * P], ident[:, :])
                m.then_inc(S("c_back"), 1)
                yield
                yield
                yield
                yield

            def held(n):
                return n if isinstance(n, int) else pe.to_reg(n)

            def delta(gi):
                L = LEVELS - 1
                yield
                for j, src in enumerate((tmp, ks, tmp, qs)):
                    pe.wait_ge(S("d_rows"), gi * 4 + j + 1)
                    if j:
                        pe.wait_ge(S("d_out0"), gi * 4 + j)
                        pe.wait_ge(S("d_out1"), gi * 4 + j)
                    turn_rows(src, (2, 3), "d_turned")
                    yield
                turned, now = held(gi * 4 + 4), held(gi + 1)
                pe.wait_ge(S("chunk_masks"), 1)
                pe.wait_ge(S("d_gm"), now)
                pe.wait_ge(S("d_out0"), turned)
                for a in range(2):
                    rows_ = slice(a * C, (a + 1) * C)
                    m = MM(AX[2][rows_, :], m_gt[rows_, :], W1[rows_, :, :].rearrange("p a c -> p (a c)"), start=True, stop=True)
                m.then_inc(S("d_arg"), 1)
                yield
                pe.wait_ge(S("d_exp"), gi + 1)
                pe.wait_ge(S("d_out1"), gi * 4 + 4)
                for dst, rhs in ((AX[2], kbT), (AX[3], qnT)):
                    for tb, a, h, rows_, c in chunks():
                        cols = slice(tb * P + a * C, tb * P + (a + 1) * C)
                        m = MM(dst[rows_, c * C:(c + 1) * C], knT[:, h, cols], rhs[:, h, cols], start=True, stop=True)
                m.then_inc(S("d_gram"), 1)
                yield
                yield
                pe.wait_ge(S("chunk_masks"), 1)
                pe.wait_ge(S("d_U1"), gi + 1)
                for tb, a, h, rows_, c in chunks():
                    m = MM(AX[2][rows_, c * C:(c + 1) * C], Um[rows_, c, :], idc[rows_, :], start=True, stop=True)
                m.then_inc(S("d_T1"), 1)
                yield
                for l in range(1, LEVELS):
                    n, before = held(gi * L + l), held(gi * L + l - 1)
                    pe.wait_ge(S("chunk_masks"), 1)
                    pe.wait_ge(S("d_level"), n)
                    pe.wait_ge(S("d_T"), n)
                    for tb, a, h, rows_, c in chunks():
                        m = MM(AX[2][rows_, c * C:(c + 1) * C], ATl[rows_, c, :], Tm[rows_, c, :], start=True, stop=True)
                    m.then_inc(S("d_Z"), 1)
                    yield
                    pe.wait_ge(S("chunk_masks"), 1)
                    pe.wait_ge(S("d_W1"), n)
                    if l > 1:
                        pe.wait_ge(S("d_U"), before)
                    for tb, a, h, rows_, c in chunks():
                        if l < LEVELS - 1:
                            MM(AX[2][rows_, c * C:(c + 1) * C], Um[rows_, c, :], W1[rows_, c, :], start=True, stop=True)
                        m = MM(AX[3][rows_, c * C:(c + 1) * C], W1[rows_, c, :], Um[rows_, c, :], start=True, stop=True)
                    m.then_inc(S("d_TU"), 1)
                    yield
                n, now = held(gi * L + L), held(gi + 1)
                pe.wait_ge(S("chunk_masks"), 1)
                pe.wait_ge(S("d_U"), n)
                pe.wait_ge(S("d_vb"), now)
                pe.wait_ge(S("d_kbe"), now)
                for tb, a, h, rows_, c in chunks():
                    m = MM(AX[2 + tb][rows_, h * HD:(h + 1) * HD], Um[rows_, c, :], vs[rows_, tb, h * HD:(h + 1) * HD],
                           start=True, stop=True)
                m.then_inc(S("d_u"), 1)
                yield
                pe.wait_ge(S("d_u_out0"), gi + 1)
                pe.wait_ge(S("d_u_out1"), gi + 1)
                for tb, a, h, rows_, c in chunks():
                    m = MM(AX[2 + a][:, c * C:(c + 1) * C], kbe[rows_, tb, h * HD:(h + 1) * HD], Um[rows_, c, :],
                           start=True, stop=True)
                m.then_inc(S("d_w"), 1)
                yield
                now = held(gi + 1)
                pe.wait_ge(S("chunk_masks"), 1)
                pe.wait_ge(S("d_w_out0"), now)
                pe.wait_ge(S("d_w_out1"), now)
                pe.wait_ge(S("d_kdec"), now)
                for n in range(4):
                    tb, a = n // 2, n % 2
                    rows_ = slice(a * C, (a + 1) * C)
                    if n:
                        pe.wait_ge(S("d_state"), gi * 3 + n)
                        for h in range(HG):
                            m = MM(AX[2][rows_, h * HD:(h + 1) * HD], wT[:, a, tb, h, :], St[:, h * HD:(h + 1) * HD],
                                   start=True, stop=True)
                        m.then_inc(S("d_wS"), 1)
                        yield
                        pe.wait_ge(S("d_vnew"), gi * 3 + n)
                        pe.wait_ge(S("d_o_out"), gi * 4 + n)
                    for h in range(HG):
                        c = slice(h * HD, (h + 1) * HD)
                        if n:
                            MM(AX[3][rows_, c], qdT[:, h, tb * P + a * C:tb * P + (a + 1) * C], St[:, c], start=True, stop=False)
                        MM(AX[3][rows_, c], qk[rows_, tb * HG + h, :], tmp[rows_, tb, c], start=n == 0, stop=True)
                    for h in range(HG):
                        c = slice(h * HD, (h + 1) * HD)
                        m = MM(AX[2][:, c], kdec[rows_, tb, c], tmp[rows_, tb, c], start=True, stop=True)
                    m.then_inc(S("d_S_used"), 1)
                    yield
                yield
                yield
                pe.wait_ge(S("d_y"), gi + 1)
                turn_rows(o_rows, (2, 3), "d_y_turned")
                yield
                yield

            def stack(t0, side, group, z_done):
                none = iter(())
                s = none
                for part in range(4):
                    run(half, 8, s)
                    finish(s)
                    s = side(0, part) if part < 3 else none
                with pe.Fori(0, 3) as i:
                    pl.enter(i, t0 + 4, 4)
                    g = group(i)
                    for part in range(4):
                        run(half, 8, s, g)
                        finish(s)
                        if part == 3:
                            finish(g)
                        s = side(i + 1, part) if part < 3 else none
                    pl.leave(3)
                finish(group(3))
                pe.wait_ge(S("z_lo"), z_done)
                run(half, 32)

            if parts >= 3:
                pe.wait_ge(S("crows_landed"), 16 * 5)
                for j in range(4):
                    turn(AX[0][:, j * P:j * P + 3 * H], crows[0:3 * H, j, :], ident[0:3 * H, 0:3 * H])
                turn(AX[1][:, 0:1], crows[0:1, 4, :], ident[0:1, 0:1]).then_inc(S("crows_turned"), 1)
                pe.wait_ge(S("ctap_out"), 1)
                norm_turned(2)
                pe.wait_ge(S("wab_landed"), 16)
                for tb in range(TB):
                    for kt in range(KD):
                        for j, v in enumerate((hT_hi, hT_lo)):
                            m = MM(AX[0][:, tb * 2 * H:(tb + 1) * 2 * H], v[:, kt, tb * P:(tb + 1) * P].bitcast(F32), wab[:, kt, :],
                                   start=kt == 0 and j == 0, stop=kt == KD - 1 and j == 1)
                m.then_inc(S("ab_done"), 1)
                pe.wait_ge(S("ab_g"), 1)
                pe.wait_ge(S("ab_beta"), 1)
                pe.wait_ge(S("chunk_masks"), 1)
                g_all = gg[:, :, :].rearrange("p t h -> p (t h)")
                for a in range(2):
                    rows_ = slice(a * C, (a + 1) * C)
                    MM(AX[2][rows_, 0:TB * H], m_le[rows_, :], g_all[rows_, :], start=True, stop=True)
                    MM(AX[3][rows_, 0:TB * H], ones[rows_, 0:C], g_all[rows_, :], start=True, stop=True)
                    MM(AX[3][rows_, P:P + TB * H], m_le[rows_, :], g_all[rows_, :], start=True, stop=True)
                    m = MM(AX[a][:, P:P + TB * H], ones[rows_, :], g_all[rows_, :], start=True, stop=True)
                m.then_inc(S("gc_done"), 1)
                pe.wait_ge(S("decays"), 1)
                stack(T_A, conv_side, delta, 4)

            def rows_side(gi, part):
                if part == 2:
                    return
                n = gi * 2 + part
                yield
                yield
                yield
                pe.wait_ge(S("b_normed"), n + 1)
                if not isinstance(gi, int) or gi or part:
                    pe.wait_ge(S("b_out0"), n)
                    pe.wait_ge(S("b_out1"), n)
                turn_rows(tok, (0, 1), "b_turned")
                yield
                yield

            def band(gi):
                for pr in range(2):
                    n = gi * 2 + pr
                    if pr == 0:
                        pe.wait_ge(S("b_out0"), gi * 2 + 2)
                        pe.wait_ge(S("b_out1"), gi * 2 + 2)
                        pe.wait_ge(S("read_out0"), gi * 4 + (T_B + 3))
                        pe.wait_ge(S("read_out1"), gi * 4 + (T_B + 3))
                        pe.wait_ge(S("z_lo"), gi + 4)
                    else:
                        pe.wait_ge(S("b_y"), n)
                    for a in range(2):
                        h = 2 * pr + a
                        for tb in range(TB):
                            m = MM(AX[2 + a][:, tb * T:(tb + 1) * T], bqT[:, h, tb * P:(tb + 1) * P], bkT[:, h, :],
                                   start=True, stop=True)
                        m.then_inc(S("b_scores"), 1)
                    yield
                    for a in range(2):
                        pe.wait_ge(S("b_exp"), n * 2 + a + 1)
                        for kb in range(TB):
                            for tb in range(TB):
                                m = turn(AX[2 + a][:, kb * T + tb * P:kb * T + (tb + 1) * P],
                                         bsc[:, a, tb, kb * P:(kb + 1) * P], ident[:, :])
                        m.then_inc(S("b_p_turned"), 1)
                    yield
                    pe.wait_ge(S("b_pT0"), n + 1)
                    pe.wait_ge(S("b_pT1"), n + 1)
                    for a in range(2):
                        c = slice((2 * pr + a) * HD, (2 * pr + a + 1) * HD)
                        for tb in range(TB):
                            for kb in range(tb + 1):
                                m = MM(AX[2 + a][:, tb * HD:(tb + 1) * HD], bpT[:, a, kb, tb * P:(tb + 1) * P], bva[:, kb, c],
                                       start=kb == 0, stop=kb == tb)
                    m.then_inc(S("b_pv"), 1)
                    yield
                pe.wait_ge(S("b_y"), gi * 2 + 2)
                turn_rows(by, (2, 3), "b_y_turned")
                yield
                yield

            if parts >= 4:
                pe.wait_ge(S("bw_landed"), 32)
                turn(AX[0][:, 0:2], bw_rows[:, :], ident[0:2, 0:2]).then_inc(S("bw_turned"), 1)
                pe.wait_ge(S("bw_out"), 1)
                norm_turned(3)
                stack(T_B, rows_side, band, 8)
    return nc


_INS = ["x", "norm_mix", "w_in", "gm_ln_g", "gm_ln_b", "gm_w_s", "gm_b_s", "na_rpb", "w_branch", "w_out", "norm_ffn",
        "w_up", "conv_k", "conv_b", "w_down", "norm_final", "norm_w_2", "a_w_in_2", "a_conv_w_2", "a_a_log_2",
        "a_dt_bias_2", "a_out_norm_w_2", "a_w_out_2", "b_w_in_2", "b_q_norm_w_2", "b_k_norm_w_2", "b_rel_bias_2",
        "b_w_out_2"]


def laid_out(name, a):
    import numpy as np
    if name == "b_rel_bias_2":
        a = a[..., ::-1]
    if name == "na_rpb":
        rows = np.zeros((1, NAH, 7, P), a.dtype)
        rows[..., GRID - NKC:GRID + NKC - 1] = a[:, :, NKR - 4:NKR + 3, :]
        a = rows
    return np.ascontiguousarray(a)


def kernel(**inputs):
    import numpy as np
    import concourse.bacc as bacc
    from concourse.bass_utils import run_bass_kernel_spmd

    nc = bacc.Bacc("TRN2", target_bir_lowering=False, num_devices=1)
    arrays, aps = {}, {}
    for name in _INS:
        a = laid_out(name, np.asarray(inputs[name]))
        arrays[f"in_{name}"] = a
        aps[name] = nc.dram_tensor(f"in_{name}", a.shape, mybir.dt.from_np(a.dtype), kind="ExternalInput").ap()
    out = nc.dram_tensor("out_rows", (1, T, D), F32, kind="ExternalOutput").ap()
    program(nc, aps, out)
    return run_bass_kernel_spmd(nc, [arrays], core_ids=[0]).results[0]["out_rows"]
```

```python
from contextlib import ExitStack
from itertools import chain

import concourse.bass as bass
from concourse import mybir

F32 = mybir.dt.float32
F32R = mybir.dt.float32r
ACT = mybir.ActivationFunctionType
ALU = mybir.AluOpType
AX_X = mybir.AxisListType.X

P = 128
T = 256
TB = T // P
D = 2048
KD = D // P
GMW = 1024
GMG = GMW // P
NAH, NAD = 16, 64
NAW = NAH * NAD
NKR, NKC, GRID = 8, 16, 64
SPAN = 6
F = 5504
FB = F // P
H, HD = 16, 128
HG = 4
C = 64
REL = 256
NEG = -1.0e30
RMS_EPS, LN_EPS = 1e-6, 1e-5

RAW = 4
SPLIT = 4
LOOK = 2
FOUR = [4] * 4
UP1, UP2 = 11, 11
DOWN1 = [2, 4, 4, 4, 4, 4]
DOWN2 = [2, 3, 4, 4, 4, 4]
assert sum(DOWN1) == 2 * UP1 and sum(DOWN1) + sum(DOWN2) == FB


def stream_plan():
    parts = [(FOUR, "h", 0, 512)] * 14
    parts += [(FOUR, "h", 0, 512), ([4, 4], "y", 0, 512), ([4, 4], "y", 8, 512)] * 4
    parts += [(FOUR, "m", 0, 512)] * 4
    parts += [(FOUR, "h", 0, 512)] * UP1 + [(DOWN1, "y", 0, 512)] * 4
    parts += [(FOUR, "h", 0, 512)] * (UP2 - 1) + [(FOUR, "h", 0, 256)] + [(DOWN2, "y", 0, 512)] * 4
    parts = [(t, *p, True, True) for t, p in enumerate(parts)]
    for _ in range(2):
        t = parts[-1][0] + 1
        parts += [(t + j, FOUR, "h", 0, 512, True, True) for j in range(16)]
        t += 16
        parts += [(t + j, [4, 4, 4], "z", 0, 512, True, False) for j in range(2)]
        parts += [(t + j, [4], "z", 12, 512, False, True) for j in range(2)]
        parts += [(t + j, FOUR, "z", 0, 512, True, True) for j in range(2, 4)]
    halves, ends = [], {}
    for t, loads, act, k0, width, begins, ends_ in parts:
        k, n = 0, sum(loads)
        for load in loads:
            first = (load + 1) // 2
            for size in (first, load - first):
                halves.append(dict(tile=t, act=act, kt=k0 + k, n=size, start=begins and k == 0,
                                   stop=ends_ and k + size == n, width=width))
                k += size
        ends[t] = len(halves)
    return halves, [ends[t] for t in range(len(ends))]


HALVES, TILE_END = stream_plan()
T_MERGE = 14
T_OUT = T_MERGE + 12
T_UP1 = T_OUT + 4
T_DOWN1 = T_UP1 + UP1
T_UP2 = T_DOWN1 + 4
T_DOWN2 = T_UP2 + UP2
T_A = T_DOWN2 + 4
T_B = T_A + 20
N_TILES = T_B + 20
assert len(TILE_END) == N_TILES


class Place:

    def __init__(self):
        self.m, self.turn, self.dm, self.dt = 0, 0, 0, 0

    def enter(self, turn, first_tile, tiles):
        self.turn, self.dt = turn, tiles
        self.dm = TILE_END[first_tile + tiles - 1] - TILE_END[first_tile - 1]
        self.m0 = self.m

    def leave(self, turns):
        assert self.m - self.m0 == self.dm, (self.m, self.m0, self.dm)
        self.m, self.turn, self.dm, self.dt = self.m0 + turns * self.dm, 0, 0, 0

    def halves(self, n):
        return self.turn * self.dm + n

    def tiles(self, n):
        return self.turn * self.dt + n


def program(nc, ins, out, parts=4):
    last_tile = {1: T_UP1, 2: T_A, 3: T_B, 4: N_TILES}[parts]
    last_half = TILE_END[last_tile - 1]
    with ExitStack() as ctx:
        sems = {}

        def S(name):
            if name not in sems:
                sems[name] = ctx.enter_context(nc.semaphore(name))
            return sems[name]

        def nbytes(shape):
            n = 4
            for s in shape[1:]:
                n *= s
            return (n + 31) // 32 * 32

        class Region:

            def __init__(self, at, end=None):
                self.at, self.end = at, end or nc.sbuf_usable_end

            def put(self, name, shape, dt=F32):
                t = nc.alloc_sbuf_tensor_at(name, shape, dt, offset=self.at)
                self.at += nbytes(shape)
                assert self.at <= self.end, (name, self.at, self.end)
                return t

        def rep(ap, n):
            dims = [list(d) for d in ap.ap]
            return bass.AP(tensor=ap.tensor, offset=ap.offset, ap=[dims[0], [0, n]] + dims[1:])

        def each(ap, n):
            return bass.AP(tensor=ap.tensor, offset=ap.offset, ap=[list(d) for d in ap.ap] + [[0, n]])

        base = Region((nc.sbuf_base + 63) // 64 * 64)
        raw = base.put("raw", [P, RAW, 2, 512])
        w_hi = base.put("w_hi", [P, SPLIT, 2, 512], F32R)
        w_lo = base.put("w_lo", [P, SPLIT, 2, 512], F32R)
        x = base.put("x_rows", [P, TB, D])
        hT_hi = base.put("hT_hi", [P, KD, T], F32R)
        hT_lo = base.put("hT_lo", [P, KD, T], F32R)
        ident = base.put("ident", [P, P])
        ones = base.put("ones", [P, P])
        gains = base.put("gains", [P, 5, KD])
        taps = base.put("taps", [P, 4, 2 * FB])
        ctap = base.put("conv_taps2", [P, 4, 3 * H])
        head_gains = base.put("head_gains", [P, 4])
        x_stats = base.put("x_stats", [P, TB, 4, 6])
        x_moments = base.put("x_moments", [P, TB, 2])
        squares = base.put("squares", [P, TB, 2])
        rms = base.put("rms", [P, 5, TB])
        rstd = base.put("rstd", [P, 5, TB])
        y_at = base.at
        yT_hi = base.put("yT_hi", [P, 2 * UP1, T], F32R)
        yT_lo = base.put("yT_lo", [P, 2 * UP1, T], F32R)
        scratch = base.at
        r2 = Region(y_at)
        zT_hi = r2.put("zT_hi", [P, KD, T], F32R)
        zT_lo = r2.put("zT_lo", [P, KD, T], F32R)
        scratch2 = r2.at

        G = [[ctx.enter_context(nc.psum_tensor(f"gemm{a}{tb}", [P, 512], F32)) for tb in range(TB)] for a in range(2)]
        AX = [ctx.enter_context(nc.psum_tensor(f"aux{i}", [P, 512], F32)) for i in range(4)]

        r = Region(scratch)
        ga = Region(scratch).put("ga", [P, TB, D])
        vg = r.put("vg", [P, TB, GMW])
        ug = r.put("ug", [P, TB, GMW])
        qkv_tok = r.put("qk_rows", [P, TB, 512])
        qT = r.put("qT", [P, HG, T])
        kT = r.put("kT", [P, HG, T])
        va = r.put("v_rows", [P, TB, 512])
        yb = r.put("yb", [P, TB, 512])
        sc = r.put("scores", [P, 2, TB, T])
        pT = r.put("pT", [P, 2, TB, T])
        mx = r.put("row_max", [P, 2, TB])
        sm = r.put("row_sum", [P, 2, TB])
        ri = r.put("row_inv", [P, 2, TB])
        bsT = r.put("bsT", [P, GMG])
        bn = r.put("bn", [P, TB, 2, 6])
        mv = r.put("mean_var", [P, TB, 2])
        lnr = r.put("ln_rstd", [P, TB])
        BR = 2
        bias = r.put("bias", [P, BR, 2, SPAN, GRID])
        wsT = r.put("wsT", [P, GMG, P])
        lng = r.put("lng", [P, GMW])
        lnb = r.put("lnb", [P, GMW])
        r = Region(scratch + nbytes([P, TB, D]))
        sgb = r.put("sgb", [P, TB, 512])
        mT_hi = r.put("mT_hi", [P, KD, T], F32R)
        mT_lo = r.put("mT_lo", [P, KD, T], F32R)

        r = Region(scratch)
        ut = r.put("up_rows", [P, TB, 512])
        cg = r.put("conv_gate", [P, 2, T])
        cv = r.put("conv_val", [P, 2, T])
        nf = r.put("norm_final", [P, D])

        r = Region(scratch2)
        tok = r.put("tok", [P, TB, 512])
        zs = r.put("silu_z", [P, TB, 512])
        both = r.at
        xc = r.put("conv", [P, HG, T])
        qs = r.put("q_rows", [P, TB, 512])
        ks = r.put("k_rows2", [P, TB, 512])
        vs = r.put("v_rows2", [P, TB, 512])
        o_at = r.at
        knT = r.put("knT", [P, HG, T])
        o_rows = Region(o_at).put("o_rows", [P, TB, 512])
        w_at = r.at
        kbT = r.put("kbT", [P, HG, T])
        wT = Region(w_at).put("wT", [P, 2, TB, HG, C])
        qnT = r.put("qnT", [P, HG, T])
        qdT = r.put("qdT", [P, HG, T])
        kbe = r.put("kbe", [P, TB, 512])
        kdec = r.put("kdec", [P, TB, 512])
        tmp = r.put("tmp", [P, TB, 512])
        dec = r.put("decay", [P, TB * HG, C])
        AT = r.put("A_turned", [P, TB * HG, C])
        ATl = r.put("A_level", [P, TB * HG, C])
        qk = r.put("qk_turned", [P, TB * HG, C])
        Tm = r.put("inverse", [P, TB * HG, C])
        Um = r.put("inverse_turned", [P, TB * HG, C])
        W1 = r.put("W1", [P, TB * HG, C])
        St = r.put("state", [P, HG * HD])
        m_le = r.put("m_le", [P, C])
        m_gt = r.put("m_gt", [P, C])
        idc = r.put("idc", [P, C])
        LEVELS = 6
        m_lev = r.put("m_lev", [P, LEVELS, C])
        alog = r.put("a_log", [P, H])
        dtb = r.put("dt_bias", [P, H])
        gg = r.put("log_decay", [P, TB, H])
        gx = r.put("softplus_parts", [P, TB, H])
        beta = r.put("beta", [P, TB, H])
        egc = r.put("exp_gc", [P, TB, H])
        edec = r.put("exp_rest", [P, TB, H])
        egl = r.put("exp_total", [P, 2, TB, H])
        ssum = r.put("row_squares", [P, 2, TB, HG])
        F_Q, F_KB, F_KBE, F_KDEC, F_V = range(5)
        fac = r.put("factors", [P, 5, TB, HG])
        sso = r.put("o_squares", [P, TB, HG])
        q = Region(w_at)
        wab = q.put("w_ab", [P, KD, 2 * H])
        x_squares = q.put("x_squares", [P, TB, D])
        wab_hi = q.put("w_ab_hi", [P, KD, 2 * H], F32R)
        wab_lo = q.put("w_ab_lo", [P, KD, 2 * H], F32R)
        abT = q.put("ab_turned", [2 * H, T])
        r = Region(both)
        bqT = r.put("bqT", [P, HG, T])
        bkT = r.put("bkT", [P, HG, T])
        bva = r.put("bva", [P, TB, 512])
        by = r.put("by", [P, TB, 512])
        bsc = r.put("bscores", [P, 2, TB, T])
        bpT = r.put("bpT", [P, 2, 3, P])
        bbias = r.put("bbias", [P, H, 2 * P])
        bss = r.put("brow_squares", [P, TB, HG])
        bmx = r.put("brow_max", [P, 2, TB])
        bsm = r.put("brow_sum", [P, 2, TB])
        bri = r.put("brow_inv", [P, 2, TB])

        W = dict(zip(("in", "branch", "out", "up", "down", "a_in", "a_out", "b_in", "b_out"),
                     (ins[n][0] for n in ("w_in", "w_branch", "w_out", "w_up", "w_down", "a_w_in_2", "a_w_out_2",
                                          "b_w_in_2", "b_w_out_2"))))
        bsq = r.put("bsquares", [P, TB, 512])
        SKEW, BAND = 7 * P, 2 * P + C
        na_skew = nc.dram_tensor("na_bias_copies", (NAH, GRID, SKEW), F32, kind="Internal").ap()
        band_skew = nc.dram_tensor("band_bias_copies", (H, C, BAND), F32, kind="Internal").ap()

        block = ctx.enter_context(nc.Block())

        @block.sync
        def _(sp):
            count = [0]

            def tile(name, loads, col, k0=0, turn=0, halves=0, width=512):
                k = k0
                for n in [size for load in loads for size in ((load + 1) // 2, load // 2)]:
                    m = count[0]
                    slot = m % RAW
                    if halves:
                        sp.wait_ge(S("gains_landed"), 16 * 4)
                    if m >= RAW:
                        sp.wait_ge(S("lo_done"), turn * halves + (m - RAW + 1))
                    src = W[name][k * P:(k + n) * P, :]
                    if name == "up":
                        src = src.rearrange("(k p) (two f) -> p k two f", p=P, two=2)[:, :, :, bass.ds(col, width // 2)]
                        for j in range(2):
                            sp.dma_start(raw[:, slot, 0:n, j * (width // 2):(j + 1) * (width // 2)],
                                         src[:, :, j, :]).then_inc(S(f"w_landed{slot}"), 16)
                    else:
                        src = src.rearrange("(k p) n -> p k n", p=P)[:, :, bass.ds(col, width)]
                        sp.dma_start(raw[:, slot, 0:n, 0:width], src).then_inc(S(f"w_landed{slot}"), 16)
                    count[0] += 1
                    k += n

            def loop(turns, halves, per_turn):
                before = count[0]
                with sp.Fori(0, turns) as i:
                    per_turn(i, dict(turn=i, halves=halves))
                assert count[0] == before + halves, (count[0], before, halves)
                count[0] = before + turns * halves

            for col in (GMW, GMW + 512, 0, 512):
                tile("in", FOUR, col)
            for g in range(2):
                for part in range(3):
                    tile("in", FOUR, 2 * GMW + part * NAW + g * 512)
            gate_a = 2 * GMW + 3 * NAW
            loop(4, 8, lambda i, kw: tile("in", FOUR, i * 512 + gate_a, **kw))

            def merge(i, kw):
                tile("in", FOUR, i * 512 + (gate_a + D), **kw)
                tile("branch", [4, 4], i * 256 * 2, 0, **kw)
                tile("branch", [4, 4], i * 512, 8, **kw)
            loop(4, 16, merge)
            loop(4, 8, lambda i, kw: tile("out", FOUR, i * 512, **kw))
            if parts >= 2:
                loop(UP1, 8, lambda i, kw: tile("up", FOUR, i * 256, **kw))
                loop(4, 2 * len(DOWN1), lambda i, kw: tile("down", DOWN1, i * 512, **kw))
                loop(UP2 - 1, 8, lambda i, kw: tile("up", FOUR, i * 256 + UP1 * 256, **kw))
                tile("up", FOUR, (UP1 + UP2 - 1) * 256, width=256)
                loop(4, 2 * len(DOWN2), lambda i, kw: tile("down", DOWN2, i * 512, 2 * UP1, **kw))
            for name, part in (("a", 3), ("b", 4)):
                if parts >= part:
                    for j in range(3):
                        tile(name + "_in", FOUR, j * D)

                    def group(i, kw):
                        tile(name + "_in", FOUR, i * 512 + 3 * D, **kw)
                        for j in range(3):
                            tile(name + "_in", FOUR, i * 512 + (j * D + 512), **kw)
                    loop(3, 32, group)
                    tile(name + "_in", FOUR, 3 * 512 + 3 * D)
                    for k0, loads in ((0, [4, 4, 4]), (12, [4])):
                        for col in (0, 512):
                            tile(name + "_out", loads, col, k0)
                    for col in (1024, 1536):
                        tile(name + "_out", FOUR, col)

            if parts == 2:
                sp.wait_ge(S("x_normed"), 4)
            for c in range(4):
                for tb in range(TB):
                    if parts != 2:
                        sp.wait_ge(S(f"read_out{tb}"), last_tile - 3 + c)
                    cols = slice(c * 512, (c + 1) * 512)
                    sp.dma_start(out[0, tb * P:(tb + 1) * P, cols], x[:, tb, cols]).then_inc(S("stored"), 16)
            sp.wait_ge(S("stored"), 16 * TB * 4)

        def increments(t):
            return 32 if T_UP1 <= t < T_DOWN1 or T_UP2 <= t < T_DOWN2 else 16

        landed, seen = [], [0] * RAW
        for m, h in enumerate(HALVES):
            seen[m % RAW] += increments(h["tile"])
            landed.append(seen[m % RAW])

        def slots(m):
            k, w = slice(0, HALVES[m]["n"]), slice(0, HALVES[m]["width"])
            return raw[:, m % RAW, k, w], w_hi[:, m % SPLIT, k, w], w_lo[:, m % SPLIT, k, w]

        def act_half(act, pl):
            m = pl.m
            if m >= last_half:
                return
            per_turn = increments(HALVES[pl.m0]["tile"]) * pl.dm // RAW if pl.dm else 0
            act.wait_ge(S(f"w_landed{m % RAW}"), pl.turn * per_turn + landed[m])
            if m >= SPLIT:
                act.wait_ge(S("half_done"), pl.halves(m - SPLIT + 1))
            src, hi, _ = slots(m)
            nc.scalar.activation(hi, src, ACT.Copy).then_inc(S("hi_done"), 1)
            pl.m += 1

        def dve_half(dve, pl):
            m = pl.m
            if m >= last_half:
                return
            dve.wait_ge(S("hi_done"), pl.halves(m + 1))
            src, hi, lo = slots(m)
            nc.vector.tensor_tensor(lo, src, hi.bitcast(F32), ALU.subtract).then_inc(S("lo_done"), 1)
            pl.m += 1

        def pe_half(pe, pl):
            m = pl.m
            if m >= last_half:
                return
            h = HALVES[m]
            t, w = h["tile"], h["width"]
            if h["start"] and t >= 2:
                for tb in range(TB):
                    pe.wait_ge(S(f"read_out{tb}"), pl.tiles(t - 1))
            pe.wait_ge(S("lo_done"), pl.halves(m + 1))
            hi, lo = {"h": (hT_hi, hT_lo), "y": (yT_hi, yT_lo), "m": (mT_hi, mT_lo), "z": (zT_hi, zT_lo)}[h["act"]]
            _, wh, wl = slots(m)
            for k in range(h["n"]):
                for tb in range(TB):
                    xh = hi[:, h["kt"] + k, tb * P:(tb + 1) * P]
                    xl = lo[:, h["kt"] + k, tb * P:(tb + 1) * P]
                    dst = G[t % 2][tb][:, 0:w]
                    nc.tensor.matmul(dst, xh, wl[:, k, :], start=h["start"] and k == 0, stop=False)
                    nc.tensor.matmul(dst, xh, wh[:, k, :], start=False, stop=False)
                    mm = nc.tensor.matmul(dst, xl, wh[:, k, :], start=False, stop=h["stop"] and k == h["n"] - 1)
            mm.then_inc(S("half_done"), 1)
            pl.m += 1

        def tile_done(eng, pl, t):
            eng.wait_ge(S("half_done"), pl.halves(TILE_END[t]))

        def run(half, halves, *sides):
            for _ in range(halves):
                half()
                for s in sides:
                    next(s, None)

        def finish(*sides):
            for s in sides:
                for _ in s:
                    pass

        @block.gpsimd
        def _(pool):
            nc.gpsimd.memset(ones[:, :], 1.0)
            nc.gpsimd.memset(ident[:, :], 0.0)
            pool.drain()
            nc.gpsimd.affine_select(out=ident[:, :], in_=ident[:, :], compare_op=ALU.not_equal, fill=1.0,
                                    base=0, pattern=[[-1, P]], channel_multiplier=1).then_inc(S("constants"), 1)
            for u in range(NAH // 2):
                pool.wait_ge(S(f"bias_landed{u % BR}"), 64 * (u // BR + 1))
                for a in range(2):
                    v = bias[a * GRID:(a + 1) * GRID, u % BR, :, :, :].rearrange("p a b k -> p (a b) k")
                    below, above = v[:, :, 0:GRID - NKC], v[:, :, NKC:GRID]
                    nc.gpsimd.affine_select(out=below, in_=below, compare_op=ALU.is_ge, fill=NEG, base=NKC // 2,
                                            pattern=[[0, 2 * SPAN], [1, GRID - NKC]], channel_multiplier=-1)
                    pool.drain()
                    nc.gpsimd.affine_select(out=above, in_=above, compare_op=ALU.is_ge, fill=NEG, base=NKC // 2 - 1 - NKC,
                                            pattern=[[0, 2 * SPAN], [-1, GRID - NKC]],
                                            channel_multiplier=1).then_inc(S("bias_masked"), 1)

            if parts >= 3:
                pool.wait_ge(S("read_out1"), T_UP1)
                nc.gpsimd.memset(m_le[:, :], 1.0)
                nc.gpsimd.memset(m_gt[:, :], 1.0)
                nc.gpsimd.memset(idc[:, :], 0.0)
                nc.gpsimd.memset(m_lev[:, :, :], 0.0)
                pool.drain()
                for l in range(LEVELS):
                    b = 1 << l
                    nc.gpsimd.memset(m_lev[:, l, :].rearrange("p (i r) -> p i r", r=2 * b)[:, :, b:2 * b], 1.0)
                pool.drain()
                for a in range(2):
                    rows_ = slice(a * C, (a + 1) * C)
                    sel = nc.gpsimd.affine_select
                    sel(out=m_le[rows_, :], in_=m_le[rows_, :], compare_op=ALU.is_ge, fill=0.0, base=0,
                        pattern=[[1, C]], channel_multiplier=-1)
                    sel(out=m_gt[rows_, :], in_=m_gt[rows_, :], compare_op=ALU.is_ge, fill=0.0, base=-1,
                        pattern=[[-1, C]], channel_multiplier=1)
                    sel(out=idc[rows_, :], in_=idc[rows_, :], compare_op=ALU.not_equal, fill=1.0, base=0,
                        pattern=[[-1, C]], channel_multiplier=1)
                    for l in range(LEVELS):
                        b = 1 << l
                        v = m_lev[rows_, l, :].rearrange("p (i r) -> p i r", r=2 * b)[:, :, b:2 * b]
                        n = C // (2 * b)
                        sel(out=v, in_=v, compare_op=ALU.is_ge, fill=0.0, base=0, pattern=[[-2 * b, n], [0, b]],
                            channel_multiplier=1)
                        pool.drain()
                        e = sel(out=v, in_=v, compare_op=ALU.is_ge, fill=0.0, base=b - 1, pattern=[[2 * b, n], [0, b]],
                                channel_multiplier=-1)
                e.then_inc(S("chunk_masks"), 1)

                def scaled(dst, src, f, event):
                    e = nc.gpsimd.tensor_tensor(dst[:, :, :].rearrange("p t (h d) -> p t h d", h=HG),
                                                src[:, :, :].rearrange("p t (h d) -> p t h d", h=HG), each(f, HD), ALU.mult)
                    e.then_inc(S(event), 1)

                def delta(gi):
                    pool.wait_ge(S("d_rows"), gi * 4 + 1)
                    scaled(kdec, ks, fac[:, F_KDEC, :, :], "d_kdec")
                    scaled(kbe, ks, fac[:, F_KBE, :, :], "d_kbe")
                    for l in range(1, LEVELS):
                        if l == 1:
                            pool.wait_ge(S("d_U1"), gi + 1)
                        else:
                            pool.wait_ge(S("d_Z"), gi * (LEVELS - 1) + l - 1)
                        nc.gpsimd.tensor_tensor(ATl[:, :, :], AT[:, :, :], rep(m_lev[:, l, :], TB * HG),
                                                ALU.mult).then_inc(S("d_level"), 1)
                    pool.wait_ge(S("d_v_rows"), gi * 2 + 2)
                    scaled(vs, vs, fac[:, F_V, :, :], "d_vb")
                with pool.Fori(0, 4) as i:
                    delta(i)
            if parts >= 4:
                pool.wait_ge(S("z_lo"), 4)
                nc.gpsimd.memset(bbias[0:C, :, P + C:], NEG).then_inc(S("band_cut"), 1)

        @block.scalar
        def _(act):
            pl = Place()
            half = lambda: act_half(act, pl)
            A = nc.scalar.activation
            none = iter(())

            def root(c):
                act.wait_ge(S("meansq"), c + 1)
                A(rms[:, c, :], rms[:, c, :], ACT.Sqrt).then_inc(S("rooted"), 1)

            def x_hi(j, s, i):
                b = 2 * s + i
                act.wait_ge(S("hT_turned"), 8 * j + b + 1)
                for kt in (2 * b, 2 * b + 1):
                    e = A(hT_hi[:, kt, :], AX[b % 4][:, (kt % 2) * T:(kt % 2 + 1) * T], ACT.Copy, scale=gains[:, j, kt:kt + 1])
                e.then_inc(S("hT_hi_done"), 1)

            def turn_x(j, s, c=None):
                yield
                yield
                if c is not None:
                    root(c)
                x_hi(j, s, 0)
                yield
                x_hi(j, s, 1)
                if c != 2:
                    yield

            def hi_parts(dst, k0, banks, event, n, done):
                act.wait_ge(S(event), n)
                for i, b in enumerate(banks):
                    e = A(dst[:, bass.ds(k0 + 2 * i, 2), :], AX[b][:, :].rearrange("p (a t) -> p a t", a=2), ACT.Copy)
                e.then_inc(S(done), 1)

            for s in range(4):
                cols = slice(s * 512, (s + 1) * 512)
                act.dma_start(x[:, :, cols], ins["x"][0, :, cols].rearrange("(t p) c -> p t c", p=P)).then_inc(S(f"x_landed{s}"), 16)
                if s == 0:
                    act.dma_start(gains[:, 0, :], ins["norm_mix"]).then_inc(S("first_gains"), 16)
            for j, v in enumerate((ins["norm_ffn"], ins["norm_w_2"][0], ins["norm_w_2"][1], ins["norm_final_cols"])):
                act.dma_start(gains[:, 1 + j, :], v).then_inc(S("gains_landed"), 16)
            act.dma_start(bsT[:, :], ins["gm_b_s"]).then_inc(S("consts_landed"), 16)
            act.dma_start(wsT[:, :, :], ins["gm_w_s"]).then_inc(S("consts_landed"), 16)
            act.dma_start(lng[:, :], ins["gm_ln_g"][0].partition_broadcast(P)).then_inc(S("consts_landed"), 16)
            act.dma_start(lnb[:, :], ins["gm_ln_b"][0].partition_broadcast(P)).then_inc(S("consts_landed"), 16)
            act.dma_start(taps[:, 0:3, :], ins["conv_k"]).then_inc(S("consts_landed"), 16)
            act.dma_start(taps[:, 3, :], ins["conv_b"]).then_inc(S("consts_landed"), 16)
            act.dma_start(ctap[:, :, :], ins["a_conv_w_2"]).then_inc(S("consts_landed"), 16)
            for j, n in enumerate(("a_out_norm_w_2", "b_q_norm_w_2", "b_k_norm_w_2")):
                act.dma_start(head_gains[:, j:j + 1], ins[n]).then_inc(S("consts_landed"), 16)

            def copy_bias(copies, src, pitch, event, h, n):
                src = bass.AP(tensor=src.tensor, offset=h * pitch, ap=[[pitch, n], [0, C], [1, copies.shape[2]]])
                act.dma_start(copies[h:h + n], src).then_inc(S(event), 16)

            def load_bias(u):
                act.wait_ge(S(f"na_copied{u // 2}"), 16)
                for a in range(2):
                    for h in range(2):
                        src = bass.AP(tensor=na_skew.tensor, offset=(2 * u + h) * GRID * SKEW + (1 - a) * P + GRID - 1,
                                      ap=[[SKEW - 1, GRID], [P, SPAN], [1, GRID]])
                        act.dma_start(bias[a * GRID:(a + 1) * GRID, u % BR, h, :, :], src).then_inc(S(f"bias_landed{u % BR}"), 16)

            act.wait_ge(S("first_gains"), 16)
            for i in range(2):
                x_hi(0, 0, i)
            run(half, LOOK)
            for s in range(1, 4):
                for i in range(2):
                    x_hi(0, s, i)
                run(half, 2)
            root(0)
            run(half, 2)
            act.wait_ge(S("consts_landed"), 16 * 10)
            act.wait_ge(S("rstd_done"), 1)

            def mixing():
                yield
                act.wait_ge(S("ln_var"), 1)
                A(lnr[:, :], mv[:, :, 1], ACT.Sqrt).then_inc(S("ln_sd"), 1)
                for _ in range(15 + 8):
                    yield
                for b in range(4):
                    yield
                    hi_parts(yT_hi, 2 * b, (2 + b % 2,), "ya_turned", b + 1, "ya_hi")

            def attend(g):
                for pr in range(4):
                    u = 4 * g + pr
                    yield
                    for a in range(2):
                        act.wait_ge(S("na_max"), 2 * u + a + 1)
                        for tb in range(TB):
                            e = A(sc[:, a, tb, :], sc[:, a, tb, :], ACT.Exp, bias=mx[:, a, tb:tb + 1],
                                  accum_out=sm[:, a, tb:tb + 1])
                        e.then_inc(S("na_exp"), 1)
                    yield
                    act.wait_ge(S("na_p_turned"), 2 * u + 1)
                    A(pT[:, 0, :, :], AX[2][:, :].rearrange("p (k t) -> p k t", k=TB), ACT.Copy).then_inc(S("na_pT0"), 1)
                    if u + BR < NAH // 2:
                        act.wait_ge(S("na_max"), 2 * u + 2)
                        load_bias(u + BR)
                    yield
                    yield
                yield
                hi_parts(yT_hi, 8 + 4 * g, (2, 3), "yb_turned", g + 1, "yb_hi")
                yield

            def qkv_side(g, part):
                for _ in range(6):
                    yield
                act.wait_ge(S("qk_turned"), 2 * g + part + 1)
                A((qT, kT)[part][:, 0:2, :], AX[0][:, :].rearrange("p (a t) -> p a t", a=2), ACT.Copy).then_inc(S("qk_out0"), 1)
                yield
                yield

            mix = mixing()
            for t in range(4):
                run(half, 8 if t else 0, mix if t >= 2 else none)
                tile_done(act, pl, t)
                for tb in range(TB):
                    A((vg if t < 2 else ug)[:, tb, (t % 2) * 512:(t % 2) * 512 + 512], G[t % 2][tb][:, :],
                      ACT.Gelu_apprx_tanh, scale=rstd[:, 0, tb:tb + 1]).then_inc(S(f"read_out{tb}"), 1)
                copy_bias(na_skew, ins["na_rpb"], SKEW, f"na_copied{t}", 4 * t, 4)
                if t == 2:
                    for u in range(BR):
                        load_bias(u)
            side = none
            att = none
            for g in range(2):
                for part in range(3):
                    t = 4 + 3 * g + part
                    run(half, 8, mix, side, att)
                    finish(side)
                    tile_done(act, pl, t)
                    if t > 4 and part < 2:
                        act.wait_ge(S("qk_turned"), 2 * g + part)
                    if part == 2 and g:
                        act.wait_ge(S("na_pv"), 4)
                    A((va if part == 2 else qkv_tok)[:, 0, :], G[t % 2][0][:, :], ACT.Copy,
                      scale=rstd[:, 0, 0:1]).then_inc(S("read_out0"), 1)
                    side = qkv_side(g, part) if part < 2 else none
                finish(att)
                att = attend(g)
            for i in range(4):
                t = 10 + i
                run(half, 8, att)
                tile_done(act, pl, t)
                if i == 0:
                    act.wait_ge(S("ya_lo"), 4)
                for tb in range(TB):
                    A(ga[:, tb, i * 512:(i + 1) * 512], G[t % 2][tb][:, :], ACT.Sigmoid,
                      scale=rstd[:, 0, tb:tb + 1]).then_inc(S(f"read_out{tb}"), 1)
            finish(att)
            def turn_merged(n):
                yield
                for i in range(2):
                    yield
                    b = 2 * n + i
                    hi_parts(mT_hi, 2 * b, (b % 4,), "merged_turned", b + 1, "merged_hi")

            for n in range(4):
                t = T_MERGE + 3 * n
                run(half, 8, turn_merged(n - 1) if n else none)
                tile_done(act, pl, t)
                if n:
                    act.wait_ge(S("merged"), n)
                for tb in range(TB):
                    A(sgb[:, tb, :], G[t % 2][tb][:, :], ACT.Sigmoid, scale=rstd[:, 0, tb:tb + 1]).then_inc(S(f"read_out{tb}"), 1)
                run(half, 8)
            run(half, 8, turn_merged(3))
            for s in range(3):
                run(half, 8, turn_x(1, s))

            def up_side(j, kt, n, width=2):
                w = width
                yield
                for b, (dst, blk) in enumerate(((cg, j * 2), (cv, j * 2 + FB))):
                    act.wait_ge(S("up_turned"), n * 2 + b + 1)
                    for e in range(w):
                        i = A(dst[:, e, :], AX[b][:, e * T:(e + 1) * T], ACT.Identity,
                              scale=taps[:, 1, bass.ds(blk + e, 1)], bias=taps[:, 3, bass.ds(blk + e, 1)])
                    i.then_inc(S("conv_mid"), 1)
                yield
                act.wait_ge(S("conv_gate_done"), n + 1)
                A(cg[:, 0:w, :], cg[:, 0:w, :], ACT.Silu).then_inc(S("silu_done"), 1)
                yield
                act.wait_ge(S("gated"), n + 1)
                A(yT_hi[:, bass.ds(kt, w), :], cv[:, 0:w, :], ACT.Copy).then_inc(S("act_hi"), 1)
                yield

            def up_read(t, n):
                tile_done(act, pl, t)
                w = HALVES[TILE_END[t] - 1]["width"]
                if not isinstance(n, int) or n:
                    act.wait_ge(S("up_turned"), n * 2)
                A(ut[:, 0, 0:w], G[t % 2][0][:, 0:w], ACT.Copy, scale=rstd[:, 1, 0:1]).then_inc(S("read_out0"), 1)

            def feed_forward(t0, j0, tiles, loads, half_tile):
                pairs = (tiles - 2) // 2
                run(half, 8, none if j0 else turn_x(1, 3, 1))
                if j0 == 0:
                    act.wait_ge(S("rstd_done"), 2)
                up_read(t0, j0)
                with act.Fori(0, pairs) as i:
                    pl.enter(i, t0 + 1, 2)
                    for s in range(2):
                        run(half, 8, up_side(i * 2 + (j0 + s), i * 4 + 2 * s, i * 2 + (j0 + s)))
                        up_read(t0 + 1 + s, i * 2 + (j0 + s + 1))
                    pl.leave(pairs)
                s = 2 * pairs
                while s < tiles - 1:
                    run(half, 8, up_side(j0 + s, 2 * s, j0 + s))
                    up_read(t0 + 1 + s, j0 + s + 1)
                    s += 1
                run(half, 2 * len(loads), up_side(j0 + s, 2 * s, j0 + s, 1 if half_tile else 2))
                for s in range(3):
                    run(half, 2 * len(loads), turn_x(2, s) if j0 else none)

            if parts >= 2:
                act.wait_ge(S("read_out1"), T_UP1 - 3)
                copy_bias(band_skew, ins["b_rel_bias_2"], 2 * REL + 1, "band_copied", 0, H)
                act.dma_start(nf[:, :], ins["norm_final"].partition_broadcast(P)).then_inc(S("nf_landed"), 16)
                feed_forward(T_UP1, 0, UP1, DOWN1, 0)
                feed_forward(T_UP2, UP1, UP2, DOWN2, 1)

            def sums_of_squares(src, dst, junk, event=None, after=None, blocks=range(TB)):
                act.drain()
                if after:
                    act.wait_ge(S(after[0]), after[1])
                for tb in blocks:
                    for h in range(HG):
                        c = slice(h * HD, (h + 1) * HD)
                        e = A(junk[:, tb, c], src[:, tb, c], ACT.Square, accum_out=dst[:, tb, h:h + 1])
                if event:
                    e.then_inc(S(event), 1)

            def conv_side(gi, part):
                n = gi * 3 + part
                yield
                for b in range(2):
                    act.wait_ge(S("c_turned"), n * 2 + b + 1)
                    for e in range(2):
                        i = A(xc[:, 2 * b + e, :], AX[b][:, e * T:(e + 1) * T], ACT.Copy,
                              scale=ctap[:, 3, bass.ds(gi * HG + (part * H + 2 * b + e), 1)])
                    i.then_inc(S("c_mid"), 1)
                yield
                yield
                act.wait_ge(S("c_conv"), n + 1)
                A(xc[:, :, :], xc[:, :, :], ACT.Silu).then_inc(S("c_silu"), 1)
                yield
                yield
                act.wait_ge(S("c_back"), n + 1)
                if part == 2:
                    dst, event = vs, "d_v_rows"
                else:
                    dst, event = (qs, ks)[part], "c_rows0"
                A(dst[:, 0, :], AX[0][:, :], ACT.Copy).then_inc(S(event), 1)
                yield
                if part < 2:
                    squares = xc[:, :, :].rearrange("p (t a) c -> p t (a c)", t=TB)
                    sums_of_squares(dst, ssum[:, part, :, :], squares, "d_sums", ("c_rows1", gi * 2 + part + 1))
                yield
                if part == 1:
                    act.wait_ge(S("d_eps"), gi + 1)
                    A(ssum[:, :, :, :], ssum[:, :, :, :], ACT.Sqrt).then_inc(S("d_root"), 1)
                yield

            def delta(gi):
                yield
                yield
                for j, dst in enumerate((kbT, qnT, knT, qdT)):
                    act.wait_ge(S("d_turned"), gi * 4 + j + 1)
                    A(dst[:, 0:2, :], AX[2][:, :].rearrange("p (a t) -> p a t", a=2), ACT.Copy).then_inc(S("d_out0"), 1)
                    yield
                act.wait_ge(S("d_arg"), gi + 1)
                A(dec[:, :, :], AX[2][:, :].rearrange("p (a c) -> p a c", c=C), ACT.Exp).then_inc(S("d_exp"), 1)
                yield
                yield
                act.wait_ge(S("d_T1"), gi + 1)
                A(Tm[:, :, :], AX[2][:, :].rearrange("p (a c) -> p a c", c=C), ACT.Copy).then_inc(S("d_T"), 1)
                yield
                for l in range(1, LEVELS):
                    yield
                    if l < LEVELS - 1:
                        act.wait_ge(S("d_TU"), gi * (LEVELS - 1) + l)
                        A(Tm[:, :, :], AX[2][:, :].rearrange("p (a c) -> p a c", c=C), ACT.Copy).then_inc(S("d_T"), 1)
                    yield
                act.wait_ge(S("d_u"), gi + 1)
                A(tmp[:, 0, :], AX[2][:, :], ACT.Copy).then_inc(S("d_u_out0"), 1)
                yield
                act.wait_ge(S("d_w"), gi + 1)
                A(wT[:, 0, :, :, :], AX[2][:, :].rearrange("p (t h c) -> p t h c", t=TB, h=HG), ACT.Copy).then_inc(S("d_w_out0"), 1)
                yield
                for n in range(4):
                    tb, a = n // 2, n % 2
                    rows_ = slice(a * C, (a + 1) * C)
                    if n:
                        yield
                    act.wait_ge(S("d_S_used"), gi * 4 + n + 1)
                    A(o_rows[rows_, tb, :], AX[3][rows_, :], ACT.Copy).then_inc(S("d_o_out"), 1)
                    yield
                    if a == 1:
                        sums_of_squares(o_rows, sso, kbe, "d_o_sums" if tb else None, blocks=(tb,))
                act.wait_ge(S("d_o_mean"), gi + 1)
                A(sso[:, :, :], sso[:, :, :], ACT.Sqrt).then_inc(S("d_o_root"), 1)
                yield
                yield
                yield
                act.wait_ge(S("d_y_turned"), gi + 1)
                for b in range(2):
                    i = A(zT_hi[:, bass.ds(gi * HG + 2 * b, 2), :], AX[2 + b][:, :].rearrange("p (a t) -> p a t", a=2), ACT.Copy,
                          scale=head_gains[:, 0:1])
                i.then_inc(S("z_hi"), 1)
                yield

            def read_rows(t, part, bufs, norm):
                tile_done(act, pl, t)
                if part == 3:
                    for tb in range(TB):
                        A(zs[:, tb, :], G[t % 2][tb][:, :], ACT.Silu, scale=rstd[:, norm, tb:tb + 1]).then_inc(S(f"read_out{tb}"), 1)
                else:
                    A(bufs[part][:, 0, :], G[t % 2][0][:, :], ACT.Copy, scale=rstd[:, norm, 0:1]).then_inc(S("read_out0"), 1)

            def stack(t0, side, group, bufs, norm, first, second, pace, out_turned):
                for part in range(3):
                    run(half, 8, side(0, part - 1) if part else first, second if part else none)
                    if part == 0:
                        finish(first)
                        act.wait_ge(S("rstd_done"), norm + 1)
                    read_rows(t0 + part, part, bufs, norm)
                finish(second)
                with act.Fori(0, 3) as i:
                    pl.enter(i, t0 + 3, 4)
                    g = group(i)
                    run(half, 8, g)
                    read_rows(t0 + 3, 3, bufs, norm)
                    for part in range(3):
                        run(half, 8, side(i + 1, part - 1) if part else side(i, 2), g)
                        if part == 2:
                            finish(g)
                        read_rows(t0 + 4 + part, part, bufs, norm)
                    pl.leave(3)
                g, s = group(3), side(3, 2)
                run(half, 3, g)
                run(half, 5, s, g)
                read_rows(t0 + 15, 3, bufs, norm)
                run(half, 12, s, *[g] * pace)
                finish(g)
                run(half, 4)
                run(half, 8, chain(out_turned(0), out_turned(1)))
                run(half, 8, out_turned(2))

            def renorm():
                yield from turn_x(2, 3, 2)
                for k in range(4):
                    act.wait_ge(S("x_normed"), k + 1)
                    tb, e = k // 2, k % 2
                    cols = slice(e * 1024, (e + 1) * 1024)
                    i = A(x_squares[:, tb, cols], x[:, tb, cols], ACT.Square, accum_out=squares[:, tb, e:e + 1])
                    if k < 3:
                        yield
                i.then_inc(S("x_squared"), 1)
                root(3)

            def decays():
                act.wait_ge(S("wab_landed"), 16)
                A(wab_hi[:, :, :], wab[:, :, :], ACT.Copy).then_inc(S("wab_hi_done"), 1)
                for _ in range(5):
                    yield
                act.wait_ge(S("ab_done"), 1)
                A(abT[:, :], AX[3][0:2 * H, 0:T], ACT.Copy).then_inc(S("ab_out"), 1)
                yield
                yield
                act.wait_ge(S("ab_landed"), 32)
                A(alog[:, :], alog[:, :], ACT.Exp)
                act.wait_ge(S("ab_sum"), 1)
                A(beta[:, :, :], gx[:, :, :], ACT.Abs)
                act.drain()
                A(beta[:, :, :], beta[:, :, :], ACT.Exp, scale=-1.0).then_inc(S("ab_exp"), 1)
                yield
                yield
                act.wait_ge(S("ab_one"), 1)
                A(beta[:, :, :], beta[:, :, :], ACT.Ln).then_inc(S("ab_ln"), 1)
                yield
                yield
                act.wait_ge(S("ab_g"), 1)
                for tb in range(TB):
                    e = A(beta[:, tb, :], AX[2][:, tb * 2 * H + H:(tb + 1) * 2 * H], ACT.Sigmoid, scale=rstd[:, 3, tb:tb + 1])
                e.then_inc(S("ab_beta"), 1)
                yield
                yield
                act.wait_ge(S("gc_done"), 1)
                A(egc[:, :, :], AX[2][:, 0:TB * H].rearrange("p (t h) -> p t h", t=TB), ACT.Exp)
                A(egl[:, 0, :, :], AX[2][:, 2 * P:2 * P + TB * H].rearrange("p (t h) -> p t h", t=TB), ACT.Exp)
                act.wait_ge(S("g_rest"), 1)
                A(egl[:, 1, :, :], AX[3][:, 2 * P:2 * P + TB * H].rearrange("p (t h) -> p t h", t=TB), ACT.Exp)
                A(edec[:, :, :], edec[:, :, :], ACT.Exp).then_inc(S("decays"), 1)
                yield

            if parts >= 3:
                act.dma_start(alog[:, :], ins["a_a_log_2"][0].partition_broadcast(P)).then_inc(S("ab_landed"), 16)
                act.dma_start(dtb[:, :], ins["a_dt_bias_2"][0].partition_broadcast(P)).then_inc(S("ab_landed"), 16)
                act.dma_start(wab[:, :, :], W["a_in"][:, 4 * D:].rearrange("(k p) n -> p k n", p=P)).then_inc(S("wab_landed"), 16)
                stack(T_A, conv_side, delta, (tok, tok, tok), 3, renorm(), decays(), 2, lambda s: turn_x(3, s))
            elif parts == 2:
                finish(renorm())

            def rows_side(gi, part):
                n = gi * 2 + part
                if part == 2:
                    return
                sums_of_squares(tok, bss, bsq, "b_sums", ("read_out1", gi * 4 + (T_B + part + 1)))
                yield
                act.wait_ge(S("b_mean"), n + 1)
                A(bss[:, :, :], bss[:, :, :], ACT.Sqrt).then_inc(S("b_root"), 1)
                yield
                yield
                yield
                act.wait_ge(S("b_turned"), n + 1)
                for e in range(2):
                    i = A((bqT, bkT)[part][:, e, :], AX[0][:, e * T:(e + 1) * T], ACT.Copy,
                          scale=head_gains[:, 1 + part:2 + part])
                i.then_inc(S("b_out0"), 1)
                yield

            def band(gi):
                for _ in range(8):
                    yield
                for pr in range(2):
                    n = gi * 2 + pr
                    yield
                    for a in range(2):
                        act.wait_ge(S("b_max"), n * 2 + a + 1)
                        for tb in range(TB):
                            seen = slice(0, (tb + 1) * P)
                            e = A(bsc[:, a, tb, seen], bsc[:, a, tb, seen], ACT.Exp, bias=bmx[:, a, tb:tb + 1], accum_out=bsm[:, a, tb:tb + 1])
                        e.then_inc(S("b_exp"), 1)
                    yield
                    yield
                    act.wait_ge(S("b_p_turned"), n * 2 + 1)
                    A(bpT[:, 0, :, :], AX[2][:, 0:3 * P].rearrange("p (k t) -> p k t", k=3), ACT.Copy).then_inc(S("b_pT0"), 1)
                    yield
                    yield
                yield
                act.wait_ge(S("b_y_turned"), gi + 1)
                for b in range(2):
                    e = A(zT_hi[:, bass.ds(gi * HG + 2 * b, 2), :], AX[2 + b][:, :].rearrange("p (a t) -> p a t", a=2), ACT.Copy)
                e.then_inc(S("z_hi"), 1)
                yield

            if parts >= 4:
                act.wait_ge(S("band_cut"), 1)
                act.wait_ge(S("band_copied"), 16)
                for a, w in enumerate((P + C, 2 * P)):
                    src = bass.AP(tensor=band_skew.tensor, offset=P - a * C, ap=[[BAND - 1, C], [C * BAND, H], [1, w]])
                    act.dma_start(bbias[a * C:(a + 1) * C, :, 0:w], src).then_inc(S("band_landed"), 16)
                stack(T_B, rows_side, band, (tok, tok, bva), 4, turn_x(3, 3, 4), none, 1, lambda s: none)

        @block.vector
        def _(dve):
            pl = Place()
            half = lambda: dve_half(dve, pl)
            V = nc.vector
            none = iter(())

            def mean_squares(c):
                dve.drain()
                for tb in range(TB):
                    V.bn_aggr(x_moments[:, tb, :], x_stats[:, tb, :, :])
                dve.drain()
                for tb in range(TB):
                    V.scalar_tensor_tensor(out=rms[:, c, tb:tb + 1], in0=x_moments[:, tb, 0:1], scalar=x_moments[:, tb, 0:1],
                                           in1=x_moments[:, tb, 1:2], op0=ALU.mult, op1=ALU.add)
                dve.drain()
                V.tensor_scalar(rms[:, c, :], rms[:, c, :], RMS_EPS, None, ALU.add).then_inc(S("meansq"), 1)

            def x_pieces(s, tb):
                V.bn_stats(x_stats[:, tb, s, :], x[:, tb, s * 512:(s + 1) * 512])

            def inverse_root(c):
                dve.wait_ge(S("rooted"), c + 1)
                V.reciprocal(rstd[:, c, :], rms[:, c, :]).then_inc(S("rstd_done"), 1)
                dve.drain()

            def x_lo(j, s, i):
                b = 2 * s + i
                dve.wait_ge(S("hT_hi_done"), 8 * j + b + 1)
                for kt in (2 * b, 2 * b + 1):
                    e = V.scalar_tensor_tensor(out=hT_lo[:, kt, :], in0=AX[b % 4][:, (kt % 2) * T:(kt % 2 + 1) * T],
                                               scalar=gains[:, j, kt:kt + 1], in1=hT_hi[:, kt, :].bitcast(F32),
                                               op0=ALU.mult, op1=ALU.subtract)
                e.then_inc(S("hT_lo_done"), 1)

            def turn_x(j, s, c=None):
                dve.drain()
                x_pieces(s, 0)
                yield
                x_pieces(s, 1)
                if c is not None:
                    mean_squares(c)
                yield
                if c is not None:
                    inverse_root(c)
                x_lo(j, s, 0)
                yield
                x_lo(j, s, 1)
                if c != 2:
                    yield

            def lo_parts(dst, hi, k0, banks, event, n, done):
                dve.wait_ge(S(event), n)
                for i, b in enumerate(banks):
                    at = bass.ds(k0 + 2 * i, 2)
                    e = V.tensor_tensor(dst[:, at, :], AX[b][:, :].rearrange("p (a t) -> p a t", a=2),
                                        hi[:, at, :].bitcast(F32), ALU.subtract)
                e.then_inc(S(done), 1)

            dve.wait_ge(S("first_gains"), 16)
            for i in range(2):
                x_lo(0, 0, i)
            run(half, LOOK)
            for s in range(4):
                if s:
                    for i in range(2):
                        x_lo(0, s, i)
                dve.wait_ge(S(f"x_landed{s}"), 16)
                for tb in range(TB):
                    x_pieces(s, tb)
                if s == 3:
                    mean_squares(0)
                    inverse_root(0)
                run(half, 2)
            dve.wait_ge(S("consts_landed"), 16 * 10)
            dve.wait_ge(S("gains_landed"), 16 * 4)
            V.tensor_tensor(gains[:, 2, :], gains[:, 2, :], gains[:, 4, :], ALU.mult)

            def mixing():
                for tb in range(TB):
                    if tb == 0:
                        dve.wait_ge(S("read_out1"), 2)
                    for c in range(2):
                        V.bn_stats(bn[:, tb, c, :], vg[:, tb, c * 512:(c + 1) * 512])
                    dve.drain()
                    e = V.bn_aggr(mv[:, tb, :], bn[:, tb, :, :])
                dve.drain()
                V.tensor_scalar(mv[:, :, 1], mv[:, :, 1], LN_EPS, None, ALU.add).then_inc(S("ln_var"), 1)
                yield
                dve.wait_ge(S("ln_sd"), 1)
                V.reciprocal(lnr[:, :], lnr[:, :])
                dve.drain()
                for tb in range(TB):
                    V.tensor_scalar(vg[:, tb, :], vg[:, tb, :], mv[:, tb, 0:1], lnr[:, tb:tb + 1], ALU.subtract, ALU.mult)
                    dve.drain()
                    yield
                    V.tensor_tensor(vg[:, tb, :], vg[:, tb, :], lng[:, :], ALU.mult)
                    dve.drain()
                    yield
                    V.tensor_tensor(vg[:, tb, :], vg[:, tb, :], lnb[:, :], ALU.add).then_inc(S("v_normed"), 1)
                    yield
                for _ in range(9):
                    yield
                dve.wait_ge(S("read_out1"), 4)
                for j in range(4):
                    tb, g0 = j // 2, (j % 2) * 4
                    dve.wait_ge(S("mixed"), j + 1)
                    for g in range(4):
                        c = slice((g0 + g) * P, (g0 + g + 1) * P)
                        e = V.scalar_tensor_tensor(out=ug[:, tb, c], in0=AX[2 + j % 2][:, g * P:(g + 1) * P],
                                                   scalar=bsT[:, g0 + g:g0 + g + 1], in1=ug[:, tb, c],
                                                   op0=ALU.add, op1=ALU.mult)
                    e.then_inc(S("ya_done"), 1)
                    yield
                    yield
                for b in range(4):
                    yield
                    lo_parts(yT_lo, yT_hi, 2 * b, (2 + b % 2,), "ya_hi", b + 1, "ya_lo")

            def attend(g):
                for pr in range(4):
                    u = 4 * g + pr
                    dve.wait_ge(S("bias_masked"), 2 * u + 2)
                    for a in range(2):
                        dve.wait_ge(S("na_scores"), 2 * u + a + 1)
                        b0 = bias[:, u % BR, a, 2, 0:1]
                        window = bass.AP(tensor=b0.tensor, offset=b0.offset,
                                         ap=[list(b0.ap[0]), [-2 * GRID, TB], [1, T]])
                        V.scalar_tensor_tensor(out=sc[:, a, :, :], in0=AX[2 + a][:, :].rearrange("p (t k) -> p t k", t=TB),
                                               scalar=float(NAD) ** -0.5, in1=window, op0=ALU.mult, op1=ALU.add)
                        dve.drain()
                        V.tensor_reduce(mx[:, a, :], sc[:, a, :, :], AX_X, ALU.max)
                        dve.drain()
                        V.tensor_scalar(mx[:, a, :], mx[:, a, :], -1.0, None, ALU.mult).then_inc(S("na_max"), 1)
                    yield
                    dve.wait_ge(S("na_exp"), 2 * u + 2)
                    V.reciprocal(ri[:, :, :], sm[:, :, :])
                    yield
                    dve.wait_ge(S("na_p_turned"), 2 * u + 2)
                    V.tensor_copy(pT[:, 1, :, :], AX[3][:, :].rearrange("p (k t) -> p k t", k=TB)).then_inc(S("na_pT1"), 1)
                    yield
                    dve.wait_ge(S("na_pv"), u + 1)
                    for a in range(2):
                        h = 2 * pr + a
                        e = V.tensor_tensor(yb[:, :, h * NAD:(h + 1) * NAD],
                                            AX[2 + a][:, 0:2 * NAD].rearrange("p (t d) -> p t d", t=TB),
                                            each(ri[:, a, :], NAD), ALU.mult)
                    e.then_inc(S("na_out"), 1)
                    yield
                yield
                yield
                lo_parts(yT_lo, yT_hi, 8 + 4 * g, (2, 3), "yb_hi", g + 1, "yb_lo")

            def qkv_side(g, part):
                for _ in range(6):
                    yield
                dve.wait_ge(S("qk_turned"), 2 * g + part + 1)
                V.tensor_copy((qT, kT)[part][:, 2:4, :], AX[1][:, :].rearrange("p (a t) -> p a t", a=2)).then_inc(S("qk_out1"), 1)
                yield
                yield

            mix = mixing()
            none = iter(())
            for t in range(4):
                run(half, 8 if t else 0, mix if t >= 2 else none)
            side = none
            att = none
            for g in range(2):
                for part in range(3):
                    t = 4 + 3 * g + part
                    run(half, 8, mix, side, att)
                    finish(side)
                    tile_done(dve, pl, t)
                    if t > 4 and part < 2:
                        dve.wait_ge(S("qk_turned"), 2 * g + part)
                    if part == 2 and g:
                        dve.wait_ge(S("na_pv"), 4)
                    V.tensor_scalar((va if part == 2 else qkv_tok)[:, 1, :], G[t % 2][1][:, :], rstd[:, 0, 1:2], None,
                                    ALU.mult).then_inc(S("read_out1"), 1)
                    side = qkv_side(g, part) if part < 2 else none
                finish(att)
                att = attend(g)
            for i in range(4):
                run(half, 8, att)
            finish(att)
            def turn_merged(n):
                yield
                for i in range(2):
                    yield
                    b = 2 * n + i
                    lo_parts(mT_lo, mT_hi, 2 * b, (b % 4,), "merged_hi", b + 1, "merged_lo")

            for n in range(4):
                run(half, 8, turn_merged(n - 1) if n else none)
                run(half, 4)
                t = T_MERGE + 3 * n + 1
                tile_done(dve, pl, t)
                if n == 0:
                    dve.wait_ge(S("read_out1"), t)
                cols = slice(n * 512, (n + 1) * 512)
                for tb in range(TB):
                    V.tensor_tensor(ga[:, tb, cols], ga[:, tb, cols], G[t % 2][tb][:, :], ALU.mult).then_inc(S(f"read_out{tb}"), 1)
                run(half, 4)
                tile_done(dve, pl, t + 1)
                dve.wait_ge(S("read_out1"), t)
                for tb in range(TB):
                    V.tensor_tensor(sgb[:, tb, :], sgb[:, tb, :], G[(t + 1) % 2][tb][:, :], ALU.mult).then_inc(S(f"read_out{tb}"), 1)
                dve.drain()
                V.tensor_tensor(ga[:, :, cols], ga[:, :, cols], sgb[:, :, :], ALU.add).then_inc(S("merged"), 1)

            def add_tile(t, at):
                tile_done(dve, pl, t)
                for tb in range(TB):
                    dst = x[:, tb, bass.ds(at, 512)]
                    V.tensor_tensor(dst, dst, G[t % 2][tb][:, :], ALU.add).then_inc(S(f"read_out{tb}"), 1)

            run(half, 8, turn_merged(3))
            add_tile(T_OUT, 0)
            for s in range(1, 4):
                run(half, 8, turn_x(1, s - 1))
                add_tile(T_OUT + s, s * 512)

            def up_side(j, kt, n, width=2):
                w = width
                yield
                for b, (dst, blk) in enumerate(((cg, j * 2), (cv, j * 2 + FB))):
                    dve.wait_ge(S("conv_mid"), n * 2 + b + 1)
                    for tap, o, i_ in ((0, slice(1, T), slice(0, T - 1)), (2, slice(0, T - 1), slice(1, T))):
                        for e in range(w):
                            src = AX[b][:, e * T:(e + 1) * T]
                            i = V.scalar_tensor_tensor(out=dst[:, e, o], in0=src[:, i_], scalar=taps[:, tap, bass.ds(blk + e, 1)],
                                                       in1=dst[:, e, o], op0=ALU.mult, op1=ALU.add)
                        if tap == 0:
                            dve.drain()
                    i.then_inc(S("conv_gate_done" if b == 0 else "conv_val_done"), 1)
                yield
                dve.drain()
                dve.wait_ge(S("silu_done"), n + 1)
                V.tensor_tensor(cv[:, 0:w, :], cg[:, 0:w, :], cv[:, 0:w, :], ALU.mult).then_inc(S("gated"), 1)
                yield
                dve.wait_ge(S("act_hi"), n + 1)
                at = bass.ds(kt, w)
                V.tensor_tensor(yT_lo[:, at, :], cv[:, 0:w, :], yT_hi[:, at, :].bitcast(F32), ALU.subtract).then_inc(S("act_lo"), 1)
                yield

            def up_read(t, n):
                tile_done(dve, pl, t)
                w = HALVES[TILE_END[t] - 1]["width"]
                if not isinstance(n, int) or n:
                    dve.wait_ge(S("up_turned"), n * 2)
                V.tensor_scalar(ut[:, 1, 0:w], G[t % 2][1][:, 0:w], rstd[:, 1, 1:2], None, ALU.mult).then_inc(S("read_out1"), 1)

            def feed_forward(t0, j0, tiles, loads, t_down, half_tile):
                pairs = (tiles - 2) // 2
                run(half, 8, none if j0 else turn_x(1, 3, 1))
                up_read(t0, j0)
                with dve.Fori(0, pairs) as i:
                    pl.enter(i, t0 + 1, 2)
                    for s in range(2):
                        run(half, 8, up_side(i * 2 + (j0 + s), i * 4 + 2 * s, i * 2 + (j0 + s)))
                        up_read(t0 + 1 + s, i * 2 + (j0 + s + 1))
                    pl.leave(pairs)
                s = 2 * pairs
                while s < tiles - 1:
                    run(half, 8, up_side(j0 + s, 2 * s, j0 + s))
                    up_read(t0 + 1 + s, j0 + s + 1)
                    s += 1
                run(half, 2 * len(loads), up_side(j0 + s, 2 * s, j0 + s, 1 if half_tile else 2))
                add_tile(t_down, 0)
                for s in range(1, 4):
                    run(half, 2 * len(loads), turn_x(2, s - 1) if j0 else none)
                    add_tile(t_down + s, s * 512)

            if parts >= 2:
                feed_forward(T_UP1, 0, UP1, DOWN1, T_DOWN1, 0)
                feed_forward(T_UP2, UP1, UP2, DOWN2, T_DOWN2, 1)

            def scaled(dst, src, f):
                return V.tensor_tensor(dst[:, :, :].rearrange("p t (h d) -> p t h d", h=HG),
                                       src[:, :, :].rearrange("p t (h d) -> p t h d", h=HG), each(f, HD), ALU.mult)

            def factors(gi):
                hs = bass.ds(gi * HG, HG)
                dve.wait_ge(S("d_sums"), gi * 2 + 2)
                V.tensor_scalar(ssum[:, :, :, :], ssum[:, :, :, :], RMS_EPS, None, ALU.add).then_inc(S("d_eps"), 1)
                dve.wait_ge(S("d_root"), gi + 1)
                V.reciprocal(ssum[:, :, :, :], ssum[:, :, :, :])
                dve.drain()
                rq, rk = ssum[:, 0, :, :], ssum[:, 1, :, :]
                dve.wait_ge(S("decays"), 1)
                V.tensor_scalar(fac[:, F_Q, :, :], rq, float(HD) ** -0.5, None, ALU.mult)
                V.tensor_tensor(fac[:, F_KB, :, :], rk, beta[:, :, hs], ALU.mult)
                V.tensor_tensor(fac[:, F_KDEC, :, :], rk, edec[:, :, hs], ALU.mult)
                V.tensor_copy(fac[:, F_V, :, :], beta[:, :, hs])
                dve.drain()
                V.tensor_tensor(fac[:, F_KBE, :, :], fac[:, F_KB, :, :], egc[:, :, hs], ALU.mult)
                dve.drain()

            def conv_side(gi, part):
                n = gi * 3 + part
                yield
                for b in range(2):
                    dve.wait_ge(S("c_mid"), n * 2 + b + 1)
                    for tap in range(3):
                        for e in range(2):
                            back = 3 - tap
                            src = AX[b][:, e * T:(e + 1) * T]
                            i = V.scalar_tensor_tensor(out=xc[:, 2 * b + e, back:], in0=src[:, 0:T - back],
                                                       scalar=ctap[:, tap, bass.ds(gi * HG + (part * H + 2 * b + e), 1)],
                                                       in1=xc[:, 2 * b + e, back:], op0=ALU.mult, op1=ALU.add)
                        if tap < 2:
                            dve.drain()
                    if b == 0:
                        yield
                i.then_inc(S("c_conv"), 1)
                yield
                yield
                yield
                dve.wait_ge(S("c_back"), n + 1)
                if part == 2:
                    dst, event = vs, "d_v_rows"
                else:
                    dst, event = (qs, ks)[part], "c_rows1"
                V.tensor_copy(dst[:, 1, :], AX[1][:, :]).then_inc(S(event), 1)
                yield
                yield
                if part == 1:
                    factors(gi)
                yield

            def delta(gi):
                hs = bass.ds(gi * HG, HG)
                rk = ssum[:, 1, :, :]
                dve.wait_ge(S("c_rows0"), gi * 2 + 2)
                scaled(tmp, ks, fac[:, F_KB, :, :]).then_inc(S("d_rows"), 1)
                yield
                yield
                for j, (dst, nxt) in enumerate(((kbT, "qn"), (qnT, "kn"), (knT, "qd"), (qdT, None))):
                    dve.wait_ge(S("d_turned"), gi * 4 + j + 1)
                    V.tensor_copy(dst[:, 2:4, :], AX[3][:, :].rearrange("p (a t) -> p a t", a=2)).then_inc(S("d_out1"), 1)
                    if nxt == "kn":
                        dve.wait_ge(S("d_kbe"), gi + 1)
                        scaled(ks, ks, rk).then_inc(S("d_rows"), 1)
                    elif nxt == "qd":
                        scaled(tmp, qs, egc[:, :, hs]).then_inc(S("d_rows"), 1)
                    elif nxt == "qn":
                        scaled(qs, qs, fac[:, F_Q, :, :]).then_inc(S("d_rows"), 1)
                    else:
                        dve.wait_ge(S("chunk_masks"), 1)
                        for tb in range(TB):
                            e = V.tensor_tensor(W1[:, tb * HG:(tb + 1) * HG, :], rep(m_le[:, :], HG), each(gg[:, tb, hs], C), ALU.mult)
                        e.then_inc(S("d_gm"), 1)
                    yield
                dve.wait_ge(S("d_exp"), gi + 1)
                V.tensor_tensor(dec[:, :, :], dec[:, :, :], rep(m_le[:, :], TB * HG), ALU.mult)
                dve.drain()
                yield
                dve.wait_ge(S("d_gram"), gi + 1)
                V.tensor_tensor(AT[:, :, :], AX[2][:, :].rearrange("p (a c) -> p a c", c=C), dec[:, :, :], ALU.mult)
                V.tensor_tensor(qk[:, :, :], AX[3][:, :].rearrange("p (a c) -> p a c", c=C), dec[:, :, :], ALU.mult)
                dve.drain()
                V.tensor_tensor(Um[:, :, :], AT[:, :, :], rep(m_lev[:, 0, :], TB * HG), ALU.mult)
                dve.drain()
                V.scalar_tensor_tensor(out=Um[:, :, :], in0=Um[:, :, :], scalar=-1.0, in1=rep(idc[:, :], TB * HG),
                                       op0=ALU.mult, op1=ALU.add).then_inc(S("d_U1"), 1)
                yield
                yield
                for l in range(1, LEVELS):
                    n = gi * (LEVELS - 1) + l
                    dve.wait_ge(S("d_Z"), n)
                    V.scalar_tensor_tensor(out=W1[:, :, :], in0=AX[2][:, :].rearrange("p (a c) -> p a c", c=C), scalar=-1.0,
                                           in1=rep(idc[:, :], TB * HG), op0=ALU.mult, op1=ALU.add).then_inc(S("d_W1"), 1)
                    yield
                    dve.wait_ge(S("d_TU"), n)
                    V.tensor_copy(Um[:, :, :], AX[3][:, :].rearrange("p (a c) -> p a c", c=C)).then_inc(S("d_U"), 1)
                    yield
                dve.wait_ge(S("d_u"), gi + 1)
                V.tensor_copy(tmp[:, 1, :], AX[3][:, :]).then_inc(S("d_u_out1"), 1)
                yield
                dve.wait_ge(S("d_w"), gi + 1)
                V.tensor_copy(wT[:, 1, :, :, :], AX[3][:, :].rearrange("p (t h c) -> p t h c", t=TB, h=HG)).then_inc(S("d_w_out1"), 1)
                yield
                for n in range(4):
                    tb, a = n // 2, n % 2
                    rows_ = slice(a * C, (a + 1) * C)
                    if n:
                        dve.wait_ge(S("d_wS"), gi * 3 + n)
                        V.tensor_tensor(tmp[rows_, tb, :], tmp[rows_, tb, :], AX[2][rows_, :], ALU.subtract).then_inc(S("d_vnew"), 1)
                        yield
                    dve.wait_ge(S("d_S_used"), gi * 4 + n + 1)
                    if n == 0:
                        e = V.tensor_copy(St[:, :], AX[2][:, :])
                    elif n < 3:
                        for h in range(HG):
                            c = slice(h * HD, (h + 1) * HD)
                            e = V.scalar_tensor_tensor(out=St[:, c], in0=St[:, c], scalar=egl[:, a, tb, bass.ds(gi * HG + h, 1)],
                                                       in1=AX[2][:, c], op0=ALU.mult, op1=ALU.add)
                    if n < 3:
                        e.then_inc(S("d_state"), 1)
                    yield
                dve.wait_ge(S("d_o_sums"), gi + 1)
                V.tensor_scalar(sso[:, :, :], sso[:, :, :], 1.0 / HD, RMS_EPS, ALU.mult, ALU.add).then_inc(S("d_o_mean"), 1)
                yield
                dve.wait_ge(S("d_o_root"), gi + 1)
                V.reciprocal(sso[:, :, :], sso[:, :, :])
                dve.drain()
                dve.wait_ge(S("read_out1"), gi * 4 + T_A + 4)
                for tb in range(TB):
                    for h in range(HG):
                        c = slice(h * HD, (h + 1) * HD)
                        e = V.scalar_tensor_tensor(out=o_rows[:, tb, c], in0=o_rows[:, tb, c], scalar=sso[:, tb, h:h + 1],
                                                   in1=zs[:, tb, c], op0=ALU.mult, op1=ALU.mult)
                e.then_inc(S("d_y"), 1)
                yield
                yield
                dve.wait_ge(S("z_hi"), gi + 1)
                for b in range(2):
                    at = bass.ds(gi * HG + 2 * b, 2)
                    e = V.scalar_tensor_tensor(out=zT_lo[:, at, :], in0=AX[2 + b][:, :].rearrange("p (a t) -> p a t", a=2),
                                               scalar=head_gains[:, 0:1], in1=zT_hi[:, at, :].bitcast(F32), op0=ALU.mult, op1=ALU.subtract)
                e.then_inc(S("z_lo"), 1)
                yield

            def read_rows(t, part, bufs, norm):
                if part < 3:
                    tile_done(dve, pl, t)
                    V.tensor_scalar(bufs[part][:, 1, :], G[t % 2][1][:, :], rstd[:, norm, 1:2], None,
                                    ALU.mult).then_inc(S("read_out1"), 1)

            def stack(t0, side, group, bufs, norm, first, second, pace, out_turned):
                for part in range(3):
                    run(half, 8, side(0, part - 1) if part else first, second if part else none)
                    if part == 0:
                        finish(first)
                    read_rows(t0 + part, part, bufs, norm)
                finish(second)
                with dve.Fori(0, 3) as i:
                    pl.enter(i, t0 + 3, 4)
                    g = group(i)
                    run(half, 8, g)
                    for part in range(3):
                        run(half, 8, side(i + 1, part - 1) if part else side(i, 2), g)
                        if part == 2:
                            finish(g)
                        read_rows(t0 + 4 + part, part, bufs, norm)
                    pl.leave(3)
                g, s = group(3), side(3, 2)
                run(half, 3, g)
                run(half, 5, s, g)
                run(half, 12, s, *[g] * pace)
                finish(g)
                for s in range(2):
                    run(half, 2)
                    add_tile(t0 + 16 + s, s * 512)
                run(half, 8, chain(out_turned(0), out_turned(1)))
                add_tile(t0 + 18, 1024)
                run(half, 8, out_turned(2))
                add_tile(t0 + 19, 1536)

            def renorm():
                yield from turn_x(2, 3, 2)
                dve.wait_ge(S("nf_landed"), 16)
                dve.wait_ge(S("hT_turned"), 8 * 3)
                for k in range(4):
                    tb, e = k // 2, k % 2
                    cols = slice(e * 1024, (e + 1) * 1024)
                    V.scalar_tensor_tensor(out=x[:, tb, cols], in0=x[:, tb, cols], scalar=rstd[:, 2, tb:tb + 1],
                                           in1=nf[:, cols], op0=ALU.mult, op1=ALU.mult).then_inc(S("x_normed"), 1)
                    if k < 3:
                        yield
                dve.wait_ge(S("x_squared"), 1)
                V.tensor_tensor(rms[:, 3, :], squares[:, :, 0], squares[:, :, 1], ALU.add)
                dve.drain()
                V.tensor_scalar(rms[:, 3, :], rms[:, 3, :], 1.0 / D, RMS_EPS, ALU.mult, ALU.add).then_inc(S("meansq"), 1)
                dve.wait_ge(S("rooted"), 4)
                V.reciprocal(rstd[:, 3, :], rms[:, 3, :])
                dve.drain()
                V.tensor_tensor(rstd[:, 3, :], rstd[:, 3, :], rstd[:, 2, :], ALU.mult).then_inc(S("rstd_done"), 1)
                dve.drain()

            def decays():
                dve.wait_ge(S("wab_hi_done"), 1)
                V.tensor_tensor(wab_lo[:, :, :], wab[:, :, :], wab_hi[:, :, :].bitcast(F32), ALU.subtract).then_inc(S("wab_lo_done"), 1)
                for _ in range(6):
                    yield
                ab = AX[2][:, 0:TB * 2 * H].rearrange("p (t c) -> p t c", t=TB)
                dve.wait_ge(S("ab_turned"), 1)
                dve.wait_ge(S("ab_landed"), 32)
                for tb in range(TB):
                    e = V.scalar_tensor_tensor(out=gx[:, tb, :], in0=ab[:, tb, 0:H], scalar=rstd[:, 3, tb:tb + 1], in1=dtb[:, :],
                                               op0=ALU.mult, op1=ALU.add)
                e.then_inc(S("ab_sum"), 1)
                yield
                yield
                dve.wait_ge(S("ab_exp"), 1)
                V.tensor_scalar(beta[:, :, :], beta[:, :, :], 1.0, None, ALU.add).then_inc(S("ab_one"), 1)
                yield
                yield
                dve.wait_ge(S("ab_ln"), 1)
                V.tensor_scalar(gx[:, :, :], gx[:, :, :], 0.0, None, ALU.max)
                dve.drain()
                V.tensor_tensor(gx[:, :, :], gx[:, :, :], beta[:, :, :], ALU.add)
                dve.drain()
                for tb in range(TB):
                    e = V.scalar_tensor_tensor(out=gg[:, tb, :], in0=gx[:, tb, :], scalar=-1.0, in1=alog[:, :],
                                               op0=ALU.mult, op1=ALU.mult)
                e.then_inc(S("ab_g"), 1)
                yield
                yield
                yield
                dve.wait_ge(S("gc_done"), 1)
                V.tensor_copy(gx[:, :, :], AX[3][:, 0:TB * H].rearrange("p (t h) -> p t h", t=TB))
                dve.drain()
                V.tensor_tensor(edec[:, :, :], gx[:, :, :], AX[3][:, P:P + TB * H].rearrange("p (t h) -> p t h", t=TB),
                                ALU.subtract).then_inc(S("g_rest"), 1)
                yield

            if parts >= 3:
                stack(T_A, conv_side, delta, (tok, tok, tok), 3, renorm(), decays(), 2, lambda s: turn_x(3, s))
            elif parts == 2:
                finish(renorm())

            def rows_side(gi, part):
                n = gi * 2 + part
                if part == 2:
                    return
                yield
                dve.wait_ge(S("b_sums"), n + 1)
                V.tensor_scalar(bss[:, :, :], bss[:, :, :], 1.0 / HD, RMS_EPS, ALU.mult, ALU.add).then_inc(S("b_mean"), 1)
                yield
                dve.wait_ge(S("b_root"), n + 1)
                V.reciprocal(bss[:, :, :], bss[:, :, :])
                dve.drain()
                scaled(tok, tok, bss[:, :, :]).then_inc(S("b_normed"), 1)
                yield
                yield
                dve.wait_ge(S("b_turned"), n + 1)
                V.tensor_scalar((bqT, bkT)[part][:, 2:4, :], AX[1][:, :].rearrange("p (a t) -> p a t", a=2),
                                head_gains[:, 1 + part:2 + part], None, ALU.mult).then_inc(S("b_out1"), 1)
                yield

            def band(gi):
                for _ in range(8):
                    yield
                for pr in range(2):
                    n = gi * 2 + pr
                    for a in range(2):
                        dve.wait_ge(S("b_scores"), n * 2 + a + 1)
                        for tb in range(TB):
                            w = (tb + 1) * P
                            window = bbias[:, bass.ds(gi * HG + (2 * pr + a), 1), P - tb * P:P - tb * P + w]
                            V.scalar_tensor_tensor(out=bsc[:, a, tb, 0:w], in0=AX[2 + a][:, tb * T:tb * T + w],
                                                   scalar=float(HD) ** -0.5, in1=window.rearrange("p a k -> p (a k)"),
                                                   op0=ALU.mult, op1=ALU.add)
                        dve.drain()
                        for tb in range(TB):
                            V.tensor_reduce(bmx[:, a, tb:tb + 1], bsc[:, a, tb, 0:(tb + 1) * P], AX_X, ALU.max)
                        dve.drain()
                        V.tensor_scalar(bmx[:, a, :], bmx[:, a, :], -1.0, None, ALU.mult).then_inc(S("b_max"), 1)
                    yield
                    yield
                    dve.wait_ge(S("b_exp"), n * 2 + 2)
                    V.reciprocal(bri[:, :, :], bsm[:, :, :])
                    yield
                    dve.wait_ge(S("b_p_turned"), n * 2 + 2)
                    V.tensor_copy(bpT[:, 1, :, :], AX[3][:, 0:3 * P].rearrange("p (k t) -> p k t", k=3)).then_inc(S("b_pT1"), 1)
                    yield
                    dve.wait_ge(S("b_pv"), n + 1)
                    dve.wait_ge(S("read_out1"), gi * 4 + T_B + 4)
                    for a in range(2):
                        c = slice((2 * pr + a) * HD, (2 * pr + a + 1) * HD)
                        for tb in range(TB):
                            e = V.scalar_tensor_tensor(out=by[:, tb, c], in0=AX[2 + a][:, tb * HD:(tb + 1) * HD],
                                                       scalar=bri[:, a, tb:tb + 1], in1=zs[:, tb, c], op0=ALU.mult, op1=ALU.mult)
                    e.then_inc(S("b_y"), 1)
                    yield
                yield
                dve.wait_ge(S("z_hi"), gi + 5)
                for b in range(2):
                    at = bass.ds(gi * HG + 2 * b, 2)
                    e = V.tensor_tensor(zT_lo[:, at, :], AX[2 + b][:, :].rearrange("p (a t) -> p a t", a=2),
                                        zT_hi[:, at, :].bitcast(F32), ALU.subtract)
                e.then_inc(S("z_lo"), 1)
                yield

            if parts >= 4:
                dve.wait_ge(S("band_landed"), 32)
                stack(T_B, rows_side, band, (tok, tok, bva), 4, turn_x(3, 3, 4), none, 1, lambda s: none)

        @block.tensor
        def _(pe):
            pl = Place()
            half = lambda: pe_half(pe, pl)
            none = iter(())
            MM, turn = nc.tensor.matmul, nc.tensor.transpose

            def turn_rows(src, banks, event, at=0):
                for i, b in enumerate(banks):
                    for e in range(2):
                        for tb in range(TB):
                            c = (at + 2 * i + e) * P
                            m = turn(AX[b][:, e * T + tb * P:e * T + (tb + 1) * P], src[:, tb, c:c + P], ident[:, :])
                m.then_inc(S(event), 1)

            def x_turned(j, s, i):
                b = 2 * s + i
                if b >= 4 or j:
                    pe.wait_ge(S("hT_lo_done"), 8 * j + b - 3 if b >= 4 else 8 * j)
                turn_rows(x, (b % 4,), "hT_turned", 2 * b)

            def turn_x(j, s, t):
                yield
                pe.wait_ge(S("read_out0"), t + 1)
                pe.wait_ge(S("read_out1"), t + 1)
                x_turned(j, s, 0)
                x_turned(j, s, 1)
                yield
                yield
                yield

            def first_tile(done, n, *sides):
                for load in range(4):
                    pe.wait_ge(S(done), n + 2 * load + 2)
                    run(half, 2, *sides)

            pe.wait_ge(S("constants"), 1)
            for s in range(2):
                pe.wait_ge(S(f"x_landed{s}"), 16)
                for i in range(2):
                    x_turned(0, s, i)
            for load in range(4):
                if load < 2:
                    pe.wait_ge(S(f"x_landed{load + 2}"), 16)
                    for i in range(2):
                        x_turned(0, load + 2, i)
                pe.wait_ge(S("hT_lo_done"), 2 * load + 2)
                run(half, 2)

            def mixing():
                for _ in range(16):
                    yield
                pe.wait_ge(S("v_normed"), 2)
                for j in range(4):
                    tb, g0 = j // 2, (j % 2) * 4
                    if j >= 2:
                        pe.wait_ge(S("ya_done"), j - 1)
                    for g in range(4):
                        m = MM(AX[2 + j % 2][:, g * P:(g + 1) * P], wsT[:, g0 + g, :], vg[:, tb, (g0 + g) * P:(g0 + g + 1) * P],
                               start=True, stop=True)
                    m.then_inc(S("mixed"), 1)
                    yield
                    yield
                pe.wait_ge(S("ya_done"), 4)
                for b in range(4):
                    if b >= 2:
                        pe.wait_ge(S("ya_lo"), b - 1)
                    turn_rows(ug, (2 + b % 2,), "ya_turned", 2 * b)
                    yield

            def attend(g):
                for pr in range(4):
                    u = 4 * g + pr
                    pe.wait_ge(S("qk_out0"), 2 * g + 2)
                    pe.wait_ge(S("qk_out1"), 2 * g + 2)
                    pe.wait_ge(S("read_out0"), 7 + 3 * g)
                    pe.wait_ge(S("read_out1"), 7 + 3 * g)
                    if pr:
                        pe.wait_ge(S("na_out"), u)
                    elif g:
                        pe.wait_ge(S("yb_lo"), g)
                    else:
                        pe.wait_ge(S("ya_lo"), 4)
                    for a in range(2):
                        rows_ = slice(a * NAD, (a + 1) * NAD)
                        for tb in range(TB):
                            m = MM(AX[2 + a][:, tb * T:(tb + 1) * T], qT[rows_, pr, tb * P:(tb + 1) * P], kT[rows_, pr, :],
                                   start=True, stop=True)
                        m.then_inc(S("na_scores"), 1)
                    yield
                    yield
                    for a in range(2):
                        pe.wait_ge(S("na_exp"), 2 * u + a + 1)
                        for kb in range(TB):
                            for tb in range(TB):
                                m = turn(AX[2 + a][:, kb * T + tb * P:kb * T + (tb + 1) * P],
                                         sc[:, a, tb, kb * P:(kb + 1) * P], ident[:, :])
                        m.then_inc(S("na_p_turned"), 1)
                    yield
                    pe.wait_ge(S("na_pT0"), u + 1)
                    pe.wait_ge(S("na_pT1"), u + 1)
                    for a in range(2):
                        h = 2 * pr + a
                        for tb in range(TB):
                            for kb in range(TB):
                                m = MM(AX[2 + a][:, tb * NAD:(tb + 1) * NAD], pT[:, a, kb, tb * P:(tb + 1) * P],
                                       va[:, kb, h * NAD:(h + 1) * NAD], start=kb == 0, stop=kb == TB - 1)
                    m.then_inc(S("na_pv"), 1)
                    yield
                pe.wait_ge(S("na_out"), 4 * g + 4)
                turn_rows(yb, (2, 3), "yb_turned")
                yield
                yield
                yield

            def qkv_side(g, part):
                for _ in range(5):
                    yield
                t = 4 + 3 * g + part
                pe.wait_ge(S("read_out0"), t + 1)
                pe.wait_ge(S("read_out1"), t + 1)
                if t > 4:
                    pe.wait_ge(S("qk_out0"), 2 * g + part)
                    pe.wait_ge(S("qk_out1"), 2 * g + part)
                turn_rows(qkv_tok, (0, 1), "qk_turned")
                yield
                yield
                yield

            mix = mixing()
            for t in range(1, 4):
                run(half, 8, mix if t >= 2 else none)
            side = none
            att = none
            for g in range(2):
                for part in range(3):
                    run(half, 8, mix, side, att)
                    finish(side)
                    side = qkv_side(g, part) if part < 2 else none
                finish(att)
                att = attend(g)
            for i in range(4):
                run(half, 8, att)
            finish(att)
            pe.wait_ge(S("yb_lo"), 2)

            def turn_merged(n):
                yield
                pe.wait_ge(S("merged"), n + 1)
                for b in (2 * n, 2 * n + 1):
                    if b >= 4:
                        pe.wait_ge(S("merged_lo"), b - 3)
                    turn_rows(ga, (b % 4,), "merged_turned", 2 * b)
                yield

            for n in range(4):
                run(half, 8, turn_merged(n - 1) if n else none)
                run(half, 8)
            first_tile("merged_lo", 0, turn_merged(3))
            for s in range(3):
                run(half, 8, turn_x(1, s, T_OUT + s))

            def up_side(t, n, width=2):
                pe.wait_ge(S("read_out0"), t)
                pe.wait_ge(S("read_out1"), t)
                for b in range(2):
                    for e in range(width):
                        for tb in range(TB):
                            c = (b * width + e) * P
                            m = turn(AX[b][:, e * T + tb * P:e * T + (tb + 1) * P], ut[:, tb, c:c + P], ident[:, :])
                    m.then_inc(S("up_turned"), 1)
                yield

            def feed_forward(t0, j0, tiles, loads, half_tile):
                pairs = (tiles - 2) // 2
                if j0:
                    run(half, 8)
                else:
                    first_tile("hT_lo_done", 8, turn_x(1, 3, T_UP1 - 1))
                with pe.Fori(0, pairs) as i:
                    pl.enter(i, t0 + 1, 2)
                    for s in range(2):
                        run(half, 8, up_side(i * 2 + (t0 + s + 1), i * 2 + (j0 + s)))
                    pl.leave(pairs)
                s = 2 * pairs
                while s < tiles - 1:
                    run(half, 8, up_side(t0 + s + 1, j0 + s))
                    s += 1
                run(half, 2 * len(loads) - 4, up_side(t0 + s + 1, j0 + s, 1 if half_tile else 2))
                pe.wait_ge(S("act_lo"), j0 + tiles)
                run(half, 4)
                for s in range(3):
                    run(half, 2 * len(loads), turn_x(2, s, T_DOWN2 + s) if j0 else none)

            if parts >= 2:
                feed_forward(T_UP1, 0, UP1, DOWN1, 0)
                feed_forward(T_UP2, UP1, UP2, DOWN2, 1)

            def chunks():
                for tb in range(TB):
                    for a in range(2):
                        for h in range(HG):
                            yield tb, a, h, slice(a * C, (a + 1) * C), tb * HG + h

            def conv_side(gi, part):
                n = gi * 3 + part
                t = gi * 4 + (T_A + part + 1)
                pe.wait_ge(S("read_out0"), t)
                pe.wait_ge(S("read_out1"), t)
                if not isinstance(gi, int) or gi or part:
                    for event in (("d_v_rows", ) if part == 0 else ("c_rows0", "c_rows1")):
                        pe.wait_ge(S(event), gi * 2 + (0 if part == 0 else part))
                for i in range(2):
                    turn_rows(tok, (i,), "c_turned", 2 * i)
                yield
                yield
                yield
                yield
                pe.wait_ge(S("c_silu"), n + 1)
                for tb in range(TB):
                    for h in range(HG):
                        m = turn(AX[tb][:, h * P:(h + 1) * P], xc[:, h, tb * P:(tb + 1) * P], ident[:, :])
                m.then_inc(S("c_back"), 1)
                yield
                yield
                yield
                yield

            def held(n):
                return n if isinstance(n, int) else pe.to_reg(n)

            def delta(gi):
                L = LEVELS - 1
                yield
                for j, src in enumerate((tmp, qs, ks, tmp)):
                    pe.wait_ge(S("d_rows"), gi * 4 + j + 1)
                    if j:
                        pe.wait_ge(S("d_out0"), gi * 4 + j)
                        pe.wait_ge(S("d_out1"), gi * 4 + j)
                    turn_rows(src, (2, 3), "d_turned")
                    yield
                turned, now = held(gi * 4 + 4), held(gi + 1)
                pe.wait_ge(S("chunk_masks"), 1)
                pe.wait_ge(S("d_gm"), now)
                pe.wait_ge(S("d_out0"), turned)
                for a in range(2):
                    rows_ = slice(a * C, (a + 1) * C)
                    m = MM(AX[2][rows_, :], m_gt[rows_, :], W1[rows_, :, :].rearrange("p a c -> p (a c)"), start=True, stop=True)
                m.then_inc(S("d_arg"), 1)
                yield
                pe.wait_ge(S("d_exp"), gi + 1)
                pe.wait_ge(S("d_out1"), gi * 4 + 4)
                for dst, rhs in ((AX[2], kbT), (AX[3], qnT)):
                    for tb, a, h, rows_, c in chunks():
                        cols = slice(tb * P + a * C, tb * P + (a + 1) * C)
                        m = MM(dst[rows_, c * C:(c + 1) * C], knT[:, h, cols], rhs[:, h, cols], start=True, stop=True)
                m.then_inc(S("d_gram"), 1)
                yield
                yield
                pe.wait_ge(S("chunk_masks"), 1)
                pe.wait_ge(S("d_U1"), gi + 1)
                for tb, a, h, rows_, c in chunks():
                    m = MM(AX[2][rows_, c * C:(c + 1) * C], Um[rows_, c, :], idc[rows_, :], start=True, stop=True)
                m.then_inc(S("d_T1"), 1)
                yield
                for l in range(1, LEVELS):
                    n, before = held(gi * L + l), held(gi * L + l - 1)
                    pe.wait_ge(S("chunk_masks"), 1)
                    pe.wait_ge(S("d_level"), n)
                    pe.wait_ge(S("d_T"), n)
                    for tb, a, h, rows_, c in chunks():
                        m = MM(AX[2][rows_, c * C:(c + 1) * C], ATl[rows_, c, :], Tm[rows_, c, :], start=True, stop=True)
                    m.then_inc(S("d_Z"), 1)
                    yield
                    pe.wait_ge(S("chunk_masks"), 1)
                    pe.wait_ge(S("d_W1"), n)
                    if l > 1:
                        pe.wait_ge(S("d_U"), before)
                    for tb, a, h, rows_, c in chunks():
                        if l < LEVELS - 1:
                            MM(AX[2][rows_, c * C:(c + 1) * C], Um[rows_, c, :], W1[rows_, c, :], start=True, stop=True)
                        m = MM(AX[3][rows_, c * C:(c + 1) * C], W1[rows_, c, :], Um[rows_, c, :], start=True, stop=True)
                    m.then_inc(S("d_TU"), 1)
                    yield
                n, now = held(gi * L + L), held(gi + 1)
                pe.wait_ge(S("chunk_masks"), 1)
                pe.wait_ge(S("d_U"), n)
                pe.wait_ge(S("d_vb"), now)
                pe.wait_ge(S("d_kbe"), now)
                for tb, a, h, rows_, c in chunks():
                    m = MM(AX[2 + tb][rows_, h * HD:(h + 1) * HD], Um[rows_, c, :], vs[rows_, tb, h * HD:(h + 1) * HD],
                           start=True, stop=True)
                m.then_inc(S("d_u"), 1)
                yield
                pe.wait_ge(S("d_u_out0"), gi + 1)
                pe.wait_ge(S("d_u_out1"), gi + 1)
                for tb, a, h, rows_, c in chunks():
                    m = MM(AX[2 + a][:, c * C:(c + 1) * C], kbe[rows_, tb, h * HD:(h + 1) * HD], Um[rows_, c, :],
                           start=True, stop=True)
                m.then_inc(S("d_w"), 1)
                yield
                now = held(gi + 1)
                pe.wait_ge(S("chunk_masks"), 1)
                pe.wait_ge(S("d_w_out0"), now)
                pe.wait_ge(S("d_w_out1"), now)
                pe.wait_ge(S("d_kdec"), now)
                for n in range(4):
                    tb, a = n // 2, n % 2
                    rows_ = slice(a * C, (a + 1) * C)
                    if n:
                        pe.wait_ge(S("d_state"), gi * 3 + n)
                        for h in range(HG):
                            m = MM(AX[2][rows_, h * HD:(h + 1) * HD], wT[:, a, tb, h, :], St[:, h * HD:(h + 1) * HD],
                                   start=True, stop=True)
                        m.then_inc(S("d_wS"), 1)
                        yield
                        pe.wait_ge(S("d_vnew"), gi * 3 + n)
                        pe.wait_ge(S("d_o_out"), gi * 4 + n)
                    for h in range(HG):
                        c = slice(h * HD, (h + 1) * HD)
                        if n:
                            MM(AX[3][rows_, c], qdT[:, h, tb * P + a * C:tb * P + (a + 1) * C], St[:, c], start=True, stop=False)
                        MM(AX[3][rows_, c], qk[rows_, tb * HG + h, :], tmp[rows_, tb, c], start=n == 0, stop=True)
                    for h in range(HG):
                        c = slice(h * HD, (h + 1) * HD)
                        m = MM(AX[2][:, c], kdec[rows_, tb, c], tmp[rows_, tb, c], start=True, stop=True)
                    m.then_inc(S("d_S_used"), 1)
                    yield
                yield
                yield
                pe.wait_ge(S("d_y"), gi + 1)
                turn_rows(o_rows, (2, 3), "d_y_turned")
                yield
                yield

            def stack(t0, side, group, z_done, norm, second, pace, out_turned):
                for part in range(3):
                    if part == 0:
                        first_tile("hT_lo_done", 8 * norm, turn_x(norm, 3, t0 - 1))
                    else:
                        run(half, 8, side(0, part - 1), second)
                finish(second)
                with pe.Fori(0, 3) as i:
                    pl.enter(i, t0 + 3, 4)
                    g = group(i)
                    run(half, 8, g)
                    for part in range(3):
                        run(half, 8, side(i + 1, part - 1) if part else side(i, 2), g)
                    finish(g)
                    pl.leave(3)
                g, s = group(3), side(3, 2)
                run(half, 3, g)
                run(half, 5, s, g)
                run(half, 12, s, *[g] * pace)
                finish(g)
                pe.wait_ge(S("z_lo"), z_done)
                run(half, 4)
                run(half, 8, chain(out_turned(0), out_turned(1)))
                run(half, 8, out_turned(2))

            def decays():
                pe.wait_ge(S("wab_lo_done"), 1)
                for kt in range(KD):
                    dst = AX[3][0:2 * H, 0:T]
                    MM(dst, wab_lo[:, kt, :], hT_hi[:, kt, :], start=kt == 0, stop=False)
                    MM(dst, wab_hi[:, kt, :], hT_hi[:, kt, :], start=False, stop=False)
                    m = MM(dst, wab_hi[:, kt, :], hT_lo[:, kt, :], start=False, stop=kt == KD - 1)
                    if kt % 4 == 3 and kt < KD - 1:
                        yield
                m.then_inc(S("ab_done"), 1)
                yield
                yield
                yield
                pe.wait_ge(S("ab_out"), 1)
                for tb in range(TB):
                    m = turn(AX[2][:, tb * 2 * H:(tb + 1) * 2 * H], abT[:, tb * P:(tb + 1) * P], ident[0:2 * H, 0:2 * H])
                m.then_inc(S("ab_turned"), 1)
                yield
                for _ in range(5):
                    yield
                pe.wait_ge(S("chunk_masks"), 1)
                pe.wait_ge(S("ab_g"), 1)
                pe.wait_ge(S("ab_beta"), 1)
                g_all = gg[:, :, :].rearrange("p t h -> p (t h)")
                for a in range(2):
                    rows_ = slice(a * C, (a + 1) * C)
                    MM(AX[2][rows_, 0:TB * H], m_le[rows_, :], g_all[rows_, :], start=True, stop=True)
                    MM(AX[3][rows_, 0:TB * H], ones[rows_, 0:C], g_all[rows_, :], start=True, stop=True)
                    MM(AX[3][rows_, P:P + TB * H], m_le[rows_, :], g_all[rows_, :], start=True, stop=True)
                    m = MM(AX[2 + a][:, 2 * P:2 * P + TB * H], ones[rows_, :], g_all[rows_, :], start=True, stop=True)
                m.then_inc(S("gc_done"), 1)
                yield

            if parts >= 3:
                stack(T_A, conv_side, delta, 4, 2, decays(), 2, lambda s: turn_x(3, s, T_B - 4 + s))
            elif parts == 2:
                finish(turn_x(2, 3, T_A - 1))

            def rows_side(gi, part):
                if part == 2:
                    return
                n = gi * 2 + part
                yield
                yield
                yield
                pe.wait_ge(S("b_normed"), n + 1)
                if not isinstance(gi, int) or gi or part:
                    pe.wait_ge(S("b_out0"), n)
                    pe.wait_ge(S("b_out1"), n)
                turn_rows(tok, (0, 1), "b_turned")
                yield
                yield

            def band(gi):
                for _ in range(8):
                    yield
                for pr in range(2):
                    n = gi * 2 + pr
                    if pr == 0:
                        pe.wait_ge(S("b_out0"), gi * 2 + 2)
                        pe.wait_ge(S("b_out1"), gi * 2 + 2)
                        pe.wait_ge(S("read_out0"), gi * 4 + (T_B + 3))
                        pe.wait_ge(S("read_out1"), gi * 4 + (T_B + 3))
                        pe.wait_ge(S("z_lo"), gi + 4)
                    else:
                        pe.wait_ge(S("b_y"), n)
                    for a in range(2):
                        h = 2 * pr + a
                        for tb in range(TB):
                            w = (tb + 1) * P
                            m = MM(AX[2 + a][:, tb * T:tb * T + w], bqT[:, h, tb * P:(tb + 1) * P], bkT[:, h, 0:w],
                                   start=True, stop=True)
                        m.then_inc(S("b_scores"), 1)
                    yield
                    yield
                    for a in range(2):
                        pe.wait_ge(S("b_exp"), n * 2 + a + 1)
                        for tb in range(TB):
                            for kb in range(tb + 1):
                                m = turn(AX[2 + a][:, (kb + tb) * P:(kb + tb + 1) * P], bsc[:, a, tb, kb * P:(kb + 1) * P], ident[:, :])
                        m.then_inc(S("b_p_turned"), 1)
                    yield
                    yield
                    pe.wait_ge(S("b_pT0"), n + 1)
                    pe.wait_ge(S("b_pT1"), n + 1)
                    for a in range(2):
                        c = slice((2 * pr + a) * HD, (2 * pr + a + 1) * HD)
                        for tb in range(TB):
                            for kb in range(tb + 1):
                                m = MM(AX[2 + a][:, tb * HD:(tb + 1) * HD], bpT[:, a, kb + tb, :], bva[:, kb, c],
                                       start=kb == 0, stop=kb == tb)
                    m.then_inc(S("b_pv"), 1)
                    yield
                pe.wait_ge(S("b_y"), gi * 2 + 2)
                turn_rows(by, (2, 3), "b_y_turned")
                yield
                yield

            if parts >= 4:
                stack(T_B, rows_side, band, 8, 3, none, 1, lambda s: none)
    return nc


_INS = ["norm_final_cols", "x", "norm_mix", "w_in", "gm_ln_g", "gm_ln_b", "gm_w_s", "gm_b_s", "na_rpb", "w_branch",
        "w_out", "norm_ffn",
        "w_up", "conv_k", "conv_b", "w_down", "norm_final", "norm_w_2", "a_w_in_2", "a_conv_w_2", "a_a_log_2",
        "a_dt_bias_2", "a_out_norm_w_2", "a_w_out_2", "b_w_in_2", "b_q_norm_w_2", "b_k_norm_w_2", "b_rel_bias_2",
        "b_w_out_2"]


def laid_out(name, a):
    import numpy as np
    if name in ("norm_mix", "norm_ffn", "norm_w_2", "norm_final_cols", "conv_k", "conv_b", "a_conv_w_2", "a_out_norm_w_2",
                "b_q_norm_w_2", "b_k_norm_w_2", "gm_b_s"):
        a = a if name in ("norm_w_2", "norm_final_cols") else a[0]
        a = np.moveaxis(a.reshape(*a.shape[:-1], -1, P), -1, -2 if name == "norm_w_2" else 0)
        a = a.reshape(P, -1) if name in ("gm_b_s", "norm_mix", "norm_ffn", "norm_final_cols", "conv_b") else a
    if name == "gm_w_s":
        a = a[0].transpose(2, 0, 1)
    if name == "b_rel_bias_2":
        a = a[..., ::-1]
    if name == "na_rpb":
        rows = np.zeros((1, NAH, 7, P), a.dtype)
        rows[..., GRID - NKC:GRID + NKC - 1] = a[:, :, NKR - 4:NKR + 3, :]
        a = rows
    return np.ascontiguousarray(a)


def kernel(**inputs):
    import numpy as np
    import concourse.bacc as bacc
    from concourse.bass_utils import run_bass_kernel_spmd

    nc = bacc.Bacc("TRN2", target_bir_lowering=False, num_devices=1)
    arrays, aps = {}, {}
    for name in _INS:
        a = laid_out(name, np.asarray(inputs[name.removesuffix("_cols")]))
        arrays[f"in_{name}"] = a
        aps[name] = nc.dram_tensor(f"in_{name}", a.shape, mybir.dt.from_np(a.dtype), kind="ExternalInput").ap()
    out = nc.dram_tensor("out_rows", (1, T, D), F32, kind="ExternalOutput").ap()
    program(nc, aps, out)
    return run_bass_kernel_spmd(nc, [arrays], core_ids=[0]).results[0]["out_rows"]
```
